# Optimizing a Trainium2 kernel written in Bass

```python
import math
import jax, jax.numpy as jnp
from jax import lax
import numpy as np

D_MODEL = 1024
BATCH = 1
SEQ = 512
DEPTH = 1

N_META = 16
BLOCK = 128
META_PAD = BLOCK - N_META
SB_HEADS = 8
SB_HEAD_DIM = 64
SB_WIDTH = SB_HEADS * SB_HEAD_DIM
CONV_WIDTH = 512
CONV_KERNEL = 31
N_GROUPS = 4
EXPERTS_PER_GROUP = 4
N_EXPERTS = N_GROUPS * EXPERTS_PER_GROUP
TOP_K = 2
EXPERT_FF = 512
IN_WIDTH = 3 * SB_WIDTH + 2 * CONV_WIDTH + 2 * D_MODEL
EPS = 1e-6

kernel_name = "sb_conformer_gated_hmoe_block"

def rmsnorm(x, g):
    x32 = x.astype(jnp.float32)
    y = x32 * lax.rsqrt(jnp.mean(x32 * x32, axis=-1, keepdims=True) + EPS)
    return (y * g.astype(jnp.float32)).astype(x.dtype)

def layernorm(x, g, b):
    x32 = x.astype(jnp.float32)
    mu = jnp.mean(x32, axis=-1, keepdims=True)
    xc = x32 - mu
    var = jnp.mean(xc * xc, axis=-1, keepdims=True)
    y = xc * lax.rsqrt(var + EPS) * g.astype(jnp.float32) + b.astype(jnp.float32)
    return y.astype(x.dtype)

def stick_breaking_attention(q, k, v):
    b, h, lp, dh = q.shape
    nb = lp // BLOCK
    scale = 1.0 / math.sqrt(dh)
    key_pos = jnp.arange(lp)
    qb = q.reshape(b, h, nb, BLOCK, dh).transpose(2, 0, 1, 3, 4)

    def one_block(args):
        q_blk, i = args
        q_pos = i * BLOCK + jnp.arange(BLOCK)
        valid = (key_pos[None, :] < q_pos[:, None]) & (key_pos[None, :] >= META_PAD)
        z = jnp.einsum('bhqd,bhkd->bhqk', q_blk, k, preferred_element_type=jnp.float32) * scale
        log_stay = jnp.where(valid, jax.nn.log_sigmoid(-z), 0.0)
        log_after = lax.cumsum(log_stay, axis=3, reverse=True) - log_stay
        a = jnp.where(valid, jnp.exp(jax.nn.log_sigmoid(z) + log_after), 0.0)
        return jnp.einsum('bhqk,bhkd->bhqd', a.astype(v.dtype), v)

    out = lax.map(one_block, (qb, jnp.arange(nb)))
    return out.transpose(1, 2, 0, 3, 4).reshape(b, h, lp, dh)

def conformer_conv(a, gate, conv_w, conv_b, ln_g, ln_b, w_o):
    u = a * jax.nn.sigmoid(gate)
    y = lax.conv_general_dilated(
        u, conv_w[:, None, :].astype(u.dtype), window_strides=(1,),
        padding=[(CONV_KERNEL - 1, 0)], dimension_numbers=('NWC', 'WIO', 'NWC'),
        feature_group_count=CONV_WIDTH) + conv_b
    y = jax.nn.silu(layernorm(y, ln_g, ln_b))
    return y @ w_o

def hierarchical_moe(xf, w_rg, b_rg, w_re, b_re, w_gate, w_up, w_down):
    t = xf.shape[0]
    g_prob = jax.nn.softmax((xf @ w_rg).astype(jnp.float32) + b_rg.astype(jnp.float32), axis=-1)
    g_p, g_idx = lax.top_k(g_prob, 1)
    e_logits = ((xf @ w_re).astype(jnp.float32) + b_re.astype(jnp.float32)).reshape(
        t, N_GROUPS, EXPERTS_PER_GROUP)
    e_logits = jnp.take_along_axis(e_logits, g_idx[:, :, None], axis=1)[:, 0]
    e_prob = jax.nn.softmax(e_logits, axis=-1)
    e_p, e_idx = lax.top_k(e_prob, TOP_K)
    e_p = e_p / jnp.sum(e_p, axis=-1, keepdims=True)
    w_tok = g_p * e_p
    expert_id = g_idx * EXPERTS_PER_GROUP + e_idx
    combine = jnp.sum(jax.nn.one_hot(expert_id, N_EXPERTS, dtype=jnp.float32) * w_tok[..., None],
                      axis=1).astype(xf.dtype)
    y = jnp.zeros_like(xf)
    for e in range(N_EXPERTS):
        hdn = jax.nn.silu(xf @ w_gate[e]) * (xf @ w_up[e])
        y = y + combine[:, e:e + 1] * (hdn @ w_down[e])
    return y

def setup_inputs(seed: int = 0) -> dict:
    key = jax.random.key(seed)
    ks = jax.random.split(key, 24)
    f32 = jnp.float32
    nrm = lambda k, shape, s: jax.random.normal(k, shape, f32) * s
    return {
        "x": nrm(ks[0], (BATCH, SEQ, D_MODEL), 1.0),
        "meta": nrm(ks[1], (N_META, D_MODEL), 1.0),
        "norm_mix": 1.0 + nrm(ks[2], (DEPTH, D_MODEL), 0.02),
        "w_in": nrm(ks[3], (DEPTH, D_MODEL, IN_WIDTH), D_MODEL ** -0.5),
        "w_sb_o": nrm(ks[4], (DEPTH, SB_WIDTH, D_MODEL), SB_WIDTH ** -0.5),
        "conv_w": nrm(ks[5], (DEPTH, CONV_KERNEL, CONV_WIDTH), CONV_KERNEL ** -0.5),
        "conv_b": nrm(ks[6], (DEPTH, CONV_WIDTH), 0.02),
        "conv_ln_g": 1.0 + nrm(ks[7], (DEPTH, CONV_WIDTH), 0.02),
        "conv_ln_b": nrm(ks[8], (DEPTH, CONV_WIDTH), 0.02),
        "w_conv_o": nrm(ks[9], (DEPTH, CONV_WIDTH, D_MODEL), CONV_WIDTH ** -0.5),
        "w_out": nrm(ks[10], (DEPTH, D_MODEL, D_MODEL), D_MODEL ** -0.5),
        "norm_ffn": 1.0 + nrm(ks[11], (DEPTH, D_MODEL), 0.02),
        "w_router_group": nrm(ks[12], (DEPTH, D_MODEL, N_GROUPS), D_MODEL ** -0.5),
        "b_router_group": nrm(ks[13], (DEPTH, N_GROUPS), 0.01),
        "w_router_expert": nrm(ks[14], (DEPTH, D_MODEL, N_EXPERTS), D_MODEL ** -0.5),
        "b_router_expert": nrm(ks[15], (DEPTH, N_EXPERTS), 0.01),
        "w_gate": nrm(ks[16], (DEPTH, N_EXPERTS, D_MODEL, EXPERT_FF), D_MODEL ** -0.5),
        "w_up": nrm(ks[17], (DEPTH, N_EXPERTS, D_MODEL, EXPERT_FF), D_MODEL ** -0.5),
        "w_down": nrm(ks[18], (DEPTH, N_EXPERTS, EXPERT_FF, D_MODEL), EXPERT_FF ** -0.5),
        "norm_final": 1.0 + nrm(ks[19], (D_MODEL,), 0.02),
    }

def reference(x, meta, norm_mix, w_in, w_sb_o, conv_w, conv_b, conv_ln_g, conv_ln_b, w_conv_o,
              w_out, norm_ffn, w_router_group, b_router_group, w_router_expert, b_router_expert,
              w_gate, w_up, w_down, norm_final):
    b = x.shape[0]
    h = jnp.concatenate(
        [jnp.broadcast_to(meta[None].astype(x.dtype), (b, N_META, D_MODEL)), x], axis=1)
    L = h.shape[1]

    def to_heads(t):
        t = t.reshape(b, L, SB_HEADS, SB_HEAD_DIM)
        t = jnp.pad(t, ((0, 0), (META_PAD, 0), (0, 0), (0, 0)))
        return t.transpose(0, 2, 1, 3)

    for l in range(DEPTH):
        xn = rmsnorm(h, norm_mix[l])
        u = xn @ w_in[l]
        o0 = 0
        q = u[..., o0:o0 + SB_WIDTH]; o0 += SB_WIDTH
        k = u[..., o0:o0 + SB_WIDTH]; o0 += SB_WIDTH
        v = u[..., o0:o0 + SB_WIDTH]; o0 += SB_WIDTH
        glu_a = u[..., o0:o0 + CONV_WIDTH]; o0 += CONV_WIDTH
        glu_b = u[..., o0:o0 + CONV_WIDTH]; o0 += CONV_WIDTH
        gate_sb = u[..., o0:o0 + D_MODEL]; o0 += D_MODEL
        gate_conv = u[..., o0:o0 + D_MODEL]

        att = stick_breaking_attention(to_heads(q), to_heads(k), to_heads(v))[:, :, META_PAD:]
        y_sb = att.transpose(0, 2, 1, 3).reshape(b, L, SB_WIDTH) @ w_sb_o[l]
        y_conv = conformer_conv(glu_a, glu_b, conv_w[l], conv_b[l], conv_ln_g[l],
                                conv_ln_b[l], w_conv_o[l])
        merged = jax.nn.sigmoid(gate_sb) * y_sb + jax.nn.sigmoid(gate_conv) * y_conv
        h = h + merged @ w_out[l]

        xn2 = rmsnorm(h, norm_ffn[l]).reshape(b * L, D_MODEL)
        y_moe = hierarchical_moe(xn2, w_router_group[l], b_router_group[l], w_router_expert[l],
                                 b_router_expert[l], w_gate[l], w_up[l], w_down[l])
        h = h + y_moe.reshape(b, L, D_MODEL)

    return rmsnorm(h, norm_final)[:, N_META:]


_drawn_inputs = setup_inputs


def setup_inputs(seed=0):
    import zlib

    import numpy as np

    out = dict(_drawn_inputs(seed))
    spreads = {}
    factors = {'norm_mix': 3.045,
     'conv_b': 3.544,
     'conv_ln_g': 18.619,
     'conv_ln_b': 20.033,
     'b_router_group': 35.293,
     'b_router_expert': 57.499,
     'norm_final': 8.086,
     'norm_ffn': 6.633}
    for name, (base, spread) in spreads.items():
        noise = np.random.default_rng([zlib.crc32(name.encode()), seed]).standard_normal(out[name].shape)
        drawn = base * np.exp(spread * noise) if base else spread * noise
        out[name] = __import__('jax').numpy.asarray(drawn.astype(out[name].dtype))
    for name, factor in factors.items():
        out[name] = (out[name] * factor).astype(out[name].dtype)
    return out
```

```python
from contextlib import ExitStack

import concourse.bass as bass
from concourse import mybir

F32 = mybir.dt.float32
F32R = mybir.dt.float32r
BF16 = mybir.dt.bfloat16
I32 = mybir.dt.int32
U32 = mybir.dt.uint32
ALU = mybir.AluOpType
ACT = mybir.ActivationFunctionType
AX = mybir.AxisListType
ds = bass.ds

P = 128
D = 1024
KB = D // P
SEQ = 512
META = 16
L = META + SEQ
TILES = SEQ // P
HALF = L // 2
DH = 64
PAIRS = 4
CONV = 512
TAPS = 31
HIST = TAPS - 1
EPS = 1e-6
SCALE = DH ** -0.5
MASKED = -1e30
COL_Q, COL_K, COL_V, COL_A, COL_B, COL_GSB, COL_GCV = 0, 512, 1024, 1536, 2048, 2560, 3584
GROUPS, PER_GROUP = 4, 4
E = GROUPS * PER_GROUP
FF = 512
FB = FF // P
TOP = 2
OVER = (TOP * SEQ - 2) // P
BLOCKS = E + OVER
ICOLS = BLOCKS + 3
CHUNK = 1024
CR = 8


class Stream:

    def __init__(self, segments):
        self.seg, g, taken = {}, 0, {}
        last_raw, last_split = {}, {}
        for name, iters, slots in segments:
            per = {r: sum(1 for a, _ in slots if a == r) for r, _ in slots}
            info = {"g": g, "n": len(slots), "slots": slots, "per": per, "base": dict(taken), "raw": [99] * len(slots),
                    "split": [99] * len(slots)}
            for _ in range(iters):
                for j, (r, s) in enumerate(slots):
                    info["raw"][j] = min(info["raw"][j], g - last_raw.get(r, g - CR))
                    info["split"][j] = min(info["split"][j], g - last_split.get(s, g - CR))
                    last_raw[r], last_split[s] = g, g
                    taken[r] = taken.get(r, 0) + 1
                    g += 1
            self.seg[name] = info

    def at(self, name, j, it):
        info = self.seg[name]
        if j >= info["n"]:
            j, it = j - info["n"], it + 1
        r, s = info["slots"][j]
        before = sum(1 for a, _ in info["slots"][:j] if a == r)
        loads = it * info["per"][r] + info["base"].get(r, 0) + before + 1
        return it * info["n"] + info["g"] + j, r, s, loads, min(info["raw"][j], CR), min(info["split"][j], CR)


RAW, SPLIT = 6, 4
STREAM = Stream([
    ("pair", PAIRS, [(0, 0), (1, 1), (2, 2), (3, 3), (4, 1)]),
    ("gate", 1, [(0, 0), (1, 1), (2, 2), (3, 3)]),
    ("mix", 3, [(0, 0), (1, 1), (2, 2), (3, 0), (4, 1), (5, 2)]),
    ("last", 1, [(0, 0), (1, 1)]),
    ("out", 1, [(2, 2), (3, 3), (4, 0), (5, 1), (0, 2), (1, 3), (3, 2), (4, 3)]),
    ("expert", E, [(j % RAW, j % SPLIT) for j in range(12)]),
    ("over", OVER, [(j % RAW, j % SPLIT) for j in range(12)]),
])


def build(nc, x, meta, norm_mix, w_in, w_sb_o, conv_w, conv_b, conv_ln_g, conv_ln_b, w_conv_o, w_out, norm_ffn,
          w_router_group, b_router_group, w_router_expert, b_router_expert, w_gate, w_up, w_down, norm_final, out,
          xn2_dram, index_dram, y_dram):
    with ExitStack() as ctx:
        ctx.enter_context(nc.allow_non_contiguous_dma(reason="small vectors"))
        at = [0]

        def sb(name, shape, dt=F32):
            n = 1
            for k in shape[1:]:
                n *= k
            t = nc.alloc_sbuf_tensor_at(name, shape, dt, offset=at[0])
            at[0] += -(-n * (2 if dt == BF16 else 4) // 32) * 32
            return t

        def sem(name):
            return ctx.enter_context(nc.semaphore(name))

        at[0] = -(-nc.sbuf_base // 32) * 32
        raw = [sb(f"raw{i}", [P, CHUNK]) for i in range(RAW)]
        w_hi = [sb(f"w_hi{i}", [P, CHUNK], F32R) for i in range(SPLIT)]
        w_lo = [sb(f"w_lo{i}", [P, CHUNK], F32R) for i in range(SPLIT)]
        h = sb("h", [P, TILES, D])
        ident = sb("ident", [P, P])
        ident_bf = sb("ident_bf", [P, P], BF16)
        mask_bf = sb("mask_bf", [P, P], BF16)
        before_bf = sb("before_bf", [P, P], BF16)
        ones_bf = sb("ones_bf", [P, P], BF16)
        mean_w = sb("mean_w", [P, P])
        ones_row = sb("ones_row", [P, L])
        eps = sb("eps", [P, 1])
        zero_row = sb("zero_row", [P, D // 4])
        sumsq = sb("sumsq", [P, 16])
        std = sb("std", [P, 16])
        rstd = sb("rstd", [P, 16])
        cw = sb("cw", [P, PAIRS, TAPS + 3])
        router_w = sb("router_w", [P, KB, GROUPS + E])
        bias_rt = sb("bias_rt", [P, GROUPS + E])
        attT_hi = sb("attT_hi", [P, PAIRS, SEQ], F32R)
        attT_lo = sb("attT_lo", [P, PAIRS, SEQ], F32R)
        sgate = sb("sgate", [P, 2, SEQ])
        cgate = sb("cgate", [P, 2, SEQ])
        merged = sb("merged", [P, SEQ])
        y = sb("y", [P, PAIRS, SEQ])
        region = at[0]
        xnT_hi = sb("xnT_hi", [P, KB, L], F32R)
        xnT_lo = sb("xnT_lo", [P, KB, L], F32R)
        region_end = at[0]
        at[0] = region
        g_ffn = sb("g_ffn", [P, D])
        xn2 = sb("xn2", [P, 2, D])
        xn2T = sb("xn2T", [P, KB, P])
        square2 = sb("square2", [P, D])
        rt = {}
        for name, n in (("logit", TILES * 20), ("ohg", TILES * 4), ("gtmp", TILES * 4), ("gsum", TILES), ("gmax", TILES),
                        ("cand", TILES * 4), ("best", TILES), ("sel", TILES * E), ("el", TILES * 4), ("ex", TILES * 4),
                        ("oh1", TILES * 4), ("oh2", TILES * 4), ("p1", TILES), ("p2", TILES), ("psum12", TILES),
                        ("H1", TILES * E), ("H2", TILES * E), ("fb", TILES * E), ("rank", TILES * E), ("t1", TILES * E),
                        ("t2", TILES * E), ("cnt", E), ("ovn", E), ("cum", E), ("cumx", E), ("t3", E), ("bex", (OVER + 1) * E),
                        ("bexi", OVER + 1), ("desc", 4), ("eidx", E), ("bidx", OVER + 1), ("onesE", E)):
            rt[name] = sb("rt_" + name, [P, n])
        H_bf = sb("H_bf", [P, TILES, E], BF16)
        w_tok = sb("w_tok", [P, TOP, TILES])
        slot_y = sb("slot_y", [P, TOP, TILES], U32)
        slot_t = sb("slot_t", [P, TOP, TILES], U32)
        token_id = sb("token_id", [P, TILES], I32)
        regs = sb("regs", [P, 2 + OVER], I32)
        assert at[0] <= region_end, (at[0], region_end)
        at[0] = region_end
        region = at[0]
        sig = sb("sig", [P, 2, L])
        stay = sb("stay", [P, 2, L + 1])
        after = sb("after", [P, 2, L])
        probT = sb("probT", [P, TILES, SEQ])
        probT_meta = sb("probT_meta", [META, SEQ])
        qT = sb("qT", [P, SEQ])
        kT = sb("kT", [P, L])
        v_sb = sb("v_sb", [P, TILES, P])
        v_meta = sb("v_meta", [META, P])
        attention_end = at[0]
        at[0] = region
        mT_hi = sb("mT_hi", [P, KB, SEQ], F32R)
        mT_lo = sb("mT_lo", [P, KB, SEQ], F32R)
        region_end = max(at[0], attention_end)
        at[0] = region
        xe = sb("xe", [P, D])
        xeT_hi = sb("xeT_hi", [P, KB, P], F32R)
        xeT_lo = sb("xeT_lo", [P, KB, P], F32R)
        silu_g = sb("silu_g", [P, FF])
        hdn = sb("hdn", [P, FF])
        hT_hi = sb("hT_hi", [P, FB, P], F32R)
        hT_lo = sb("hT_lo", [P, FB, P], F32R)
        y_sb = sb("y_sb", [P, D])
        index_sb = sb("index_sb", [P, ICOLS], I32)
        index_1 = sb("index_1", [P, 1], U32)
        zero_i = sb("zero_i", [P, ICOLS], I32)
        assert at[0] <= region_end
        at[0] = region_end
        region = at[0]
        a_sb = sb("a_sb", [P, L])
        b_sb = sb("b_sb", [P, L])
        u_pad = sb("u_pad", [P, HIST + L])
        y_acc = sb("y_acc", [P, SEQ])
        cw_c = sb("cw_c", [P, TAPS + 3])
        conv_end = at[0]
        at[0] = region
        rstd_ln = sb("rstd_ln", [P, SEQ])
        silu_y = sb("silu_y", [P, 2, SEQ])
        at[0] = max(conv_end, at[0])
        region = at[0]
        x_meta = sb("x_meta", [META, D])
        xn = sb("xn", [P, 2, D])
        g_mix = sb("g_mix", [P, D])
        pack = sb("pack", [TAPS + 3, CONV])
        norm_end = at[0]
        at[0] = region
        yT_hi = sb("yT_hi", [P, PAIRS, SEQ], F32R)
        yT_lo = sb("yT_lo", [P, PAIRS, SEQ], F32R)
        at[0] = region
        pick = sb("pick", [P, 2, D])
        g_fin = sb("g_fin", [P, D])
        fin = sb("fin", [P, D])
        at[0] = max(at[0], norm_end)
        assert at[0] <= nc.sbuf_usable_end, (at[0], nc.sbuf_usable_end)
        square = y

        ps = ctx.enter_context(nc.psum_tensor("ps", [P, 8, 512], F32))

        s_const = sem("s_const")
        s_x = sem("s_x")
        s_small = sem("s_small")
        s_sq = sem("s_sq")
        s_std = sem("s_std")
        s_rstd = sem("s_rstd")
        s_xn = sem("s_xn")
        s_xt = sem("s_xt")
        s_xhi = sem("s_xhi")
        s_xlo = sem("s_xlo")
        s_cwt = sem("s_cwt")
        s_cw = sem("s_cw")
        load = [sem(f"load{i}") for i in range(RAW)]
        hi_done = sem("hi_done")
        lo_done = sem("lo_done")
        used = sem("used")
        ev = sem("ev")
        z_done = sem("z_done")
        sig_done = sem("sig_done")
        scan_done = sem("scan_done")
        prob_done = sem("prob_done")
        t_done = sem("t_done")
        tev = sem("tev")
        mev = sem("mev")
        av_done = sem("av_done")
        av_hi = sem("av_hi")
        av_lo = sem("av_lo")
        u_done = sem("u_done")
        cwc = sem("cwc")
        conv_done = sem("conv_done")
        g_ev = sem("g_ev")
        ln_mean = sem("ln_mean")
        ln_xc = sem("ln_xc")
        ln_sq = sem("ln_sq")
        ln_var = sem("ln_var")
        ln_std = sem("ln_std")
        ln_rstd = sem("ln_rstd")
        ln_n = sem("ln_n")
        ln_act = sem("ln_act")
        ln_hi = sem("ln_hi")
        ln_lo = sem("ln_lo")
        br_done = sem("br_done")
        br_ev = sem("br_ev")
        m_hi = sem("m_hi")
        m_lo = sem("m_lo")
        res = sem("res")
        s_sq2 = sem("s_sq2")
        s_std2 = sem("s_std2")
        s_xn2 = sem("s_xn2")
        s_xn2_out = [sem(f"s_xn2_out{i}") for i in range(TILES)]
        s_xt2 = sem("s_xt2")
        s_xe2 = sem("s_xe2")
        s_logit = sem("s_logit")
        s_gffn = sem("s_gffn")
        s_gexp = sem("s_gexp")
        s_need = sem("s_need")
        s_hot = sem("s_hot")
        s_rank = sem("s_rank")
        s_hotx = sem("s_hotx")
        br_mul = sem("br_mul")
        s_slot = sem("s_slot")
        s_zero = sem("s_zero")
        s_yzero = sem("s_yzero")
        s_index = sem("s_index")
        s_regs = sem("s_regs")
        idx1 = sem("idx1")
        gath = sem("gath")
        tx = sem("tx")
        xe_hi = sem("xe_hi")
        xe_lo = sem("xe_lo")
        silu = sem("silu")
        hdn_done = sem("hdn_done")
        ht = sem("ht")
        ht_hi = sem("ht_hi")
        ht_lo = sem("ht_lo")
        yev = sem("yev")
        ystore = sem("ystore")
        y_free = sem("y_free")
        pick_sem = [sem(f"pick{k}") for k in range(TOP)]
        sum1 = sem("sum1")
        sum2 = sem("sum2")
        s_sq3 = sem("s_sq3")
        s_std3 = sem("s_std3")
        s_r3 = sem("s_r3")
        s_fin = sem("s_fin")
        s_out = sem("s_out")
        s_gfin = sem("s_gfin")
        passed = sem("passed")
        dchain = sem("dchain")
        pchain = sem("pchain")

        def cols(w, n):
            return w.rearrange("p (k n) -> p k n", n=n)

        def w_in_cols(col):
            return w_in[0].rearrange("(p k) n -> p k n", k=KB)[:, :, col]

        def split_hi(act, name, j, it):
            g, r, s, loads, _, back = STREAM.at(name, j, it)
            act.wait_ge(load[r], loads * 32)
            act.wait_ge(used, g - back + 1 + CR)
            act.activation(w_hi[s][:, :], raw[r][:, :], ACT.Copy).then_inc(hi_done, 1)

        def split_lo(dve, name, j, it):
            g, r, s, _, _, _ = STREAM.at(name, j, it)
            dve.wait_ge(hi_done, g + 1)
            dve.tensor_tensor(w_lo[s][:, :], raw[r][:, :], w_hi[s][:, :].bitcast(F32), ALU.subtract)\
               .then_inc(lo_done, 1)

        def weights(pe, name, j, it, n):
            g, _, s, _, _, _ = STREAM.at(name, j, it)
            pe.wait_ge(lo_done, g + 1 + CR)
            return cols(w_hi[s][:, :], n), cols(w_lo[s][:, :], n)

        def taken(eng, name, j, it):
            eng.wait_ge(used, STREAM.at(name, j, it)[0] + 1 + CR)

        def product(pe, dst, left, right, start, stop):
            pe.matmul(dst, left[0], right[0], start=start, stop=False)
            pe.matmul(dst, left[0], right[1], start=False, stop=False)
            return pe.matmul(dst, left[1], right[0], start=False, stop=stop)

        def first_lo(dve, i):
            if i < TILES:
                src = ps[:, 2 * i:2 * i + 2, :].rearrange("p b (k n) -> p (b k) n", n=P)
                to = slice(META + i * P, META + (i + 1) * P)
            else:
                src, to = ps[:, 0, 0:KB * META].rearrange("p (k n) -> p k n", n=META), slice(0, META)
            dve.wait_ge(s_xhi, i + 1)
            dve.tensor_tensor(xnT_lo[:, :, to], src, xnT_hi[:, :, to].bitcast(F32), ALU.subtract).then_inc(s_xlo, 1)

        block = ctx.enter_context(nc.Block())

        @block.sync
        def _(sp):
            for i in range(TILES):
                sp.dma_start(h[:, i, :], x[0, i * P:(i + 1) * P, :]).then_inc(s_x, 16)
            sp.dma_start(x_meta[:, :], meta).then_inc(s_x, 16)

            def chunk(name, j, it, pieces):
                g, r, _, _, back, _ = STREAM.at(name, j, it)
                sp.wait_ge(lo_done, g - back + 1 + CR)
                sp.sem_inc(passed, 1)
                sp.dma_start(*pieces(raw[r])).then_inc(load[r], 32)

            def in_cols(col):
                return lambda slot: (cols(slot[:, :], P), w_in_cols(col))

            def branch_chunk(name, j, it, m):
                g, r, _, _, back, _ = STREAM.at(name, j, it)
                sp.wait_ge(lo_done, g - back + 1 + CR)
                sp.sem_inc(passed, 1)
                v = raw[r][:, :].rearrange("p (b c n) -> p b c n", b=2, n=P)
                sp.dma_start(v[:, 0], w_sb_o[0].rearrange("(c p) n -> p c n", p=P)[:, :, ds(m * P, P)])\
                  .then_inc(load[r], 16)
                sp.dma_start(v[:, 1], w_conv_o[0].rearrange("(c p) n -> p c n", p=P)[:, :, ds(m * P, P)])\
                  .then_inc(load[r], 16)

            with sp.Fori(0, PAIRS) as c:
                for j, col in enumerate((COL_A, COL_K, COL_Q, COL_B, COL_V)):
                    chunk("pair", j, c, in_cols(ds(c * P + col, P)))
            for m in range(2):
                chunk("gate", 2 * m, 0, in_cols(ds(COL_GSB + m * P, P)))
                chunk("gate", 2 * m + 1, 0, in_cols(ds(COL_GCV + m * P, P)))
            with sp.Fori(0, 3) as n:
                for k in range(2):
                    branch_chunk("mix", 3 * k, n, n * 2 + k)
                    chunk("mix", 3 * k + 1, n, in_cols(ds(n * (2 * P) + (COL_GSB + (k + 2) * P), P)))
                    chunk("mix", 3 * k + 2, n, in_cols(ds(n * (2 * P) + (COL_GCV + (k + 2) * P), P)))
            for k in range(2):
                branch_chunk("last", k, 0, 6 + k)
            wo = w_out[0].rearrange("(m p) n -> p m n", p=P)
            for half in range(2):
                for q in range(4):
                    chunk("out", 4 * half + q, 0, lambda slot: (
                        cols(slot[:, :], 512), wo[:, 2 * q:2 * q + 2, 512 * half:512 * half + 512]))

            def expert_loads(name, it, e, which):
                for j in which:
                    part, q = (j % 12) // 4, j % 4
                    if part < 2:
                        src = (w_gate, w_up)[part][0, ds(e, 1)].rearrange("e (p k) n -> p (e k) n", k=KB)
                        chunk(name, j, it, lambda slot: (cols(slot[:, :], FF), src[:, 2 * q:2 * q + 2, :]))
                    else:
                        src = w_down[0, ds(e, 1)].rearrange("e (p f) n -> p (e f) n", f=FB)
                        chunk(name, j, it, lambda slot: (slot[:, :], src[:, q, :]))

            for j in range(5):
                expert_loads("expert", 0, 0, range(j, j + 1))
            for i in range(TILES):
                sp.wait_ge(s_xn2, i + 1)
                sp.dma_start(xn2_dram[i * P:(i + 1) * P, :], xn2[:, i % 2, :]).then_inc(s_xn2_out[i], 16)
            expert_loads("expert", 0, 0, range(5, 12))
            with sp.Fori(1, E) as e:
                expert_loads("expert", e, e, range(12))
            sp.wait_ge(s_regs, 1)
            count = sp.value_load(regs[0:1, 0:1], min_val=0, max_val=OVER)
            first = sp.value_load(regs[0:1, 1:2], min_val=0, max_val=E - 1)
            expert_loads("over", 0, first, range(3))
            with sp.Fori(0, OVER) as b:
                with sp.If(b < count):
                    e = sp.value_load(regs[0:1, ds(b + 1, 1)], min_val=0, max_val=E - 1)
                    expert_loads("over", b, e, range(3, 12))
                    following = sp.value_load(regs[0:1, ds(b + 2, 1)], min_val=0, max_val=E - 1)
                    expert_loads("over", b, following, range(12, 15))
            for i in range(TILES):
                sp.wait_ge(s_fin, i + 1)
                sp.dma_start(out[0, i * P:(i + 1) * P, :], fin[:, :]).then_inc(s_out, 16)
            sp.wait_ge(s_out, 16 * TILES)

        @block.gpsimd
        def _(pool):
            for s in (u_done, prob_done):
                pool.sem_inc(s, CR)
            n = [0]

            def link(ins):
                n[0] += 1
                ins.then_inc(pchain, 1)
                pool.wait_ge(pchain, n[0])

            pool.dma_start(g_mix[:, :], norm_mix[0].partition_broadcast(P)).then_inc(s_small, 16)
            pool.dma_start(pack[0:TAPS, :], conv_w[0]).then_inc(s_small, 16)
            pool.dma_start(pack[TAPS:TAPS + 1, :], conv_b).then_inc(s_small, 16)
            pool.dma_start(pack[TAPS + 1:TAPS + 2, :], conv_ln_g).then_inc(s_small, 16)
            pool.dma_start(pack[TAPS + 2:TAPS + 3, :], conv_ln_b).then_inc(s_small, 16)
            pool.dma_start(router_w[:, :, 0:GROUPS], w_router_group[0].rearrange("(p k) n -> p k n", k=KB))\
                .then_inc(s_small, 16)
            pool.dma_start(router_w[:, :, GROUPS:], w_router_expert[0].rearrange("(p k) n -> p k n", k=KB))\
                .then_inc(s_small, 16)
            pool.dma_start(bias_rt[:, 0:GROUPS], b_router_group[0].partition_broadcast(P)).then_inc(s_small, 16)
            pool.dma_start(bias_rt[:, GROUPS:], b_router_expert[0].partition_broadcast(P)).then_inc(s_small, 16)
            link(pool.memset(ident[:, :], 0.0))
            link(pool.affine_select(out=ident[:, :], in_=ident[:, :], compare_op=ALU.not_equal, fill=1.0, base=0,
                                    pattern=[[-1, P]], channel_multiplier=1))
            link(pool.tensor_copy(ident_bf[:, :], ident[:, :]))
            link(pool.memset(mask_bf[:, :], 0.0))
            link(pool.affine_select(out=mask_bf[:, :], in_=mask_bf[:, :], compare_op=ALU.is_gt, fill=MASKED, base=0,
                                    pattern=[[-1, P]], channel_multiplier=1))
            link(pool.memset(before_bf[:, :], 0.0))
            link(pool.affine_select(out=before_bf[:, :], in_=before_bf[:, :], compare_op=ALU.is_ge, fill=1.0, base=0,
                                    pattern=[[-1, P]], channel_multiplier=1))
            pool.memset(ones_bf[:, :], 1.0)
            pool.memset(mean_w[:, :], 1.0 / CONV)
            pool.memset(ones_row[:, :], 1.0)
            pool.memset(eps[:, :], EPS)
            pool.memset(stay[:, :, L:L + 1], 1.0)
            link(pool.memset(u_pad[:, 0:HIST], 0.0))
            pool.memset(sumsq[:, :], 1.0).then_inc(s_const, 1)
            link(pool.memset(zero_row[:, :], 0.0))
            for b in range(E, BLOCKS):
                pool.dma_start(y_dram[b * P:(b + 1) * P, :].rearrange("p (r c) -> p r c", r=4),
                               zero_row[:, :].unsqueeze(1).to_broadcast([P, 4, D // 4])).then_inc(s_yzero, 16)

            with pool.Fori(0, PAIRS) as c:
                pool.wait_ge(ev, c * 5 + 4 + CR)
                pool.wait_ge(conv_done, c + CR)
                pool.tensor_tensor(u_pad[:, HIST:], a_sb[:, :], b_sb[:, :], ALU.mult).then_inc(u_done, 1)
                for u in range(8):
                    off = (u % 4) * P
                    pool.wait_ge(scan_done, c * 8 + u + 1)
                    pool.tensor_tensor(sig[:, u % 2, off:], sig[:, u % 2, off:], after[:, u % 2, off:], ALU.mult)\
                        .then_inc(prob_done, 1)

            taken(pool, "out", 3, 0)
            for k in range(4):
                pool.memset(rt["desc"][:, k:k + 1], 4.0 - k)
            pool.memset(rt["onesE"][:, :], 1.0)
            pool.iota(rt["eidx"][:, :], pattern=[[1, E]], base=0, channel_multiplier=0,
                      allow_small_or_imprecise_dtypes=True)
            pool.iota(rt["bidx"][:, :], pattern=[[1, OVER + 1]], base=0, channel_multiplier=0,
                      allow_small_or_imprecise_dtypes=True)
            pool.iota(token_id[:, :], pattern=[[P, TILES]], base=0, channel_multiplier=1).then_inc(s_need, 1)
            pool.dma_start(g_ffn[:, :], norm_ffn[0].partition_broadcast(P)).then_inc(s_gffn, 16)
            taken(pool, "out", 7, 0)
            pool.wait_ge(s_yzero, 16 * OVER)
            link(pool.memset(zero_i[:, :], 0))
            pool.dma_start(index_dram.rearrange("(p n) a -> p (n a)", n=ICOLS), zero_i[:, :]).then_inc(s_zero, 16)
            pool.wait_ge(s_zero, 16)
            pool.wait_ge(s_slot, 1)
            for k in range(TOP):
                for i in range(TILES):
                    pool.indirect_dma_start(
                        out=index_dram, out_offset=bass.IndirectOffsetOnAxis(ap=slot_t[:, k, i:i + 1], axis=0),
                        in_=token_id[:, i:i + 1], in_offset=None).then_inc(s_index, 16)
            pool.wait_ge(s_index, 16 * TOP * TILES)
            pool.dma_start(index_sb[:, :], index_dram.rearrange("(p n) a -> p (n a)", n=ICOLS)).then_inc(s_index, 16)
            pool.wait_ge(s_index, 16 * (TOP * TILES + 1))
            for i in range(TILES):
                pool.wait_ge(s_xn2_out[i], 16)

            def gather(b, nth):
                pool.tensor_copy(index_1[:, :], index_sb[:, ds(b, 1)]).then_inc(idx1, 1)
                pool.wait_ge(idx1, nth + 1)
                pool.sem_inc(passed, 1)
                pool.indirect_dma_start(out=xe[:, :], out_offset=None, in_=xn2_dram,
                                        in_offset=bass.IndirectOffsetOnAxis(ap=index_1[:, 0:1], axis=0))\
                    .then_inc(gath, 16)
                pool.wait_ge(gath, nth * 16 + 16)

            def expert_pool(b):
                pool.wait_ge(tx, b * 2 + 4)
                gather(b + 2, b + 2)
                pool.wait_ge(yev, b + 1 + CR)
                pool.dma_start(y_dram[ds(b * P, P), :], y_sb[:, :]).then_inc(ystore, 16)
                pool.wait_ge(ystore, b * 16 + 16)
                pool.sem_inc(y_free, 1)

            pool.dma_start(g_fin[:, :], norm_final.partition_broadcast(P)).then_inc(s_gfin, 16)
            pool.sem_inc(y_free, CR)
            gather(0, 0)
            pool.wait_ge(tx, 2)
            gather(1, 1)
            with pool.Fori(0, E) as b:
                expert_pool(b)
            pool.wait_ge(s_regs, 1)
            count = pool.value_load(regs[0:1, 0:1], min_val=0, max_val=OVER)
            with pool.Fori(0, OVER) as b:
                with pool.If(b < count):
                    expert_pool(b + E)
            for i in range(TILES):
                for k in range(TOP):
                    if i:
                        pool.wait_ge(sum1 if k == 0 else sum2, i)
                    pool.indirect_dma_start(
                        out=pick[:, k, :], out_offset=None, in_=y_dram,
                        in_offset=bass.IndirectOffsetOnAxis(ap=slot_y[:, k, i:i + 1], axis=0)).then_inc(pick_sem[k], 16)

        @block.scalar
        def _(act):
            for s in (ev, sig_done, tev, mev, g_ev, silu, yev):
                act.sem_inc(s, CR)

            act.wait_ge(s_const, 1)
            act.wait_ge(s_x, 16 * (TILES + 1))
            for i in range(TILES):
                act.activation(square[:, 0:2, :].rearrange("p a n -> p (a n)"), h[:, i, :], ACT.Square,
                               accum_out=sumsq[:, i:i + 1]).then_inc(s_sq, 1)
                act.wait_ge(s_sq, i + 1)
            act.activation(square[0:META, 0:2, :].rearrange("p a n -> p (a n)"), x_meta[:, :], ACT.Square,
                           accum_out=sumsq[0:META, TILES:TILES + 1]).then_inc(s_sq, 1)
            act.wait_ge(s_sq, TILES + 1)
            act.activation(std[:, 0:TILES + 1], sumsq[:, 0:TILES + 1], ACT.Sqrt, bias=eps[:, :],
                           scale=1.0 / D).then_inc(s_std, 1)
            for i in range(TILES + 1):
                act.wait_ge(s_xt, i + 1)
                if i < TILES:
                    src = ps[:, 2 * i:2 * i + 2, :].rearrange("p b (k n) -> p (b k) n", n=P)
                    dst = xnT_hi[:, :, META + i * P:META + (i + 1) * P]
                else:
                    src = ps[:, 0, 0:KB * META].rearrange("p (k n) -> p k n", n=META)
                    dst = xnT_hi[:, :, 0:META]
                act.activation(dst, src, ACT.Copy).then_inc(s_xhi, 1)
            act.wait_ge(s_cwt, 1)
            act.activation(cw[:, :, :], ps[:, 2, 0:PAIRS * (TAPS + 3)].rearrange("p (c n) -> p c n", c=PAIRS),
                           ACT.Copy).then_inc(s_cw, 1)
            for j in range(3):
                split_hi(act, "pair", j, 0)

            two = ps[:, 0:2, 0:HALF]
            pr = ps[:, 3:5, 0:HALF]
            with act.Fori(0, PAIRS) as c:
                def halves(t):
                    return t[:, :].rearrange("p (b n) -> p b n", b=2)

                def out_of_psum(nth, dst, src, func=ACT.Copy, last=True):
                    ins = act.activation(dst, src, func)
                    if last:
                        ins.then_inc(ev, 1)

                taken(act, "pair", 0, c)
                act.wait_ge(u_done, c + CR)
                out_of_psum(1, halves(a_sb), pr)
                split_hi(act, "pair", 3, c)
                taken(act, "pair", 1, c)
                out_of_psum(2, halves(kT), two)
                split_hi(act, "pair", 4, c)
                taken(act, "pair", 2, c)
                out_of_psum(3, qT[:, :], ps[:, 2, :])
                taken(act, "pair", 3, c)
                out_of_psum(4, halves(b_sb), pr, ACT.Sigmoid)

                def sigmoids(u):
                    i, ub = 3 - u % 4, u % 2
                    off = L - META - (i + 1) * P
                    act.wait_ge(z_done, c * 8 + u + 1)
                    act.wait_ge(t_done, c * 8 + u - 1 + CR)
                    if i == 3:
                        src, view = two, lambda t: t[:, ub, off:L].rearrange("p (b n) -> p b n", b=2)
                    else:
                        src, view = ps[:, 2 * (u % 2), 0:L - off], lambda t: t[:, ub, off:L]
                    act.activation(view(sig), src, ACT.Sigmoid, scale=SCALE)
                    act.activation(view(stay), src, ACT.Sigmoid, scale=-SCALE).then_inc(sig_done, 1)

                def copy_weights(u):
                    i = 3 - u % 4
                    act.wait_ge(t_done, c * 8 + u + 1 + CR)
                    act.wait_ge(av_done, c * 2 + u // 4 + CR)
                    act.activation(probT[:, 0:i + 1, i * P:(i + 1) * P],
                                   ps[:, 5, 0:(i + 1) * P].rearrange("p (j n) -> p j n", n=P), ACT.Copy)\
                       .then_inc(tev, 1)
                    if i == 0:
                        act.activation(probT_meta[:, :], ps[0:META, 6, :], ACT.Copy).then_inc(mev, 1)

                sigmoids(0)
                sigmoids(1)
                taken(act, "pair", 4, c)
                out_of_psum(5, v_sb[:, :, :], ps[:, 5, :].rearrange("p (j n) -> p j n", n=P), last=False)
                out_of_psum(5, v_meta[:, :], ps[0:META, 6, 0:P])
                for u in range(8):
                    copy_weights(u)
                    if u + 2 < 8:
                        sigmoids(u + 2)
                    if 4 <= u < 7:
                        split_hi(act, "pair", 5 + u - 4, c)
                act.wait_ge(av_done, c * 2 + 2 + CR)
                act.activation(attT_hi[:, ds(c, 1), :].rearrange("p a n -> p (a n)"), ps[:, 7, :], ACT.Copy)\
                   .then_inc(av_hi, 1)

            def gates(m2, base, name, j, it):
                for k, dst in enumerate((sgate, cgate)):
                    taken(act, name, j + k, it)
                    act.wait_ge(br_ev, base + k - 3 + CR)
                    act.activation(dst[:, m2, :], ps[:, 2 * k, :], ACT.Sigmoid).then_inc(g_ev, 1)

            split_hi(act, "gate", 3, 0)
            gates(0, 0, "gate", 0, 0)
            for m in range(PAIRS):
                act.wait_ge(ln_xc, m + 1)
                if m >= 2:
                    act.wait_ge(ln_var, m - 1)
                act.activation(silu_y[:, m % 2, :], y[:, m, :], ACT.Square).then_inc(ln_sq, 1)
                if m < 2:
                    taken(act, "gate", 2 + m, 0)
                    act.activation((sgate, cgate)[m][:, 1, :], ps[:, 2 * m, :], ACT.Sigmoid).then_inc(g_ev, 1)
                    split_hi(act, "mix", m, 0)
            act.wait_ge(ln_var, PAIRS)
            act.activation(rstd_ln[:, :], ps[:, 6, :], ACT.Sqrt, bias=eps[:, :]).then_inc(ln_std, 1)
            for m in range(PAIRS):
                act.wait_ge(ln_n, m + 1)
                if m >= 2:
                    act.wait_ge(ln_lo, m - 1)
                act.activation(silu_y[:, m % 2, :], y[:, m, :], ACT.Silu, scale=cw[:, m, TAPS + 1:TAPS + 2],
                               bias=cw[:, m, TAPS + 2:TAPS + 3]).then_inc(ln_act, 1)
                act.wait_ge(ln_act, m + 1)
                act.activation(yT_hi[:, m, :], silu_y[:, m % 2, :], ACT.Copy).then_inc(ln_hi, 1)
            split_hi(act, "mix", 2, 0)

            def merge_hi(m):
                act.wait_ge(br_ev, m * 2 + 2 + CR)
                act.activation(mT_hi[:, ds(m, 1), :].rearrange("p a n -> p (a n)"), merged[:, :], ACT.Copy)\
                   .then_inc(m_hi, 1)

            with act.Fori(0, 3) as it:
                for k in range(2):
                    split_hi(act, "mix", 3 * k + 3, it)
                    merge_hi(it * 2 + k)
                    split_hi(act, "mix", 3 * k + 4, it)
                    gates(k, it * 4 + (4 + 2 * k), "mix", 3 * k + 1, it)
                    split_hi(act, "mix", 3 * k + 5, it)
            split_hi(act, "out", 1, 0)
            merge_hi(6)
            split_hi(act, "out", 2, 0)
            merge_hi(7)
            for j in range(3, 8):
                split_hi(act, "out", j, 0)
            for j in range(3):
                split_hi(act, "expert", j, 0)
            for i in range(TILES):
                act.wait_ge(res, TILES + i + 1)
                act.activation(square2[:, :], h[:, i, :], ACT.Square, accum_out=sumsq[:, 8 + i:9 + i])\
                   .then_inc(s_sq2, 1)
                act.wait_ge(s_sq2, i + 1)
            act.activation(std[:, 8:8 + TILES], sumsq[:, 8:8 + TILES], ACT.Sqrt, bias=eps[:, :],
                           scale=1.0 / D).then_inc(s_std2, 1)
            for i in range(TILES):
                act.wait_ge(s_xt2, i + 1)
                if i:
                    act.wait_ge(s_logit, i)
                act.activation(xn2T[:, :, :], ps[:, 2 * (i % 2):2 * (i % 2) + 2, :]
                               .rearrange("p b (k n) -> p (b k) n", n=P), ACT.Copy).then_inc(s_xe2, 1)
            act.wait_ge(s_gexp, 1)
            act.activation(rt["gtmp"][:, :], rt["gtmp"][:, :], ACT.Exp).then_inc(s_hot, 1)
            act.wait_ge(s_gexp, 2)
            act.activation(rt["ex"][:, :], rt["el"][:, :], ACT.Exp).then_inc(s_hot, 1)

            def inputs_hi(b, half):
                act.wait_ge(tx, b * 2 + half + 1)
                act.activation(xeT_hi[:, 4 * half:4 * half + 4, :], ps[:, half, :].rearrange("p (k n) -> p k n", n=P),
                               ACT.Copy).then_inc(xe_hi, 1)

            def expert_act(name, it, b):
                for j in (3, 4, 5, 6):
                    split_hi(act, name, j, it)
                taken(act, name, 3, it)
                act.wait_ge(hdn_done, b + CR)
                act.activation(silu_g[:, :], ps[:, 2, :], ACT.Silu).then_inc(silu, 1)
                for j in (7, 8, 9, 10, 11):
                    split_hi(act, name, j, it)
                inputs_hi(b + 1, 0)
                act.wait_ge(ht, b + 1)
                act.activation(hT_hi[:, :, :], ps[:, 4, :].rearrange("p (f n) -> p f n", n=P), ACT.Copy)\
                   .then_inc(ht_hi, 1)
                inputs_hi(b + 1, 1)
                for j in (12, 13, 14):
                    split_hi(act, name, j, it)
                taken(act, name, 11, it)
                act.wait_ge(y_free, b + CR)
                act.activation(y_sb[:, :], ps[:, 5:7, :].rearrange("p b n -> p (b n)"), ACT.Copy).then_inc(yev, 1)

            inputs_hi(0, 0)
            inputs_hi(0, 1)
            with act.Fori(0, E) as b:
                expert_act("expert", b, b)
            act.wait_ge(s_regs, 1)
            count = act.value_load(regs[0:1, 0:1], min_val=0, max_val=OVER)
            with act.Fori(0, OVER) as b:
                with act.If(b < count):
                    expert_act("over", b, b + E)
            for i in range(TILES):
                act.wait_ge(sum2, i + 1)
                act.activation(square2[:, :], h[:, i, :], ACT.Square, accum_out=sumsq[:, 12 + i:13 + i])\
                   .then_inc(s_sq3, 1)
                act.wait_ge(s_sq3, i + 1)
                act.activation(std[:, 12 + i:13 + i], sumsq[:, 12 + i:13 + i], ACT.Sqrt, bias=eps[:, :],
                               scale=1.0 / D).then_inc(s_std3, 1)

        @block.vector
        def _(dve):
            for s in (lo_done, conv_done, av_lo, br_ev, xe_lo, hdn_done):
                dve.sem_inc(s, CR)

            class Chain:
                done, start, run, per = 0, 0, None, 0

                def loop(self, run, per):
                    self.start, self.run, self.per, self.done = self.start + self.done, run, per, 0

                def end(self, runs):
                    assert self.done == self.per, self.done
                    self.start, self.run, self.done = self.start + runs * self.per, None, 0

                def link(self, ins):
                    self.done += 1
                    ins.then_inc(dchain, 1)
                    at = self.start + self.done
                    dve.wait_ge(dchain, at if self.run is None else self.run * self.per + at)

            chain = Chain()
            link = chain.link

            dve.wait_ge(s_std, 1)
            link(dve.reciprocal(rstd[:, 0:TILES + 1], std[:, 0:TILES + 1]))
            dve.wait_ge(s_small, 16 * 9)
            dve.wait_ge(s_const, 1)
            for i in range(TILES + 1):
                n, src = (P, h[:, i, :]) if i < TILES else (META, x_meta[:, :])
                if i >= 2:
                    dve.wait_ge(s_xt, i - 1)
                dve.scalar_tensor_tensor(out=xn[0:n, i % 2, :], in0=src, scalar=rstd[0:n, i:i + 1],
                                         in1=g_mix[0:n, :], op0=ALU.mult, op1=ALU.mult).then_inc(s_xn, 1)
                if i >= 1:
                    first_lo(dve, i - 1)
            first_lo(dve, TILES)
            dve.wait_ge(s_cw, 1)
            for j in range(3):
                split_lo(dve, "pair", j, 0)

            with dve.Fori(0, PAIRS) as c:
                chain.loop(c, TAPS)
                tap = [0]

                def taps(n):
                    for _ in range(n):
                        k = tap[0]
                        if k == TAPS:
                            return
                        tap[0] += 1
                        win = u_pad[:, META + k:META + k + SEQ]
                        if k == 0:
                            dve.wait_ge(u_done, c + 1 + CR)
                            link(dve.tensor_copy(cw_c[:, :], cw[:, ds(c, 1), :].rearrange("p a n -> p (a n)")))
                            link(dve.tensor_scalar(y_acc[:, :], win, cw_c[:, 0:1], cw_c[:, TAPS:TAPS + 1],
                                                   ALU.mult, ALU.add))
                        elif k < TAPS - 1:
                            link(dve.scalar_tensor_tensor(out=y_acc[:, :], in0=win, scalar=cw_c[:, k:k + 1],
                                                          in1=y_acc[:, :], op0=ALU.mult, op1=ALU.add))
                        else:
                            ins = dve.scalar_tensor_tensor(
                                out=y[:, ds(c, 1), :].rearrange("p a n -> p (a n)"), in0=win,
                                scalar=cw_c[:, k:k + 1], in1=y_acc[:, :], op0=ALU.mult, op1=ALU.add)
                            ins.then_inc(conv_done, 1)

                def scan(u):
                    ub, off = u % 2, (u % 4) * P
                    dve.wait_ge(sig_done, c * 8 + u + 1 + CR)
                    dve.wait_ge(prob_done, c * 8 + u - 1 + CR)
                    dve.tensor_tensor_scan(after[:, ub, off:L][:, ::-1], stay[:, ub, off + 1:L + 1][:, ::-1],
                                           ones_row[:, off:L], 1.0, ALU.mult, ALU.mult).then_inc(scan_done, 1)

                split_lo(dve, "pair", 3, c)
                split_lo(dve, "pair", 4, c)
                for u in range(8):
                    scan(u)
                    if u:
                        taps(2)
                    if 4 <= u < 7:
                        split_lo(dve, "pair", 5 + u - 4, c)
                taps(2)
                dve.wait_ge(av_hi, c + 1)
                dve.tensor_tensor(attT_lo[:, ds(c, 1), :].rearrange("p a n -> p (a n)"), ps[:, 7, :],
                                  attT_hi[:, ds(c, 1), :].rearrange("p a n -> p (a n)").bitcast(F32), ALU.subtract)\
                   .then_inc(av_lo, 1)
                taps(TAPS)
                chain.end(PAIRS)
            split_lo(dve, "gate", 3, 0)

            dve.wait_ge(ln_mean, 1)
            for m in range(PAIRS):
                dve.tensor_tensor(y[:, m, :], y[:, m, :], ps[:, 5, :], ALU.subtract).then_inc(ln_xc, 1)
            for j in range(2):
                split_lo(dve, "mix", j, 0)
            dve.wait_ge(ln_std, 1)
            dve.reciprocal(rstd_ln[:, :], rstd_ln[:, :]).then_inc(ln_rstd, 1)
            dve.wait_ge(ln_rstd, 1)
            for m in range(PAIRS):
                dve.tensor_tensor(y[:, m, :], y[:, m, :], rstd_ln[:, :], ALU.mult).then_inc(ln_n, 1)
            for m in range(PAIRS):
                dve.wait_ge(ln_hi, m + 1)
                dve.tensor_tensor(yT_lo[:, m, :], silu_y[:, m % 2, :], yT_hi[:, m, :].bitcast(F32), ALU.subtract)\
                   .then_inc(ln_lo, 1)
            split_lo(dve, "mix", 2, 0)

            def merge(m, m2, name, j, it):
                dve.wait_ge(g_ev, m * 2 + 2 + CR)
                dve.wait_ge(br_done, m + 1)
                dve.tensor_tensor(sgate[:, m2, :], sgate[:, m2, :], ps[:, 3, :], ALU.mult).then_inc(br_ev, 1)
                taken(dve, name, j, it)
                dve.wait_ge(br_ev, m * 2 + 1 + CR)
                dve.tensor_tensor(cgate[:, m2, :], cgate[:, m2, :], ps[:, 4, :], ALU.mult).then_inc(br_mul, 1)
                dve.wait_ge(br_mul, m + 1)
                dve.tensor_tensor(merged[:, :], sgate[:, m2, :], cgate[:, m2, :], ALU.add).then_inc(br_ev, 1)

            def merge_lo(m):
                dve.wait_ge(m_hi, m + 1)
                dve.tensor_tensor(mT_lo[:, ds(m, 1), :].rearrange("p a n -> p (a n)"), merged[:, :],
                                  mT_hi[:, ds(m, 1), :].rearrange("p a n -> p (a n)").bitcast(F32), ALU.subtract)\
                   .then_inc(m_lo, 1)

            with dve.Fori(0, 3) as it:
                for k in range(2):
                    merge(it * 2 + k, k, "mix", 3 * k, it)
                    split_lo(dve, "mix", 3 * k + 3, it)
                    merge_lo(it * 2 + k)
                    split_lo(dve, "mix", 3 * k + 4, it)
                    split_lo(dve, "mix", 3 * k + 5, it)
            merge(6, 0, "last", 0, 0)
            split_lo(dve, "out", 1, 0)
            merge_lo(6)
            merge(7, 1, "last", 1, 0)
            split_lo(dve, "out", 2, 0)
            merge_lo(7)

            def residual(half):
                taken(dve, "out", 4 * half + 3, 0)
                for i in range(TILES):
                    part = h[:, i, 512 * half:512 * half + 512]
                    dve.tensor_tensor(part, part, ps[:, 4 * half + i, :], ALU.add).then_inc(res, 1)

            split_lo(dve, "out", 3, 0)
            for j in (4, 5, 6):
                split_lo(dve, "out", j, 0)
            residual(0)
            split_lo(dve, "out", 7, 0)
            for j in range(3):
                split_lo(dve, "expert", j, 0)
            residual(1)

            dve.wait_ge(s_std2, 1)
            link(dve.reciprocal(rstd[:, 8:8 + TILES], std[:, 8:8 + TILES]))
            dve.wait_ge(s_gffn, 16)
            for i in range(TILES):
                if i >= 2:
                    dve.wait_ge(s_xt2, i - 1)
                    dve.wait_ge(s_xn2_out[i - 2], 16)
                dve.scalar_tensor_tensor(out=xn2[:, i % 2, :], in0=h[:, i, :], scalar=rstd[:, 8 + i:9 + i],
                                         in1=g_ffn[:, :], op0=ALU.mult, op1=ALU.mult).then_inc(s_xn2, 1)

            T = TILES

            def v2(name):
                return rt[name][:, :].rearrange("p (t n) -> p t n", t=T)

            def v3(name):
                return rt[name][:, :].rearrange("p (t g n) -> p t g n", t=T, g=GROUPS)

            def over(name, n):
                return rt[name][:, :].unsqueeze(2).to_broadcast([P, T, n])

            def row(name, n):
                return rt[name][:, :].unsqueeze(1).to_broadcast([P, T, n])

            def tt(o, a, b, op):
                link(dve.tensor_tensor(o, a, b, op))

            def reduce(o, a, op=ALU.add):
                link(dve.tensor_reduce(o, a, AX.X, op))

            def first_best(src, hot, best):
                reduce(rt[best][:, :], v2(src), ALU.max)
                tt(v2("cand"), v2(src), over(best, 4), ALU.is_equal)
                tt(v2("cand"), v2("cand"), row("desc", 4), ALU.mult)
                reduce(rt["best"][:, :], v2("cand"), ALU.max)
                tt(v2(hot), v2("cand"), over("best", 4), ALU.is_equal)

            dve.wait_ge(s_logit, T)
            dve.wait_ge(s_need, 1)
            link(dve.tensor_tensor(v2("logit"), ps[:, 7, 0:T * 20].rearrange("p (t n) -> p t n", t=T),
                                   bias_rt[:, :].unsqueeze(1).to_broadcast([P, T, 20]), ALU.add))
            link(dve.tensor_copy(v2("gtmp"), v2("logit")[:, :, 0:4]))
            first_best("gtmp", "ohg", "gmax")
            tt(v2("gtmp"), v2("gtmp"), over("gmax", 4), ALU.subtract)
            dve.sem_inc(s_gexp, 1)
            tt(v3("sel"), v2("logit")[:, :, 4:20].rearrange("p t (g n) -> p t g n", g=4),
               v2("ohg").unsqueeze(3).to_broadcast([P, T, 4, 4]), ALU.mult)
            reduce(v2("el"), v3("sel").rearrange("p t g n -> p t n g"))
            reduce(rt["best"][:, :], v2("el"), ALU.max)
            tt(v2("el"), v2("el"), over("best", 4), ALU.subtract)
            dve.sem_inc(s_gexp, 1)
            dve.wait_ge(s_hot, 1)
            reduce(rt["gsum"][:, :], v2("gtmp"))
            link(dve.reciprocal(rt["gsum"][:, :], rt["gsum"][:, :]))
            dve.wait_ge(s_hot, 2)
            first_best("ex", "oh1", "p1")
            link(dve.scalar_tensor_tensor(out=rt["ex"][:, :], in0=rt["oh1"][:, :], scalar=-4.0, in1=rt["ex"][:, :],
                                          op0=ALU.mult, op1=ALU.add))
            first_best("ex", "oh2", "p2")
            tt(rt["psum12"][:, :], rt["p1"][:, :], rt["p2"][:, :], ALU.add)
            link(dve.reciprocal(rt["psum12"][:, :], rt["psum12"][:, :]))
            tt(rt["psum12"][:, :], rt["psum12"][:, :], rt["gsum"][:, :], ALU.mult)
            tt(w_tok[:, 0, :], rt["p1"][:, :], rt["psum12"][:, :], ALU.mult)
            tt(w_tok[:, 1, :], rt["p2"][:, :], rt["psum12"][:, :], ALU.mult)
            for hot, full in (("oh1", "H1"), ("oh2", "H2")):
                tt(v3(full), v2("ohg").unsqueeze(3).to_broadcast([P, T, 4, 4]),
                   v2(hot).unsqueeze(2).to_broadcast([P, T, 4, 4]), ALU.mult)
            tt(H_bf[:, :, :], v2("H1"), v2("H2"), ALU.add)
            dve.sem_inc(s_hotx, 1)
            dve.wait_ge(s_rank, 1)
            link(dve.tensor_copy(v2("rank"), ps[:, 6, 0:T * E].rearrange("p (t n) -> p t n", t=T)))
            link(dve.tensor_copy(rt["cnt"][:, :], ps[:, 6, T * E:T * E + E]))
            link(dve.tensor_scalar(rt["ovn"][:, :], rt["cnt"][:, :], float(P), None, ALU.is_gt))
            for k in range(2, TILES):
                link(dve.tensor_scalar(rt["t3"][:, :], rt["cnt"][:, :], float(k * P), None, ALU.is_gt))
                tt(rt["ovn"][:, :], rt["ovn"][:, :], rt["t3"][:, :], ALU.add)
            link(dve.tensor_tensor_scan(rt["cum"][:, :], rt["onesE"][:, :], rt["ovn"][:, :], 0.0, ALU.mult, ALU.add))
            tt(rt["cumx"][:, :], rt["cum"][:, :], rt["ovn"][:, :], ALU.subtract)
            bex = rt["bex"][:, :].rearrange("p (b n) -> p b n", n=E)
            tt(bex, rt["cum"][:, :].unsqueeze(1).to_broadcast([P, OVER + 1, E]),
               rt["bidx"][:, :].unsqueeze(2).to_broadcast([P, OVER + 1, E]), ALU.is_le)
            reduce(rt["bexi"][:, :], bex)
            link(dve.tensor_scalar(rt["bexi"][:, :], rt["bexi"][:, :], float(E - 1), None, ALU.min))
            link(dve.tensor_copy(regs[:, 1:], rt["bexi"][:, :]))
            dve.tensor_copy(regs[:, 0:1], rt["cum"][:, E - 1:E]).then_inc(s_regs, 1)
            link(dve.tensor_scalar(v2("fb"), v2("rank"), float(P), None, ALU.is_ge))
            link(dve.tensor_scalar(rt["t3"][:, :], rt["cumx"][:, :], float(E - 1), None, ALU.add))
            tt(rt["t3"][:, :], rt["t3"][:, :], rt["eidx"][:, :], ALU.subtract)
            tt(v2("t1"), v2("fb"), row("t3", E), ALU.mult)
            tt(v2("t1"), v2("t1"), row("eidx", E), ALU.add)
            for k in range(2, TILES):
                link(dve.tensor_scalar(v2("t2"), v2("rank"), float(k * P), None, ALU.is_ge))
                tt(v2("fb"), v2("fb"), v2("t2"), ALU.add)
            tt(v2("t1"), v2("t1"), v2("fb"), ALU.add)
            link(dve.scalar_tensor_tensor(out=rt["rank"][:, :], in0=rt["fb"][:, :], scalar=-float(P),
                                          in1=rt["rank"][:, :], op0=ALU.mult, op1=ALU.add))
            link(dve.scalar_tensor_tensor(out=rt["t2"][:, :], in0=rt["t1"][:, :], scalar=float(P),
                                          in1=rt["rank"][:, :], op0=ALU.mult, op1=ALU.add))
            link(dve.scalar_tensor_tensor(out=rt["t1"][:, :], in0=rt["rank"][:, :], scalar=float(ICOLS),
                                          in1=rt["t1"][:, :], op0=ALU.mult, op1=ALU.add))
            for k, full in enumerate(("H1", "H2")):
                for src, dst in (("t2", slot_y), ("t1", slot_t)):
                    tt(v2("sel"), v2(full), v2(src), ALU.mult)
                    reduce(rt["best"][:, :], v2("sel"))
                    link(dve.tensor_copy(dst[:, k, :], rt["best"][:, :]))
            dve.sem_inc(s_slot, 1)

            def inputs_lo(b, half):
                dve.wait_ge(xe_hi, b * 2 + half + 1)
                dve.tensor_tensor(xeT_lo[:, 4 * half:4 * half + 4, :],
                                  ps[:, half, :].rearrange("p (k n) -> p k n", n=P),
                                  xeT_hi[:, 4 * half:4 * half + 4, :].bitcast(F32), ALU.subtract).then_inc(xe_lo, 1)

            def expert_dve(name, it, b):
                for j in range(3, 11):
                    split_lo(dve, name, j, it)
                taken(dve, name, 7, it)
                dve.wait_ge(silu, b + 1 + CR)
                dve.tensor_tensor(hdn[:, :], silu_g[:, :], ps[:, 3, :], ALU.mult).then_inc(hdn_done, 1)
                split_lo(dve, name, 11, it)
                inputs_lo(b + 1, 0)
                dve.wait_ge(ht_hi, b + 1)
                dve.tensor_tensor(hT_lo[:, :, :], ps[:, 4, :].rearrange("p (f n) -> p f n", n=P),
                                  hT_hi[:, :, :].bitcast(F32), ALU.subtract).then_inc(ht_lo, 1)
                inputs_lo(b + 1, 1)
                for j in range(12, 15):
                    split_lo(dve, name, j, it)

            inputs_lo(0, 0)
            inputs_lo(0, 1)
            with dve.Fori(0, E) as b:
                expert_dve("expert", b, b)
            count = dve.value_load(regs[0:1, 0:1], min_val=0, max_val=OVER)
            with dve.Fori(0, OVER) as b:
                with dve.If(b < count):
                    expert_dve("over", b, b + E)

            dve.wait_ge(s_gfin, 16)
            for i in range(TILES):
                for k, s in ((0, sum1), (1, sum2)):
                    dve.wait_ge(pick_sem[k], 16 * (i + 1))
                    dve.scalar_tensor_tensor(out=h[:, i, :], in0=pick[:, k, :], scalar=w_tok[:, k, i:i + 1],
                                             in1=h[:, i, :], op0=ALU.mult, op1=ALU.add).then_inc(s, 1)
                    dve.wait_ge(s, i + 1)
                dve.wait_ge(s_std3, i + 1)
                link(dve.reciprocal(rstd[:, 12 + i:13 + i], std[:, 12 + i:13 + i]))
                if i:
                    dve.wait_ge(s_out, 16 * i)
                dve.scalar_tensor_tensor(out=fin[:, :], in0=h[:, i, :], scalar=rstd[:, 12 + i:13 + i],
                                         in1=g_fin[:, :], op0=ALU.mult, op1=ALU.mult).then_inc(s_fin, 1)

        @block.tensor
        def _(pe):
            for s in (used, t_done, av_done):
                pe.sem_inc(s, CR)
            pe.wait_ge(s_const, 1)

            for i in range(TILES + 1):
                n = P if i < TILES else META
                pe.wait_ge(s_xn, i + 1)
                if i == TILES:
                    pe.wait_ge(s_xlo, 1)
                src = xn[0:n, i % 2, :].rearrange("p (q k) -> p k q", k=KB)
                for k in range(KB):
                    dst = ps[:, 2 * i + k // 4, (k % 4) * P:(k % 4 + 1) * P] if i < TILES else \
                        ps[:, 0, k * META:(k + 1) * META]
                    last = pe.transpose(dst, src[:, k, :], ident[0:n, 0:n])
                last.then_inc(s_xt, 1)
            pe.wait_ge(s_xlo, 2)
            n = TAPS + 3
            for c in range(PAIRS):
                last = pe.transpose(ps[:, 2, c * n:(c + 1) * n], pack[0:n, c * P:(c + 1) * P], ident[0:n, 0:n])
            last.then_inc(s_cwt, 1)
            pe.wait_ge(s_xlo, TILES + 1)
            pe.wait_ge(s_cw, 1)

            def channels_by_tokens(name, j, it, outs):
                hi, lo = weights(pe, name, j, it, P)
                for dst, tok in outs:
                    for k in range(KB):
                        last = product(pe, dst, (hi[:, k, :], lo[:, k, :]), (xnT_hi[:, k, tok], xnT_lo[:, k, tok]),
                                       k == 0, k == KB - 1)
                return last

            all_tokens = [slice(0, HALF), slice(HALF, L)]

            with pe.Fori(0, PAIRS) as c:
                def project(j, outs, count=None):
                    last = channels_by_tokens("pair", j, c, outs)
                    last.then_inc(used, 1)

                pe.wait_ge(ev, c * 5 + CR)
                project(0, [(ps[:, 3 + b, 0:HALF], all_tokens[b]) for b in range(2)])
                pe.wait_ge(sig_done, c * 8 - 1 + CR)
                project(1, [(ps[:, b, 0:HALF], all_tokens[b]) for b in range(2)])
                pe.wait_ge(sig_done, c * 8 + CR)
                project(2, [(ps[:, 2, :], slice(META, L))])
                pe.wait_ge(ev, c * 5 + 1 + CR)
                project(3, [(ps[:, 3 + b, 0:HALF], all_tokens[b]) for b in range(2)])

                def scores(u):
                    hh, i = u // 4, 3 - u % 4
                    if u >= 2:
                        pe.wait_ge(sig_done, c * 8 + u - 1 + CR)
                    q = qT[hh * DH:(hh + 1) * DH, i * P:(i + 1) * P]
                    n = META + (i + 1) * P
                    for b, (lo, hi) in enumerate([(0, HALF), (HALF, L)] if i == 3 else [(0, n)]):
                        dst = ps[:, 2 * (u % 2) + b, :]
                        pe.matmul(dst[:, 0:hi - lo], q, kT[hh * DH:(hh + 1) * DH, lo:hi], start=True, stop=hi < n)
                    last = pe.matmul(dst[:, hi - lo - P:hi - lo], ident_bf[:, :], mask_bf[:, :], start=False, stop=True)
                    last.then_inc(z_done, 1)

                def turn(u):
                    i, ub = 3 - u % 4, u % 2
                    off = L - META - (i + 1) * P
                    pe.wait_ge(prob_done, c * 8 + u + 1 + CR)
                    if u:
                        pe.wait_ge(tev, c * 8 + u + CR)
                    if u == 4:
                        pe.wait_ge(mev, c * 2 + 1 + CR)
                    pe.transpose(ps[0:META, 6, i * P:(i + 1) * P], sig[:, ub, off:off + META], ident[:, :])
                    for j in range(i + 1):
                        at_ = off + META + j * P
                        last = pe.transpose(ps[:, 5, j * P:(j + 1) * P], sig[:, ub, at_:at_ + P], ident[:, :])
                    last.then_inc(t_done, 1)

                def values(hh):
                    pe.wait_ge(mev, c * 2 + hh + 1 + CR)
                    pe.wait_ge(tev, c * 8 + 4 * hh + 4 + CR)
                    if hh == 0:
                        pe.wait_ge(av_lo, c + CR)
                    rows = slice(hh * DH, (hh + 1) * DH)
                    pe.matmul(ps[rows, 7, :], v_meta[:, rows], probT_meta[:, :], start=True, stop=False)
                    for j in range(TILES):
                        last = pe.matmul(ps[rows, 7, j * P:], v_sb[:, j, rows], probT[:, j, j * P:], start=False,
                                         stop=(j == TILES - 1))
                    last.then_inc(av_done, 1)

                pe.wait_ge(ev, c * 5 + 3 + CR)
                scores(0)
                scores(1)
                pe.wait_ge(tev, c * 8 + CR)
                pe.wait_ge(mev, c * 2 + CR)
                hi, lo = weights(pe, "pair", 4, c, P)
                for j in range(TILES + 1):
                    tok = slice(META + j * P, META + (j + 1) * P) if j < TILES else slice(0, META)
                    dst = ps[:, 5, j * P:(j + 1) * P] if j < TILES else ps[0:META, 6, 0:P]
                    for k in range(KB):
                        last = product(pe, dst, (xnT_hi[:, k, tok], xnT_lo[:, k, tok]), (hi[:, k, :], lo[:, k, :]),
                                       k == 0, k == KB - 1)
                last.then_inc(used, 1)
                pe.wait_ge(ev, c * 5 + 5 + CR)
                for u in range(8):
                    turn(u)
                    if u + 2 < 8:
                        scores(u + 2)
                    if u == 3:
                        values(0)
                values(1)

            def gate(name, j, it, k, count):
                pe.wait_ge(g_ev, count - 1 + CR)
                last = channels_by_tokens(name, j, it, [(ps[:, 2 * k, :], slice(META, L))])
                last.then_inc(used, 1)

            gate("gate", 0, 0, 0, 0)
            gate("gate", 1, 0, 1, 1)
            gate("gate", 2, 0, 0, 2)
            pe.wait_ge(conv_done, PAIRS + CR)
            for m in range(PAIRS):
                last = pe.matmul(ps[:, 5, :], mean_w[:, :], y[:, m, :], start=(m == 0), stop=(m == PAIRS - 1))
            last.then_inc(ln_mean, 1)
            gate("gate", 3, 0, 1, 3)
            for m in range(PAIRS):
                pe.wait_ge(ln_sq, m + 1)
                pe.matmul(ps[:, 6, :], mean_w[:, :], silu_y[:, m % 2, :], start=(m == 0), stop=(m == PAIRS - 1))\
                  .then_inc(ln_var, 1)

            def branches(name, j, it, m):
                hi, lo = weights(pe, name, j, it, P)
                if not isinstance(m, int) or m:
                    pe.wait_ge(br_ev, m * 2 + CR)
                else:
                    pe.wait_ge(av_lo, PAIRS + CR)
                for b, (left_hi, left_lo) in enumerate(((attT_hi, attT_lo), (yT_hi, yT_lo))):
                    if b:
                        pe.wait_ge(ln_lo, PAIRS)
                    for c in range(PAIRS):
                        w = (hi[:, 4 * b + c, :], lo[:, 4 * b + c, :])
                        last = product(pe, ps[:, 3 + b, :], w, (left_hi[:, c, :], left_lo[:, c, :]), c == 0, c == PAIRS - 1)
                    if b == 0:
                        last.then_inc(br_done, 1)
                last.then_inc(used, 1)

            pe.wait_ge(av_lo, PAIRS + CR)
            with pe.Fori(0, 3) as it:
                for k in range(2):
                    branches("mix", 3 * k, it, it * 2 + k)
                    gate("mix", 3 * k + 1, it, 0, it * 4 + 4 + 2 * k)
                    gate("mix", 3 * k + 2, it, 1, it * 4 + 5 + 2 * k)
            for k in range(2):
                branches("last", k, 0, 6 + k)

            for half in range(2):
                if half == 0:
                    pe.wait_ge(g_ev, 16 + CR)
                    pe.wait_ge(br_ev, 14 + CR)
                for q in range(4):
                    hi, lo = weights(pe, "out", 4 * half + q, 0, 512)
                    for m2 in range(2):
                        m = 2 * q + m2
                        pe.wait_ge(m_lo, m + 1)
                        if half == 0 and m == 0:
                            pe.wait_ge(br_ev, 16 + CR)
                        for i in range(TILES):
                            tok = slice(i * P, (i + 1) * P)
                            last = product(pe, ps[:, 4 * half + i, :], (mT_hi[:, m, tok], mT_lo[:, m, tok]),
                                           (hi[:, m2, :], lo[:, m2, :]), m == 0, m == 2 * 4 - 1)
                    last.then_inc(used, 1)

            pe.wait_ge(s_small, 16 * 9)
            pe.wait_ge(res, 2 * TILES)
            for i in range(TILES):
                pe.wait_ge(s_xn2, i + 1)
                if i >= 2:
                    pe.wait_ge(s_xe2, i - 1)
                src = xn2[:, i % 2, :].rearrange("p (q k) -> p k q", k=KB)
                for k in range(KB):
                    last = pe.transpose(ps[:, 2 * (i % 2) + k // 4, (k % 4) * P:(k % 4 + 1) * P], src[:, k, :], ident[:, :])
                last.then_inc(s_xt2, 1)
                pe.wait_ge(s_xe2, i + 1)
                for k in range(KB):
                    last = pe.matmul(ps[:, 7, i * 20:(i + 1) * 20], xn2T[:, k, :], router_w[:, k, :], start=(k == 0),
                                     stop=(k == KB - 1))
                last.then_inc(s_logit, 1)
            pe.wait_ge(s_hotx, 1)
            for i in range(TILES + 1):
                for j in range(min(i + 1, TILES)):
                    last = pe.matmul(ps[:, 6, i * E:(i + 1) * E], (before_bf if j == i else ones_bf)[:, :], H_bf[:, j, :],
                                     start=(j == 0), stop=(j == min(i, TILES - 1)))
            last.then_inc(s_rank, 1)

            def inputs(b, half):
                pe.wait_ge(gath, b * 16 + 16)
                pe.wait_ge(xe_lo, b * 2 + half - 1 + CR)
                src = xe[:, :].rearrange("p (q k) -> p k q", k=KB)
                for k in range(4):
                    last = pe.transpose(ps[:, half, k * P:(k + 1) * P], src[:, 4 * half + k, :], ident[:, :])
                last.then_inc(tx, 1)

            def expert_pe(name, it, b):
                pe.wait_ge(xe_lo, b * 2 + 2 + CR)
                for part in range(2):
                    if part == 0:
                        pe.wait_ge(silu, b + CR)
                    else:
                        pe.wait_ge(hdn_done, b + CR)
                    for q in range(4):
                        hi, lo = weights(pe, name, 4 * part + q, it, FF)
                        for k2 in range(2):
                            k = 2 * q + k2
                            last = product(pe, ps[:, 2 + part, :], (xeT_hi[:, k, :], xeT_lo[:, k, :]),
                                           (hi[:, k2, :], lo[:, k2, :]), k == 0, k == KB - 1)
                        last.then_inc(used, 1)
                inputs(b + 1, 0)
                pe.wait_ge(hdn_done, b + 1 + CR)
                src = hdn[:, :].rearrange("p (q f) -> p f q", f=FB)
                for f in range(FB):
                    last = pe.transpose(ps[:, 4, f * P:(f + 1) * P], src[:, f, :], ident[:, :])
                last.then_inc(ht, 1)
                inputs(b + 1, 1)
                pe.wait_ge(ht_lo, b + 1)
                pe.wait_ge(yev, b + CR)
                for f in range(FB):
                    hi, lo = weights(pe, name, 8 + f, it, 512)
                    for c in range(2):
                        last = product(pe, ps[:, 5 + c, :], (hT_hi[:, f, :], hT_lo[:, f, :]), (hi[:, c, :], lo[:, c, :]),
                                       f == 0, f == FB - 1)
                    last.then_inc(used, 1)

            inputs(0, 0)
            inputs(0, 1)
            with pe.Fori(0, E) as b:
                expert_pe("expert", b, b)
            pe.wait_ge(s_regs, 1)
            count = pe.value_load(regs[0:1, 0:1], min_val=0, max_val=OVER)
            with pe.Fori(0, OVER) as b:
                with pe.If(b < count):
                    expert_pe("over", b, b + E)


_INS = ["x", "meta", "norm_mix", "w_in", "w_sb_o", "conv_w", "conv_b", "conv_ln_g", "conv_ln_b", "w_conv_o", "w_out",
        "norm_ffn", "w_router_group", "b_router_group", "w_router_expert", "b_router_expert", "w_gate", "w_up", "w_down",
        "norm_final"]


def kernel(**inputs):
    import numpy as np
    import concourse.bacc as bacc
    from concourse.bass_utils import run_bass_kernel_spmd

    nc = bacc.Bacc("TRN2", target_bir_lowering=False, num_devices=1)
    arrays, args = {}, []
    for name in _INS:
        a = np.ascontiguousarray(inputs[name])
        arrays[f"in_{name}"] = a
        args.append(nc.dram_tensor(f"in_{name}", a.shape, mybir.dt.from_np(a.dtype), kind="ExternalInput").ap())
    args.append(nc.dram_tensor("out", (1, SEQ, D), F32, kind="ExternalOutput").ap())
    args.append(nc.dram_tensor("xn2_dram", (SEQ, D), F32, kind="Internal").ap())
    args.append(nc.dram_tensor("index_dram", (P * ICOLS, 1), I32, kind="Internal").ap())
    args.append(nc.dram_tensor("y_dram", (BLOCKS * P, D), F32, kind="Internal").ap())
    build(nc, *args)
    return run_bass_kernel_spmd(nc, [arrays], core_ids=[0]).results[0]["out"]
```

```python
from contextlib import ExitStack

import concourse.bass as bass
from concourse import mybir

F32 = mybir.dt.float32
F32R = mybir.dt.float32r
BF16 = mybir.dt.bfloat16
I32 = mybir.dt.int32
U32 = mybir.dt.uint32
ALU = mybir.AluOpType
ACT = mybir.ActivationFunctionType
AX = mybir.AxisListType
ds = bass.ds

P = 128
D = 1024
KB = D // P
SEQ = 512
META = 16
L = META + SEQ
TILES = SEQ // P
HALF = L // 2
DH = 64
PAIRS = 4
CONV = 512
TAPS = 31
HIST = TAPS - 1
EPS = 1e-6
SCALE = DH ** -0.5
MASKED = -1e30
COL_Q, COL_K, COL_V, COL_A, COL_B, COL_GSB, COL_GCV = 0, 512, 1024, 1536, 2048, 2560, 3584
GROUPS, PER_GROUP = 4, 4
E = GROUPS * PER_GROUP
FF = 512
FB = FF // P
TOP = 2
OVER = (TOP * SEQ - 2) // P
BLOCKS = E + OVER
ICOLS = BLOCKS + 3
CHUNK = 1024
CR = 24


class Stream:

    def __init__(self, segments):
        self.seg, g, taken = {}, 0, {}
        last_raw, last_split = {}, {}
        for name, iters, slots, peeled in segments:
            per = {r: sum(1 for a, _ in slots if a == r) for r, _ in slots}
            info = {"peeled": peeled, "g": g, "n": len(slots), "slots": slots, "per": per, "base": dict(taken), "raw": [99] * len(slots),
                    "split": [99] * len(slots), "first": [99] * len(slots)}
            for it in range(iters):
                for j, (r, s) in enumerate(slots):
                    dist = "first" if peeled and it == 0 else "raw"
                    info[dist][j] = min(info[dist][j], g - last_raw.get(r, g - CR))
                    info["split"][j] = min(info["split"][j], g - last_split.get(s, g - CR))
                    last_raw[r], last_split[s] = g, g
                    taken[r] = taken.get(r, 0) + 1
                    g += 1
            self.seg[name] = info

    def at(self, name, j, it):
        info = self.seg[name]
        if j >= info["n"]:
            j, it = j - info["n"], it + 1
        r, s = info["slots"][j]
        before = sum(1 for a, _ in info["slots"][:j] if a == r)
        loads = it * info["per"][r] + info["base"].get(r, 0) + before + 1
        dist = info["first" if info["peeled"] and isinstance(it, int) and it == 0 else "raw"]
        return it * info["n"] + info["g"] + j, r, s, loads, min(dist[j], CR), min(info["split"][j], CR)


RAW, SPLIT = 24, 6
AHEAD = 5
STREAM = Stream([
    ("pair", PAIRS, [(0, 0), (1, 1), (2, 2), (3, 3), (4, 1)], False),
    ("gate", 1, [(0, 0), (1, 1), (2, 2), (3, 3), (4, 1), (5, 2)], False),
    ("mix", 2, [(0, 0), (1, 1), (2, 2), (3, 0), (4, 1), (5, 2)], False),
    ("last", 1, [(0, 0), (1, 1), (2, 2), (3, 3), (4, 0), (5, 1)], False),
    ("out", 1, [(0, 2), (1, 3), (2, 0), (3, 1), (4, 2), (5, 3), (3, 2), (4, 3)], False),
    ("expert", E // 2, [(j, j % SPLIT) for j in range(24)], True),
    ("over", OVER, [(j, j % SPLIT) for j in range(12)], False),
])


def build(nc, x, meta, norm_mix, w_in, w_sb_o, conv_w, conv_b, conv_ln_g, conv_ln_b, w_conv_o, w_out, norm_ffn,
          w_router_group, b_router_group, w_router_expert, b_router_expert, w_gate, w_up, w_down, norm_final, out,
          xn2_dram, y_dram):
    with ExitStack() as ctx:
        ctx.enter_context(nc.allow_non_contiguous_dma(reason="small vectors"))
        at = [0]

        def sb(name, shape, dt=F32):
            n = 1
            for k in shape[1:]:
                n *= k
            t = nc.alloc_sbuf_tensor_at(name, shape, dt, offset=at[0])
            at[0] += -(-n * (2 if dt == BF16 else 4) // 32) * 32
            return t

        def sem(name):
            return ctx.enter_context(nc.semaphore(name))

        at[0] = -(-nc.sbuf_base // 32) * 32
        raw = [sb(f"raw{i}", [P, CHUNK]) for i in range(6)]
        w_hi = [sb(f"w_hi{i}", [P, CHUNK], F32R) for i in range(4)]
        w_lo = [sb(f"w_lo{i}", [P, CHUNK], F32R) for i in range(4)]
        h = sb("h", [P, TILES, D])
        ident = sb("ident", [P, P])
        ident_bf = sb("ident_bf", [P, P], BF16)
        mask_bf = sb("mask_bf", [P, P], BF16)
        before_bf = sb("before_bf", [P, P], BF16)
        ones_bf = sb("ones_bf", [P, P], BF16)
        mean_w = sb("mean_w", [P, P])
        ones_row = sb("ones_row", [P, L])
        eps = sb("eps", [P, 1])
        table = sb("table", [P, 1])
        zero_row = sb("zero_row", [P, D // 4])
        sumsq = sb("sumsq", [P, 16])
        std = sb("std", [P, 16])
        rstd = sb("rstd", [P, 16])
        w_tok = sb("w_tok", [P, TOP, TILES])
        slot_y = sb("slot_y", [P, TOP, TILES], U32)
        regs = sb("regs", [P, 2 + OVER], I32)
        cw = sb("cw", [P, PAIRS, TAPS + 3])
        router_w = sb("router_w", [P, KB, GROUPS + E])
        bias_rt = sb("bias_rt", [P, GROUPS + E])
        region = at[0]
        attT_hi = sb("attT_hi", [P, PAIRS, SEQ], F32R)
        attT_lo = sb("attT_lo", [P, PAIRS, SEQ], F32R)
        vT = nc.alloc_sbuf_tensor_at("vT", [P, L], F32, offset=at[0])
        sgate = sb("sgate", [P, 2, SEQ])
        cgate = sb("cgate", [P, 2, SEQ])
        merged = sb("merged", [P, SEQ])
        y = sb("y", [P, PAIRS, SEQ])
        region_end = at[0]
        at[0] = region
        raw += [sb(f"raw{i}", [P, CHUNK]) for i in range(6, 12)]
        w_hi.append(sb("w_hi4", [P, CHUNK], F32R))
        w_lo.append(sb("w_lo4", [P, CHUNK], F32R))
        assert at[0] <= region_end
        at[0] = region_end
        region = at[0]
        xnT_hi = sb("xnT_hi", [P, KB, L], F32R)
        xnT_lo = sb("xnT_lo", [P, KB, L], F32R)
        region_end = at[0]
        at[0] = region
        g_ffn = sb("g_ffn", [P, D])
        square2 = sb("square2", [P, D])
        xn2 = sb("xn2", [P, TILES, D])
        rt = {}
        for name, n in (("logit", TILES * 20), ("ohg", TILES * 4), ("gtmp", TILES * 4), ("gsum", TILES), ("gmax", TILES),
                        ("cand", TILES * 4), ("best", TILES), ("sel", TILES * E), ("el", TILES * 4), ("ex", TILES * 4),
                        ("oh1", TILES * 4), ("oh2", TILES * 4), ("p1", TILES), ("p2", TILES), ("psum12", TILES),
                        ("H12", TOP * TILES * E), ("sel_t1", TOP * TILES * E), ("sel_place_of", TOP * TILES * E), ("place_of", TILES * E), ("block", TOP * TILES), ("place", TOP * TILES),
                        ("row", TOP * TILES), ("hot", TOP * TILES * ICOLS), ("number", P), ("token", TOP * TILES), ("fb", TILES * E), ("t1", TILES * E),
                        ("t2", TILES * E), ("ovn", E), ("cum", E), ("t3", E), ("bex", (OVER + 1) * E),
                        ("bexi", OVER + 1), ("desc", 4), ("eidx", E), ("rest", E), ("bidx", OVER + 1), ("onesE", E), ("over3", E * (TILES - 1)), ("ge3", TILES * E * (TILES - 1)), ("steps", TILES - 1)):
            rt[name] = sb("rt_" + name, [P, n])
        H_bf = sb("H_bf", [P, TILES, E], BF16)
        assert at[0] <= region_end, (at[0], region_end)
        at[0] = region
        late = {i: sb(f"raw{i}", [P, CHUNK]) for i in (14, 15, 16, 17, 18, 19, 22, 23)}
        assert at[0] <= region_end, (at[0], region_end)
        at[0] = region_end
        region = at[0]
        sig = sb("sig", [P, 3, L])
        stay = sb("stay", [P, 3, L + 1])
        after = sb("after", [P, 3, L])
        probT = sb("probT", [P, TILES, SEQ])
        probT_meta = sb("probT_meta", [META, SEQ])
        qT = sb("qT", [P, SEQ])
        kT = sb("kT", [P, L])
        v_sb = sb("v_sb", [P, TILES, P])
        v_meta = sb("v_meta", [META, P])
        attention_end = at[0]
        at[0] = region
        mT_hi = sb("mT_hi", [P, KB, SEQ], F32R)
        mT_lo = sb("mT_lo", [P, KB, SEQ], F32R)
        region_end = max(at[0], attention_end)
        sq_ln = nc.alloc_sbuf_tensor_at("sq_ln", [P, PAIRS, SEQ], F32, offset=region)
        at[0] = region
        xe = sb("xe", [P, D])
        xeT_hi = sb("xeT_hi", [P, KB, P], F32R)
        xeT_lo = sb("xeT_lo", [P, KB, P], F32R)
        silu_g = sb("silu_g", [P, FF])
        hdn = sb("hdn", [P, FF])
        hT_hi = sb("hT_hi", [P, FB, P], F32R)
        hT_lo = sb("hT_lo", [P, FB, P], F32R)
        y_sb = sb("y_sb", [P, D])
        index_sb = sb("index_sb", [P, ICOLS], I32)
        index_1 = sb("index_1", [P, 1], U32)
        w_hi.append(sb("w_hi5", [P, CHUNK], F32R))
        w_lo.append(sb("w_lo5", [P, CHUNK], F32R))
        assert at[0] <= region_end
        at[0] = region_end
        region = at[0]
        a_sb = sb("a_sb", [P, L])
        b_sb = sb("b_sb", [P, L])
        u_pad = sb("u_pad", [P, HIST + L])
        y_acc = sb("y_acc", [P, SEQ])
        cw_c = sb("cw_c", [P, TAPS + 3])
        conv_end = at[0]
        block_hot = nc.alloc_sbuf_tensor_at("block_hot", [P, TOP * TILES, ICOLS], F32R, offset=region + 4 * SEQ)
        late.update({20 + i: nc.alloc_sbuf_tensor_at(f"raw{20 + i}", [P, CHUNK], F32, offset=region + i * 4 * CHUNK)
                     for i in range(2)})
        assert region + 2 * 4 * CHUNK <= conv_end
        logitT = nc.alloc_sbuf_tensor_at("logitT", [GROUPS + E, SEQ], F32, offset=region)
        at[0] = region
        rstd_ln = sb("rstd_ln", [P, SEQ])
        silu_y = sb("silu_y", [P, 2, SEQ])
        at[0] = max(conv_end, at[0])
        region = at[0]
        x_meta = sb("x_meta", [META, D])
        xn = sb("xn", [P, 2, D])
        g_mix = sb("g_mix", [P, D])
        pack = sb("pack", [TAPS + 3, CONV])
        norm_end = at[0]
        at[0] = region
        yT_hi = sb("yT_hi", [P, PAIRS, SEQ], F32R)
        yT_lo = sb("yT_lo", [P, PAIRS, SEQ], F32R)
        at[0] = region
        pick = sb("pick", [P, 2, D])
        late.update({12 + i: nc.alloc_sbuf_tensor_at(f"raw{12 + i}", [P, CHUNK], F32, offset=region + i * 4 * CHUNK)
                     for i in range(2)})
        raw += [late[i] for i in range(12, RAW)]
        xn2T = nc.alloc_sbuf_tensor_at("xn2T", [P, 2, KB, P], F32, offset=region)
        g_fin = sb("g_fin", [P, D])
        place_hot = sb("place_hot", [P, TOP * TILES, P], F32R)
        at[0] = max(at[0], norm_end)
        assert at[0] <= nc.sbuf_usable_end, (at[0], nc.sbuf_usable_end)
        square = y

        ps = ctx.enter_context(nc.psum_tensor("ps", [P, 8, 512], F32))

        s_const = sem("s_const")
        s_x = [sem(f"s_x{i}") for i in range(TILES + 1)]
        s_gmix = sem("s_gmix")
        s_pack = sem("s_pack")
        s_router = sem("s_router")
        s_sq = sem("s_sq")
        s_std = sem("s_std")
        s_rstd = sem("s_rstd")
        s_xn = sem("s_xn")
        s_xt = sem("s_xt")
        s_xhi = sem("s_xhi")
        s_xlo = sem("s_xlo")
        s_cwt = sem("s_cwt")
        s_cw = sem("s_cw")
        load = [sem(f"load{i}") for i in range(RAW)]
        hi_done = sem("hi_done")
        lo_done = sem("lo_done")
        used = sem("used")
        ev = sem("ev")
        z_done = sem("z_done")
        sig_done = sem("sig_done")
        scan_done = sem("scan_done")
        prob_done = sem("prob_done")
        t_done = sem("t_done")
        tev = sem("tev")
        mev = sem("mev")
        vt_done = sem("vt_done")
        v_ev = sem("v_ev")
        av_done = sem("av_done")
        av_hi = sem("av_hi")
        av_lo = sem("av_lo")
        u_done = sem("u_done")
        cwc = sem("cwc")
        conv_done = sem("conv_done")
        g_ev = sem("g_ev")
        ln_mean = sem("ln_mean")
        ln_xc = sem("ln_xc")
        ln_sq = sem("ln_sq")
        ln_var = sem("ln_var")
        ln_std = sem("ln_std")
        ln_rstd = sem("ln_rstd")
        ln_n = sem("ln_n")
        ln_act = sem("ln_act")
        ln_hi = sem("ln_hi")
        ln_lo = sem("ln_lo")
        br_done = sem("br_done")
        br_ev = sem("br_ev")
        m_hi = sem("m_hi")
        m_lo = sem("m_lo")
        out_done = sem("out_done")
        res = sem("res")
        s_sq2 = sem("s_sq2")
        s_std2 = sem("s_std2")
        s_xn2 = sem("s_xn2")
        s_xn2_out = [sem(f"s_xn2_out{i}") for i in range(TILES)]
        s_xt2 = sem("s_xt2")
        s_xe2 = sem("s_xe2")
        s_logit = sem("s_logit")
        s_lcopy = sem("s_lcopy")
        s_lturn = sem("s_lturn")
        s_gffn = sem("s_gffn")
        s_gexp = sem("s_gexp")
        s_need = sem("s_need")
        s_hot = sem("s_hot")
        s_rank = sem("s_rank")
        s_hotx = sem("s_hotx")
        br_mul = sem("br_mul")
        s_slot = sem("s_slot")
        s_yzero = sem("s_yzero")
        s_place = sem("s_place")
        s_table = sem("s_table")
        s_regs = sem("s_regs")
        s_rows = sem("s_rows")
        s_weights = sem("s_weights")
        idx1 = sem("idx1")
        gath = sem("gath")
        tx = sem("tx")
        xe_hi = sem("xe_hi")
        xe_lo = sem("xe_lo")
        silu = sem("silu")
        hdn_done = sem("hdn_done")
        ht = sem("ht")
        ht_hi = sem("ht_hi")
        ht_lo = sem("ht_lo")
        yev = sem("yev")
        ystore = sem("ystore")
        y_free = sem("y_free")
        pick_sem = [[sem(f"pick{k}_{i}") for i in range(TILES)] for k in range(TOP)]
        sum1 = sem("sum1")
        sum2 = sem("sum2")
        s_sq3 = sem("s_sq3")
        s_std3 = sem("s_std3")
        s_recip3 = sem("s_recip3")
        s_r3 = sem("s_r3")
        s_fin_last = sem("s_fin_last")
        s_fin = sem("s_fin")
        s_out = sem("s_out")
        s_gfin = sem("s_gfin")
        passed = sem("passed")
        dchain = sem("dchain")
        pchain = sem("pchain")

        def cols(w, n):
            return w.rearrange("p (k n) -> p k n", n=n)

        def w_in_cols(col):
            return w_in[0].rearrange("(p k) n -> p k n", k=KB)[:, :, col]

        def split_hi(act, name, j, it):
            g, r, s, loads, _, back = STREAM.at(name, j, it)
            act.wait_ge(load[r], loads * 32)
            act.wait_ge(used, g - back + 1 + CR)
            act.copy(w_hi[s][:, :], raw[r][:, :]).then_inc(hi_done, 1)

        def split_lo(dve, name, j, it):
            g, r, s, _, _, _ = STREAM.at(name, j, it)
            dve.wait_ge(hi_done, g + 1)
            dve.tensor_tensor(w_lo[s][:, :], raw[r][:, :], w_hi[s][:, :].bitcast(F32), ALU.subtract)\
               .then_inc(lo_done, 1)

        def weights(pe, name, j, it, n):
            g, _, s, _, _, _ = STREAM.at(name, j, it)
            pe.wait_ge(lo_done, g + 1 + CR)
            return cols(w_hi[s][:, :], n), cols(w_lo[s][:, :], n)

        def taken(eng, name, j, it):
            eng.wait_ge(used, STREAM.at(name, j, it)[0] + 1 + CR)

        def product(pe, dst, left, right, start, stop):
            pe.matmul(dst, left[0], right[0], start=start, stop=False)
            pe.matmul(dst, left[0], right[1], start=False, stop=False)
            return pe.matmul(dst, left[1], right[0], start=False, stop=stop)

        gate_bank = [(0, 2), (1, 7)]
        branch_bank = [(3, 4), (5, 6)]
        out_bank = [3, 4, 0, 2, 1, 7, 5, 6]
        turn_bank = [5, 1]

        def last_user(u):
            return u - 2 if u >= 3 else (-1, 0, -2)[u]

        ht_bank = [ps[:, 4, 0:2 * P], ps[:, 7, 0:2 * P]]

        def picked(k, i):
            return xn2[:, i, :] if k == 0 else pick[:, i % 2, :]

        def first_lo(dve, i):
            if i < TILES:
                src = ps[:, 2 * i:2 * i + 2, :].rearrange("p b (k n) -> p (b k) n", n=P)
                to = slice(META + i * P, META + (i + 1) * P)
            else:
                src, to = ps[:, 0, 0:KB * META].rearrange("p (k n) -> p k n", n=META), slice(0, META)
            dve.wait_ge(s_xhi, i + 1)
            dve.tensor_tensor(xnT_lo[:, :, to], src, xnT_hi[:, :, to].bitcast(F32), ALU.subtract).then_inc(s_xlo, 1)

        block = ctx.enter_context(nc.Block())

        @block.sync
        def _(sp):
            for i in range(TILES):
                sp.dma_start(h[:, i, :], x[0, i * P:(i + 1) * P, :]).then_inc(s_x[i], 16)
            sp.dma_start(x_meta[:, :], meta).then_inc(s_x[TILES], 16)

            def chunk(name, j, it, pieces):
                g, r, _, _, back, _ = STREAM.at(name, j, it)
                sp.wait_ge(lo_done, g - back + 1 + CR)
                sp.sem_inc(passed, 1)
                sp.dma_start(*pieces(raw[r])).then_inc(load[r], 32)

            def in_cols(col):
                return lambda slot: (cols(slot[:, :], P), w_in_cols(col))

            def branch_chunk(name, j, it, m):
                g, r, _, _, back, _ = STREAM.at(name, j, it)
                sp.wait_ge(lo_done, g - back + 1 + CR)
                sp.sem_inc(passed, 1)
                v = raw[r][:, :].rearrange("p (b c n) -> p b c n", b=2, n=P)
                sp.dma_start(v[:, 0], w_sb_o[0].rearrange("(c p) n -> p c n", p=P)[:, :, ds(m * P, P)])\
                  .then_inc(load[r], 16)
                sp.dma_start(v[:, 1], w_conv_o[0].rearrange("(c p) n -> p c n", p=P)[:, :, ds(m * P, P)])\
                  .then_inc(load[r], 16)

            with sp.Fori(0, PAIRS) as c:
                for j, col in enumerate((COL_A, COL_K, COL_Q, COL_B, COL_V)):
                    chunk("pair", j, c, in_cols(ds(c * P + col, P)))
            for m in range(3):
                chunk("gate", 2 * m, 0, in_cols(ds(COL_GSB + m * P, P)))
                chunk("gate", 2 * m + 1, 0, in_cols(ds(COL_GCV + m * P, P)))
            with sp.Fori(0, 2) as n:
                for k in range(2):
                    branch_chunk("mix", 3 * k, n, n * 2 + k)
                    chunk("mix", 3 * k + 1, n, in_cols(ds(n * (2 * P) + (COL_GSB + (k + 3) * P), P)))
                    chunk("mix", 3 * k + 2, n, in_cols(ds(n * (2 * P) + (COL_GCV + (k + 3) * P), P)))
            branch_chunk("last", 0, 0, 4)
            chunk("last", 1, 0, in_cols(ds(COL_GSB + 7 * P, P)))
            chunk("last", 2, 0, in_cols(ds(COL_GCV + 7 * P, P)))
            for k in range(3):
                branch_chunk("last", 3 + k, 0, 5 + k)
            wo = w_out[0].rearrange("(m p) n -> p m n", p=P)
            for half in range(2):
                for q in range(4):
                    chunk("out", 4 * half + q, 0, lambda slot: (
                        cols(slot[:, :], 512), wo[:, 2 * q:2 * q + 2, 512 * half:512 * half + 512]))

            def expert_loads(name, it, e, which):
                for j in which:
                    part, q = (j % 12) // 4, j % 4
                    if part < 2:
                        src = (w_gate, w_up)[part][0, ds(e, 1)].rearrange("e (p k) n -> p (e k) n", k=KB)
                        chunk(name, j, it, lambda slot: (cols(slot[:, :], FF), src[:, 2 * q:2 * q + 2, :]))
                    else:
                        src = w_down[0, ds(e, 1)].rearrange("e (f p) n -> p (e f) n", f=FB)
                        chunk(name, j, it, lambda slot: (slot[:, :], src[:, q, :]))

            expert_loads("expert", 0, 0, range(6))
            taken(sp, "last", 5, 0)
            sp.wait_ge(br_ev, 16 + CR)
            expert_loads("expert", 0, 0, range(6, 12))
            for i in range(TILES):
                sp.wait_ge(s_xn2, i + 1)
                sp.dma_start(xn2_dram[i * P:(i + 1) * P, :], xn2[:, i, :]).then_inc(s_xn2_out[i], 16)
            expert_loads("expert", 0, 1, (14,))
            sp.wait_ge(s_sq2, TILES)
            expert_loads("expert", 0, 1, (15,))
            sp.wait_ge(s_logit, TILES)
            expert_loads("expert", 0, 1, (12, 13))
            sp.wait_ge(s_xt2, TILES)
            for i in range(TILES):
                sp.wait_ge(s_xn2_out[i], 16)
                expert_loads("expert", 0, 1, (16 + i,))
            sp.wait_ge(s_table, 1)
            sp.wait_ge(gath, 16)
            expert_loads("expert", 0, 1, (20, 21))
            sp.wait_ge(s_weights, 1)
            expert_loads("expert", 0, 1, (22, 23))
            with sp.Fori(1, E // 2) as it:
                expert_loads("expert", it, it * 2, range(12))
                expert_loads("expert", it, it * 2 + 1, range(12, 24))
            sp.wait_ge(s_regs, 1)
            count = sp.value_load(regs[0:1, 0:1], min_val=0, max_val=OVER)
            first = sp.value_load(regs[0:1, 1:2], min_val=0, max_val=E - 1)
            expert_loads("over", 0, first, range(AHEAD))
            with sp.Fori(0, OVER) as b:
                with sp.If(b < count):
                    e = sp.value_load(regs[0:1, ds(b + 1, 1)], min_val=0, max_val=E - 1)
                    expert_loads("over", b, e, range(AHEAD, 12))
                    following = sp.value_load(regs[0:1, ds(b + 2, 1)], min_val=0, max_val=E - 1)
                    expert_loads("over", b, following, range(12, 12 + AHEAD))
            for i in range(TILES):
                if i < TILES - 2:
                    sp.wait_ge(s_fin, i + 1)
                else:
                    sp.wait_ge(s_fin_last, i - (TILES - 2) + 1)
                sp.dma_start(out[0, i * P:(i + 1) * P, :], h[:, i, :]).then_inc(s_out, 16)
            sp.wait_ge(s_out, 16 * TILES)

        @block.gpsimd
        def _(pool):
            for s in (u_done, prob_done):
                pool.sem_inc(s, CR)
            n = [0]

            def link(ins):
                n[0] += 1
                ins.then_inc(pchain, 1)
                pool.wait_ge(pchain, n[0])

            pool.dma_start(g_mix[:, :], norm_mix[0].partition_broadcast(P)).then_inc(s_gmix, 16)
            pool.memset(eps[:, :], EPS).then_inc(s_const, 1)
            link(pool.memset(ident[:, :], 0.0))
            pool.affine_select(out=ident[:, :], in_=ident[:, :], compare_op=ALU.not_equal, fill=1.0, base=0,
                               pattern=[[-1, P]], channel_multiplier=1).then_inc(s_const, 1)
            for row, src in ((0, conv_w[0]), (TAPS, conv_b), (TAPS + 1, conv_ln_g), (TAPS + 2, conv_ln_b)):
                pool.dma_start(pack[row:row + (TAPS if row == 0 else 1), :], src).then_inc(s_pack, 16)
            pool.wait_ge(s_const, 2)
            pool.tensor_copy(ident_bf[:, :], ident[:, :])
            link(pool.memset(mask_bf[:, :], 0.0))
            pool.affine_select(out=mask_bf[:, :], in_=mask_bf[:, :], compare_op=ALU.is_gt, fill=MASKED, base=0,
                               pattern=[[-1, P]], channel_multiplier=1)
            link(pool.memset(before_bf[:, :], 0.0))
            pool.affine_select(out=before_bf[:, :], in_=before_bf[:, :], compare_op=ALU.is_ge, fill=1.0, base=0,
                               pattern=[[-1, P]], channel_multiplier=1)
            pool.memset(ones_bf[:, :], 1.0)
            pool.memset(mean_w[:, :], 1.0 / CONV)
            pool.memset(ones_row[:, :], 1.0)
            pool.memset(stay[:, :, L:L + 1], 1.0)
            link(pool.memset(u_pad[:, 0:HIST], 0.0))
            pool.sem_inc(s_const, 1)
            pool.dma_start(router_w[:, :, 0:GROUPS], w_router_group[0].rearrange("(p k) n -> p k n", k=KB))\
                .then_inc(s_router, 16)
            pool.dma_start(router_w[:, :, GROUPS:], w_router_expert[0].rearrange("(p k) n -> p k n", k=KB))\
                .then_inc(s_router, 16)
            pool.dma_start(bias_rt[:, 0:GROUPS], b_router_group[0].partition_broadcast(P)).then_inc(s_router, 16)
            pool.dma_start(bias_rt[:, GROUPS:], b_router_expert[0].partition_broadcast(P)).then_inc(s_router, 16)

            with pool.Fori(0, PAIRS) as c:
                pool.wait_ge(ev, c * 5 + 4 + CR)
                pool.wait_ge(conv_done, c + CR)
                pool.tensor_tensor(u_pad[:, HIST:], a_sb[:, :], b_sb[:, :], ALU.mult).then_inc(u_done, 1)
                for u in range(8):
                    off = (u % 4) * P
                    pool.wait_ge(scan_done, c * 8 + u + 1)
                    pool.tensor_tensor(sig[:, u % 3, off:], sig[:, u % 3, off:], after[:, u % 3, off:], ALU.mult)\
                        .then_inc(prob_done, 1)

            taken(pool, "out", 3, 0)
            for k in range(4):
                pool.memset(rt["desc"][:, k:k + 1], 4.0 - k)
            pool.memset(rt["onesE"][:, :], 1.0)

            def number(name, pattern, base=0, per_partition=0):
                return pool.iota(rt[name][:, :], pattern=pattern, base=base, channel_multiplier=per_partition,
                                 allow_small_or_imprecise_dtypes=True)

            number("eidx", [[1, E]])
            number("steps", [[P, TILES - 1]], base=P)
            number("rest", [[-1, E]], base=E - 1)
            number("bidx", [[1, OVER + 1]])
            number("number", [[1, P]])
            number("token", [[0, TOP], [P, TILES]], per_partition=1).then_inc(s_need, 1)
            pool.dma_start(g_ffn[:, :], norm_ffn[0].partition_broadcast(P)).then_inc(s_gffn, 16)
            link(pool.memset(zero_row[:, :], 0.0))
            for b in range(E, BLOCKS):
                pool.dma_start(y_dram[b * P:(b + 1) * P, :].rearrange("p (r c) -> p r c", r=4),
                               zero_row[:, :].unsqueeze(1).to_broadcast([P, 4, D // 4]))\
                    .then_inc(s_yzero if b < BLOCKS - 1 else ystore, 16)
            taken(pool, "last", 5, 0)
            pool.dma_start(g_fin[:, :], norm_final.partition_broadcast(P)).then_inc(s_gfin, 16)
            pool.wait_ge(s_yzero, 16 * (OVER - 1))
            pool.wait_ge(ystore, 16)
            for i in range(TILES):
                pool.wait_ge(s_xn2_out[i], 16)
            pool.wait_ge(s_slot, 1)

            def gather(b, nth):
                if not isinstance(nth, int) or nth:
                    pool.wait_ge(gath, nth * 16)
                pool.tensor_copy(index_1[:, :], index_sb[:, ds(b, 1)]).then_inc(idx1, 1)
                pool.wait_ge(idx1, nth + 1)
                pool.sem_inc(passed, 1)
                pool.indirect_dma_start(out=xe[:, :], out_offset=None, in_=xn2_dram,
                                        in_offset=bass.IndirectOffsetOnAxis(ap=index_1[:, 0:1], axis=0))\
                    .then_inc(gath, 16)

            def expert_pool(b):
                pool.wait_ge(tx, b * 2 + 4)
                gather(b + 2, b + 2)
                pool.wait_ge(ystore, b * 16 + 16)
                pool.sem_inc(y_free, 1)
                pool.wait_ge(yev, b + 1 + CR)
                pool.dma_start(y_dram[ds(b * P, P), :], y_sb[:, :]).then_inc(ystore, 16)

            gather(0, 0)
            pool.wait_ge(tx, 2)
            gather(1, 1)
            with pool.Fori(0, E) as b:
                expert_pool(b)
            pool.wait_ge(s_regs, 1)
            count = pool.value_load(regs[0:1, 0:1], min_val=0, max_val=OVER)
            with pool.Fori(0, OVER) as b:
                with pool.If(b < count):
                    expert_pool(b + E)
            pool.wait_ge(s_rows, 1)
            pool.wait_ge(ystore, count * 16 + 16 * (E + 1))
            pool.sem_inc(passed, 1)
            for i in range(TILES):
                for k in range(TOP):
                    if k and i >= 2:
                        pool.wait_ge(sum2, i - 1)
                    pool.indirect_dma_start(
                        out=picked(k, i), out_offset=None, in_=y_dram,
                        in_offset=bass.IndirectOffsetOnAxis(ap=slot_y[:, k, i:i + 1], axis=0))\
                        .then_inc(pick_sem[k][i], 16)
            pool.wait_ge(s_gfin, 16)
            for i in range(TILES - 2):
                pool.wait_ge(s_r3, i + 1)
                pool.tensor_tensor(h[:, i, :], h[:, i, :], g_fin[:, :], ALU.mult).then_inc(s_fin, 1)

        @block.scalar
        def _(act):
            for s in (ev, v_ev, sig_done, tev, mev, g_ev, silu, yev):
                act.sem_inc(s, CR)

            act.wait_ge(s_const, 1)
            act.activation(table[:, :], eps[:, :], ACT.Sqrt)
            scratch = square[:, 0:2, :].rearrange("p a n -> p (a n)")

            def first_norm(i):
                n, src = (P, h[:, i, :]) if i < TILES else (META, x_meta[:, :])
                act.wait_ge(s_x[i], 16)
                if i:
                    act.wait_ge(s_sq, i)
                act.activation(scratch[0:n], src, ACT.Square, accum_out=sumsq[0:n, i:i + 1]).then_inc(s_sq, 1)
                act.wait_ge(s_sq, i + 1)
                act.activation(std[0:n, i:i + 1], sumsq[0:n, i:i + 1], ACT.Sqrt, bias=eps[0:n, :], scale=1.0 / D)\
                   .then_inc(s_std, 1)

            first_norm(0)
            first_norm(1)
            for i in range(TILES + 1):
                act.wait_ge(s_xt, i + 1)
                if i < TILES:
                    src = ps[:, 2 * i:2 * i + 2, :].rearrange("p b (k n) -> p (b k) n", n=P)
                    dst = xnT_hi[:, :, META + i * P:META + (i + 1) * P]
                else:
                    src = ps[:, 0, 0:KB * META].rearrange("p (k n) -> p k n", n=META)
                    dst = xnT_hi[:, :, 0:META]
                act.copy(dst, src).then_inc(s_xhi, 1)
                if i + 2 < TILES + 1:
                    first_norm(i + 2)
            split_hi(act, "pair", 0, 0)
            act.wait_ge(s_cwt, 1)
            act.copy(cw[:, :, :], ps[:, 2, 0:PAIRS * (TAPS + 3)].rearrange("p (c n) -> p c n", c=PAIRS)).then_inc(s_cw, 1)
            for j in range(1, 4):
                split_hi(act, "pair", j, 0)

            two = ps[:, 0:2, 0:HALF]
            pr = ps[:, 3:5, 0:HALF]
            act.activation(table[:, :], eps[:, :], ACT.Sigmoid)
            with act.Fori(0, PAIRS) as c:
                def halves(t):
                    return t[:, :].rearrange("p (b n) -> p b n", b=2)

                def out_of_psum(nth, dst, src, func=None, last=True):
                    ins = act.activation(dst, src, func) if func else act.copy(dst, src)
                    if last:
                        ins.then_inc(ev, 1)

                taken(act, "pair", 0, c)
                act.wait_ge(u_done, c + CR)
                out_of_psum(1, halves(a_sb), pr)
                taken(act, "pair", 1, c)
                out_of_psum(2, halves(kT), two)
                split_hi(act, "pair", 4, c)
                taken(act, "pair", 2, c)
                out_of_psum(3, qT[:, :], ps[:, 2, :])
                split_hi(act, "pair", 5, c)
                taken(act, "pair", 3, c)
                out_of_psum(4, halves(b_sb), pr, ACT.Sigmoid)

                def sigmoids(u):
                    i, ub = 3 - u % 4, u % 3
                    off = L - META - (i + 1) * P
                    act.wait_ge(z_done, c * 8 + u + 1)
                    act.wait_ge(t_done, c * 8 + last_user(u) + CR)
                    if i == 3:
                        src, view = two, lambda t: t[:, ub, off:L].rearrange("p (b n) -> p b n", b=2)
                    else:
                        src, view = ps[:, 2 * (u % 2), 0:L - off], lambda t: t[:, ub, off:L]
                    act.activation(view(sig), src, ACT.Sigmoid, scale=SCALE)
                    act.activation(view(stay), src, ACT.Sigmoid, scale=-SCALE).then_inc(sig_done, 1)

                def copy_weights(u):
                    i = 3 - u % 4
                    act.wait_ge(t_done, c * 8 + u + 1 + CR)
                    act.wait_ge(av_done, c * 2 + u // 4 + CR)
                    act.copy(probT[:, 0:i + 1, i * P:(i + 1) * P],
                                   ps[:, turn_bank[u % 2], 0:(i + 1) * P].rearrange("p (j n) -> p j n", n=P))\
                       .then_inc(tev, 1)
                    if i == 0:
                        act.copy(probT_meta[:, :], ps[0:META, 6, :]).then_inc(mev, 1)

                sigmoids(0)
                sigmoids(1)
                taken(act, "pair", 4, c)
                out_of_psum(5, halves(vT), pr)
                for u in range(8):
                    copy_weights(u)
                    if u + 2 < 8:
                        sigmoids(u + 2)
                    if u == 0:
                        act.wait_ge(vt_done, c + 1)
                        act.copy(v_sb[:, :, :], ps[:, 7, :].rearrange("p (j n) -> p j n", n=P))
                        act.copy(v_meta[:, :], ps[0:META, 3, 0:P]).then_inc(v_ev, 1)
                    if 5 <= u:
                        split_hi(act, "pair", u + 1, c)
                act.wait_ge(av_done, c * 2 + 2 + CR)
                act.copy(attT_hi[:, ds(c, 1), :].rearrange("p a n -> p (a n)"), ps[:, 7, :])\
                   .then_inc(av_hi, 1)

            def gates(m, m2, name, j, it, which=range(2)):
                for k in which:
                    dst = (sgate, cgate)[k]
                    taken(act, name, j + k, it)
                    if not isinstance(m, int) or m >= 2:
                        act.wait_ge(br_ev, m * 2 - 2 + CR)
                    act.activation(dst[:, m2, :], ps[:, gate_bank[m2][k], :], ACT.Sigmoid).then_inc(g_ev, 1)

            taken(act, "gate", 0, 0)
            act.activation(sgate[:, 0, 0:HALF - META], ps[:, 3, META:HALF], ACT.Sigmoid)
            act.activation(sgate[:, 0, HALF - META:], ps[:, 4, 0:HALF], ACT.Sigmoid).then_inc(g_ev, 1)
            gates(0, 0, "gate", 0, 0, [1])
            split_hi(act, "gate", 4, 0)
            split_hi(act, "gate", 5, 0)
            gates(1, 1, "gate", 2, 0)
            for m in range(PAIRS):
                act.wait_ge(ln_xc, m + 1)
                act.activation(sq_ln[:, m, :], y[:, m, :], ACT.Square).then_inc(ln_sq, 1)
            split_hi(act, "mix", 0, 0)
            act.wait_ge(ln_var, 1)
            act.activation(rstd_ln[:, :], ps[:, 6, :], ACT.Sqrt, bias=eps[:, :]).then_inc(ln_std, 1)
            act.activation(table[:, :], eps[:, :], ACT.Silu)
            split_hi(act, "mix", 1, 0)
            for m in range(PAIRS):
                act.wait_ge(ln_n, m + 1)
                if m >= 2:
                    act.wait_ge(ln_lo, m - 1)
                act.activation(silu_y[:, m % 2, :], y[:, m, :], ACT.Silu, scale=cw[:, m, TAPS + 1:TAPS + 2],
                               bias=cw[:, m, TAPS + 2:TAPS + 3]).then_inc(ln_act, 1)
                act.wait_ge(ln_act, m + 1)
                act.copy(yT_hi[:, m, :], silu_y[:, m % 2, :]).then_inc(ln_hi, 1)
            split_hi(act, "mix", 2, 0)

            def merge_hi(m):
                act.wait_ge(br_ev, m * 2 + 2 + CR)
                act.copy(mT_hi[:, ds(m, 1), :].rearrange("p a n -> p (a n)"), merged[:, :])\
                   .then_inc(m_hi, 1)

            act.activation(table[:, :], eps[:, :], ACT.Sigmoid)
            with act.Fori(0, 2) as it:
                for k in range(2):
                    split_hi(act, "mix", 3 * k + 3, it)
                    merge_hi(it * 2 + k)
                    gates(it * 2 + (k + 2), k, "mix", 3 * k - 2, it)
                    split_hi(act, "mix", 3 * k + 4, it)
                    split_hi(act, "mix", 3 * k + 5, it)
            split_hi(act, "last", 3, 0)
            merge_hi(4)
            gates(6, 0, "last", -2, 0)
            split_hi(act, "last", 4, 0)
            split_hi(act, "last", 5, 0)
            split_hi(act, "out", 0, 0)
            merge_hi(5)
            gates(7, 1, "last", 1, 0)
            split_hi(act, "out", 1, 0)
            merge_hi(6)
            split_hi(act, "out", 2, 0)
            merge_hi(7)
            for j in range(3, 8):
                split_hi(act, "out", j, 0)
            act.wait_ge(m_lo, KB)
            for j in range(3):
                split_hi(act, "expert", j, 0)
            act.activation(table[:, :], eps[:, :], ACT.Sqrt)

            def norm2(i):
                act.wait_ge(res, TILES + i + 1)
                if i:
                    act.wait_ge(s_sq2, i)
                act.activation(square2[:, :], h[:, i, :], ACT.Square, accum_out=sumsq[:, 8 + i:9 + i])\
                   .then_inc(s_sq2, 1)
                act.wait_ge(s_sq2, i + 1)
                act.activation(std[:, 8 + i:9 + i], sumsq[:, 8 + i:9 + i], ACT.Sqrt, bias=eps[:, :],
                               scale=1.0 / D).then_inc(s_std2, 1)

            norm2(0)
            norm2(1)
            for i in range(TILES):
                act.wait_ge(s_xt2, i + 1)
                if i >= 2:
                    act.wait_ge(s_logit, i - 1)
                act.copy(xn2T[:, i % 2, :, :], ps[:, 2 * (i % 2):2 * (i % 2) + 2, :]
                         .rearrange("p b (k n) -> p (b k) n", n=P)).then_inc(s_xe2, 1)
                if i + 2 < TILES:
                    norm2(i + 2)
                else:
                    split_hi(act, "expert", i + 1, 0)
            act.activation(table[:, :], eps[:, :], ACT.Exp)
            act.wait_ge(s_logit, TILES)
            act.copy(logitT[:, :], ps[0:GROUPS + E, 4, :]).then_inc(s_lcopy, 1)
            act.wait_ge(s_gexp, 1)
            act.activation(rt["gtmp"][:, :], rt["gtmp"][:, :], ACT.Exp).then_inc(s_hot, 1)
            act.wait_ge(s_gexp, 2)
            act.activation(rt["ex"][:, :], rt["el"][:, :], ACT.Exp).then_inc(s_hot, 1)

            def inputs_hi(b, half):
                act.wait_ge(tx, b * 2 + half + 1)
                act.copy(xeT_hi[:, 4 * half:4 * half + 4, :], ps[:, half, :].rearrange("p (k n) -> p k n", n=P)).then_inc(xe_hi, 1)

            def hidden_hi(b, half):
                act.wait_ge(ht, b * 2 + half + 1)
                act.copy(hT_hi[:, 2 * half:2 * half + 2, :], ht_bank[half].rearrange("p (f n) -> p f n", n=P))\
                   .then_inc(ht_hi, 1)

            def expert_act(name, it, b, o=0):
                for j in (5, 6):
                    split_hi(act, name, o + j, it)
                taken(act, name, o + 3, it)
                act.wait_ge(hdn_done, b * 2 + CR)
                act.activation(silu_g[:, :], ps[:, 2, :], ACT.Silu).then_inc(silu, 1)
                for j in range(7, 12):
                    split_hi(act, name, o + j, it)
                hidden_hi(b, 0)
                inputs_hi(b + 1, 0)
                hidden_hi(b, 1)
                inputs_hi(b + 1, 1)
                for j in range(12, 12 + AHEAD):
                    split_hi(act, name, o + j, it)
                taken(act, name, o + 11, it)
                act.wait_ge(y_free, b + 1)
                act.copy(y_sb[:, :], ps[:, 5:7, :].rearrange("p b n -> p (b n)")).then_inc(yev, 1)

            inputs_hi(0, 0)
            inputs_hi(0, 1)
            act.activation(table[:, :], eps[:, :], ACT.Silu)
            with act.Fori(0, E // 2) as it:
                for k in range(2):
                    expert_act("expert", it, it * 2 + k, 12 * k)
            act.wait_ge(s_regs, 1)
            count = act.value_load(regs[0:1, 0:1], min_val=0, max_val=OVER)
            with act.Fori(0, OVER) as b:
                with act.If(b < count):
                    expert_act("over", b, b + E)
            act.activation(table[:, :], eps[:, :], ACT.Sqrt)
            for i in range(TILES):
                act.wait_ge(sum2, i + 1)
                act.activation(square2[:, :], h[:, i, :], ACT.Square, accum_out=sumsq[:, 12 + i:13 + i])\
                   .then_inc(s_sq3, 1)
                act.wait_ge(s_sq3, i + 1)
                act.activation(std[:, 12 + i:13 + i], sumsq[:, 12 + i:13 + i], ACT.Sqrt, bias=eps[:, :],
                               scale=1.0 / D).then_inc(s_std3, 1)
                if i < TILES - 2:
                    act.wait_ge(s_recip3, i + 1)
                    act.activation(h[:, i, :], h[:, i, :], ACT.Copy, scale=rstd[:, 12 + i:13 + i]).then_inc(s_r3, 1)

        @block.vector
        def _(dve):
            for s in (lo_done, conv_done, av_lo, br_ev, xe_lo, hdn_done):
                dve.sem_inc(s, CR)

            class Chain:
                done, start, run, per = 0, 0, None, 0

                def loop(self, run, per):
                    self.start, self.run, self.per, self.done = self.start + self.done, run, per, 0

                def end(self, runs):
                    assert self.done == self.per, self.done
                    self.start, self.run, self.done = self.start + runs * self.per, None, 0

                def free(self, ins):
                    self.done += 1
                    ins.then_inc(dchain, 1)

                def link(self, ins):
                    self.done += 1
                    ins.then_inc(dchain, 1)
                    at = self.start + self.done
                    dve.wait_ge(dchain, at if self.run is None else self.run * self.per + at)

            chain = Chain()
            link, free = chain.link, chain.free

            for i in range(TILES + 1):
                n, src = (P, h[:, i, :]) if i < TILES else (META, x_meta[:, :])
                dve.wait_ge(s_std, i + 1)
                link(dve.reciprocal(rstd[0:n, i:i + 1], std[0:n, i:i + 1]))
                if i == 0:
                    dve.wait_ge(s_gmix, 16)
                if i >= 2:
                    dve.wait_ge(s_xt, i - 1)
                dve.scalar_tensor_tensor(out=xn[0:n, i % 2, :], in0=src, scalar=rstd[0:n, i:i + 1],
                                         in1=g_mix[0:n, :], op0=ALU.mult, op1=ALU.mult).then_inc(s_xn, 1)
                if i >= 1:
                    first_lo(dve, i - 1)
            first_lo(dve, TILES)
            split_lo(dve, "pair", 0, 0)
            dve.wait_ge(s_cw, 1)
            for j in range(1, 4):
                split_lo(dve, "pair", j, 0)
            dve.wait_ge(s_const, 3)

            with dve.Fori(0, PAIRS) as c:
                chain.loop(c, TAPS)
                tap = [0]

                def taps(n):
                    for _ in range(n):
                        k = tap[0]
                        if k == TAPS:
                            return
                        tap[0] += 1
                        win = u_pad[:, META + k:META + k + SEQ]
                        if k == 0:
                            dve.wait_ge(u_done, c + 1 + CR)
                            link(dve.tensor_copy(cw_c[:, :], cw[:, ds(c, 1), :].rearrange("p a n -> p (a n)")))
                            link(dve.tensor_scalar(y_acc[:, :], win, cw_c[:, 0:1], cw_c[:, TAPS:TAPS + 1],
                                                   ALU.mult, ALU.add))
                        elif k < TAPS - 1:
                            link(dve.scalar_tensor_tensor(out=y_acc[:, :], in0=win, scalar=cw_c[:, k:k + 1],
                                                          in1=y_acc[:, :], op0=ALU.mult, op1=ALU.add))
                        else:
                            ins = dve.scalar_tensor_tensor(
                                out=y[:, ds(c, 1), :].rearrange("p a n -> p (a n)"), in0=win,
                                scalar=cw_c[:, k:k + 1], in1=y_acc[:, :], op0=ALU.mult, op1=ALU.add)
                            ins.then_inc(conv_done, 1)

                def scan(u):
                    ub, off = u % 3, (u % 4) * P
                    dve.wait_ge(sig_done, c * 8 + u + 1 + CR)
                    dve.wait_ge(prob_done, c * 8 + last_user(u) + CR)
                    dve.tensor_tensor_scan(after[:, ub, off:L][:, ::-1], stay[:, ub, off + 1:L + 1][:, ::-1],
                                           ones_row[:, off:L], 1.0, ALU.mult, ALU.mult).then_inc(scan_done, 1)

                split_lo(dve, "pair", 4, c)
                split_lo(dve, "pair", 5, c)
                for u in range(8):
                    scan(u)
                    if u == 1:
                        taps(6)
                    elif 1 < u < 7:
                        taps(2 - u % 2)
                split_lo(dve, "pair", 6, c)
                dve.wait_ge(av_hi, c + 1)
                dve.tensor_tensor(attT_lo[:, ds(c, 1), :].rearrange("p a n -> p (a n)"), ps[:, 7, :],
                                  attT_hi[:, ds(c, 1), :].rearrange("p a n -> p (a n)").bitcast(F32), ALU.subtract)\
                   .then_inc(av_lo, 1)
                split_lo(dve, "pair", 7, c)
                split_lo(dve, "pair", 8, c)
                taps(TAPS)
                chain.end(PAIRS)
            split_lo(dve, "gate", 4, 0)
            dve.wait_ge(ln_mean, 1)
            for m in range(PAIRS):
                dve.tensor_tensor(y[:, m, :], y[:, m, :], ps[:, 5, :], ALU.subtract).then_inc(ln_xc, 1)
            split_lo(dve, "gate", 5, 0)
            split_lo(dve, "mix", 0, 0)
            dve.wait_ge(ln_std, 1)
            dve.reciprocal(rstd_ln[:, :], rstd_ln[:, :]).then_inc(ln_rstd, 1)
            dve.wait_ge(ln_rstd, 1)
            for m in range(PAIRS):
                dve.tensor_tensor(y[:, m, :], y[:, m, :], rstd_ln[:, :], ALU.mult).then_inc(ln_n, 1)
            split_lo(dve, "mix", 1, 0)
            for m in range(PAIRS):
                dve.wait_ge(ln_hi, m + 1)
                dve.tensor_tensor(yT_lo[:, m, :], silu_y[:, m % 2, :], yT_hi[:, m, :].bitcast(F32), ALU.subtract)\
                   .then_inc(ln_lo, 1)
            split_lo(dve, "mix", 2, 0)

            def merge(m, m2, name, j, it):
                dve.wait_ge(g_ev, m * 2 + 2 + CR)
                dve.wait_ge(br_done, m + 1)
                dve.tensor_tensor(sgate[:, m2, :], sgate[:, m2, :], ps[:, branch_bank[m2][0], :], ALU.mult).then_inc(br_ev, 1)
                taken(dve, name, j, it)
                dve.wait_ge(br_ev, m * 2 + 1 + CR)
                dve.tensor_tensor(cgate[:, m2, :], cgate[:, m2, :], ps[:, branch_bank[m2][1], :], ALU.mult).then_inc(br_mul, 1)
                dve.wait_ge(br_mul, m + 1)
                dve.tensor_tensor(merged[:, :], sgate[:, m2, :], cgate[:, m2, :], ALU.add).then_inc(br_ev, 1)

            def merge_lo(m):
                dve.wait_ge(m_hi, m + 1)
                dve.tensor_tensor(mT_lo[:, ds(m, 1), :].rearrange("p a n -> p (a n)"), merged[:, :],
                                  mT_hi[:, ds(m, 1), :].rearrange("p a n -> p (a n)").bitcast(F32), ALU.subtract)\
                   .then_inc(m_lo, 1)

            with dve.Fori(0, 2) as it:
                for k in range(2):
                    merge(it * 2 + k, k, "mix", 3 * k, it)
                    split_lo(dve, "mix", 3 * k + 3, it)
                    merge_lo(it * 2 + k)
                    split_lo(dve, "mix", 3 * k + 4, it)
                    split_lo(dve, "mix", 3 * k + 5, it)
            merge(4, 0, "last", 0, 0)
            split_lo(dve, "last", 3, 0)
            merge_lo(4)
            split_lo(dve, "last", 4, 0)
            split_lo(dve, "last", 5, 0)
            split_lo(dve, "out", 0, 0)
            merge(5, 1, "last", 3, 0)
            merge_lo(5)
            split_lo(dve, "out", 1, 0)
            merge(6, 0, "last", 4, 0)
            merge_lo(6)
            split_lo(dve, "out", 2, 0)
            merge(7, 1, "last", 5, 0)
            merge_lo(7)

            def residual(half, tiles):
                for i in tiles:
                    if i < TILES - 1:
                        dve.wait_ge(out_done, (TILES - 1) * half + i + 1)
                    else:
                        taken(dve, "out", 4 * half + 3, 0)
                    part = h[:, i, 512 * half:512 * half + 512]
                    dve.tensor_tensor(part, part, ps[:, out_bank[4 * half + i], :], ALU.add).then_inc(res, 1)

            for j in range(3, 7):
                split_lo(dve, "out", j, 0)
            residual(0, range(TILES))
            split_lo(dve, "out", 7, 0)
            for j in range(3):
                split_lo(dve, "expert", j, 0)

            def norm2(i):
                dve.wait_ge(s_std2, i + 1)
                link(dve.reciprocal(rstd[:, 8 + i:9 + i], std[:, 8 + i:9 + i]))
                if i == 0:
                    dve.wait_ge(s_gffn, 16)
                dve.scalar_tensor_tensor(out=xn2[:, i, :], in0=h[:, i, :], scalar=rstd[:, 8 + i:9 + i],
                                         in1=g_ffn[:, :], op0=ALU.mult, op1=ALU.mult).then_inc(s_xn2, 1)

            residual(1, range(2))
            for i in range(TILES):
                norm2(i)
                if i + 2 < TILES:
                    residual(1, range(i + 2, i + 3))
            for j in range(3, AHEAD):
                split_lo(dve, "expert", j, 0)

            T = TILES

            def v2(name):
                return rt[name][:, :].rearrange("p (t n) -> p t n", t=T)

            def v3(name):
                return rt[name][:, :].rearrange("p (t g n) -> p t g n", t=T, g=GROUPS)

            def over(name, n):
                return rt[name][:, :].unsqueeze(2).to_broadcast([P, T, n])

            def row(name, n):
                return rt[name][:, :].unsqueeze(1).to_broadcast([P, T, n])

            def tt(o, a, b, op):
                link(dve.tensor_tensor(o, a, b, op))

            def reduce(o, a, op=ALU.add):
                link(dve.tensor_reduce(o, a, AX.X, op))

            def first_best(src, hot, best):
                reduce(rt[best][:, :], src, ALU.max)
                tt(v2("cand"), src, over(best, 4), ALU.is_equal)
                tt(v2("cand"), v2("cand"), row("desc", 4), ALU.mult)
                reduce(rt["best"][:, :], v2("cand"), ALU.max)
                tt(v2(hot), v2("cand"), over("best", 4), ALU.is_equal)

            dve.wait_ge(s_lturn, 1)
            dve.wait_ge(s_router, 16 * 4)
            dve.wait_ge(s_need, 1)
            link(dve.tensor_tensor(v2("logit"), ps[:, 7, 0:T * 20].rearrange("p (t n) -> p t n", t=T),
                                   bias_rt[:, :].unsqueeze(1).to_broadcast([P, T, 20]), ALU.add))
            first_best(v2("logit")[:, :, 0:4], "ohg", "gmax")
            free(dve.tensor_tensor(v2("gtmp"), v2("logit")[:, :, 0:4], over("gmax", 4), ALU.subtract))
            tt(v3("sel"), v2("logit")[:, :, 4:20].rearrange("p t (g n) -> p t g n", g=4),
               v2("ohg").unsqueeze(3).to_broadcast([P, T, 4, 4]), ALU.mult)
            dve.sem_inc(s_gexp, 1)
            reduce(v2("el"), v3("sel").rearrange("p t g n -> p t n g"))
            reduce(rt["best"][:, :], v2("el"), ALU.max)
            tt(v2("el"), v2("el"), over("best", 4), ALU.subtract)
            dve.sem_inc(s_gexp, 1)
            dve.wait_ge(s_hot, 2)
            first_best(v2("ex"), "oh1", "p1")
            link(dve.scalar_tensor_tensor(out=rt["ex"][:, :], in0=rt["oh1"][:, :], scalar=-4.0, in1=rt["ex"][:, :],
                                          op0=ALU.mult, op1=ALU.add))
            first_best(v2("ex"), "oh2", "p2")
            H12 = rt["H12"][:, :].rearrange("p (k t n) -> p k t n", k=TOP, t=T)
            for k, hot in enumerate(("oh1", "oh2")):
                (free, link)[k](dve.tensor_tensor(
                    H12[:, k].rearrange("p t (g n) -> p t g n", g=GROUPS), v2("ohg").unsqueeze(3).to_broadcast([P, T, 4, 4]),
                    v2(hot).unsqueeze(2).to_broadcast([P, T, 4, 4]), ALU.mult))
            tt(H_bf[:, :, :], H12[:, 0], H12[:, 1], ALU.add)
            dve.sem_inc(s_hotx, 1)
            reduce(rt["gsum"][:, :], v2("gtmp"))
            free(dve.reciprocal(rt["gsum"][:, :], rt["gsum"][:, :]))
            tt(rt["psum12"][:, :], rt["p1"][:, :], rt["p2"][:, :], ALU.add)
            dve.wait_ge(s_rank, 1)
            S = T - 1
            rank = ps[:, 6, 0:T * E]
            over3 = rt["over3"][:, :].rearrange("p (n s) -> p n s", s=S)
            ge3 = rt["ge3"][:, :].rearrange("p (m s) -> p m s", s=S)
            free(dve.tensor_tensor(over3, ps[:, 6, T * E:T * E + E].unsqueeze(2).to_broadcast([P, E, S]),
                                   rt["steps"][:, :].unsqueeze(1).to_broadcast([P, E, S]), ALU.is_gt))
            tt(ge3, rank.unsqueeze(2).to_broadcast([P, T * E, S]),
               rt["steps"][:, :].unsqueeze(1).to_broadcast([P, T * E, S]), ALU.is_ge)
            free(dve.tensor_reduce(rt["ovn"][:, :], over3, AX.X, ALU.add))
            reduce(rt["fb"][:, :], ge3)
            free(dve.tensor_tensor_scan(rt["cum"][:, :], rt["onesE"][:, :], rt["ovn"][:, :], 0.0, ALU.mult, ALU.add))
            free(dve.tensor_tensor(rt["t3"][:, :], rt["rest"][:, :], rt["ovn"][:, :], ALU.subtract))
            link(dve.scalar_tensor_tensor(out=rt["place_of"][:, :], in0=rt["fb"][:, :], scalar=-float(P), in1=rank,
                                          op0=ALU.mult, op1=ALU.add))
            free(dve.tensor_tensor(v2("t2"), v2("fb"), row("eidx", E), ALU.add))
            tt(rt["t3"][:, :], rt["cum"][:, :], rt["t3"][:, :], ALU.add)
            tt(v2("t1"), ge3[:, :, 0].rearrange("p (t n) -> p t n", t=T), row("t3", E), ALU.mult)
            tt(rt["t1"][:, :], rt["t1"][:, :], rt["t2"][:, :], ALU.add)
            sel = {}
            for src in ("t1", "place_of"):
                sel[src] = rt["sel_" + src][:, :].rearrange("p (k t n) -> p k t n", k=TOP, t=T)
                (free if src == "t1" else link)(dve.tensor_tensor(
                    sel[src], H12, v2(src).unsqueeze(1).to_broadcast([P, TOP, T, E]), ALU.mult))
            free(dve.tensor_reduce(rt["block"][:, :], rt["sel_t1"][:, :].rearrange("p (m n) -> p m n", n=E), AX.X, ALU.add))
            reduce(rt["place"][:, :], rt["sel_place_of"][:, :].rearrange("p (m n) -> p m n", n=E))
            M = TOP * T
            hot = rt["hot"][:, :].rearrange("p (m n) -> p m n", n=ICOLS)
            free(dve.tensor_tensor(hot, rt["number"][:, 0:ICOLS].unsqueeze(1).to_broadcast([P, M, ICOLS]),
                                   rt["block"][:, :].unsqueeze(2).to_broadcast([P, M, ICOLS]), ALU.is_equal))
            tt(place_hot[:, :, :], rt["number"][:, :].unsqueeze(1).to_broadcast([P, M, P]),
               rt["place"][:, :].unsqueeze(2).to_broadcast([P, M, P]), ALU.is_equal)
            dve.tensor_tensor(block_hot[:, :, :], hot, rt["token"][:, :].unsqueeze(2).to_broadcast([P, M, ICOLS]),
                              ALU.mult).then_inc(s_place, 1)
            bex = rt["bex"][:, :].rearrange("p (b n) -> p b n", n=E)
            tt(bex, rt["cum"][:, :].unsqueeze(1).to_broadcast([P, OVER + 1, E]),
               rt["bidx"][:, :].unsqueeze(2).to_broadcast([P, OVER + 1, E]), ALU.is_le)
            dve.wait_ge(s_table, 1)
            dve.tensor_copy(index_sb[:, :], ps[:, 5, 0:ICOLS]).then_inc(s_slot, 1)
            reduce(rt["bexi"][:, :], bex)
            link(dve.tensor_scalar(rt["bexi"][:, :], rt["bexi"][:, :], float(E - 1), None, ALU.min))
            link(dve.tensor_copy(regs[:, 1:], rt["bexi"][:, :]))
            dve.tensor_copy(regs[:, 0:1], rt["cum"][:, E - 1:E]).then_inc(s_regs, 1)
            free(dve.reciprocal(rt["psum12"][:, :], rt["psum12"][:, :]))
            link(dve.scalar_tensor_tensor(out=rt["row"][:, :], in0=rt["block"][:, :], scalar=float(P),
                                          in1=rt["place"][:, :], op0=ALU.mult, op1=ALU.add))
            dve.tensor_copy(slot_y[:, :, :], rt["row"][:, :].rearrange("p (k t) -> p k t", k=TOP)).then_inc(s_rows, 1)
            tt(rt["psum12"][:, :], rt["psum12"][:, :], rt["gsum"][:, :], ALU.mult)
            tt(w_tok[:, 0, :], rt["p1"][:, :], rt["psum12"][:, :], ALU.mult)
            tt(w_tok[:, 1, :], rt["p2"][:, :], rt["psum12"][:, :], ALU.mult)
            dve.sem_inc(s_weights, 1)

            def inputs_lo(b, half):
                dve.wait_ge(xe_hi, b * 2 + half + 1)
                dve.tensor_tensor(xeT_lo[:, 4 * half:4 * half + 4, :],
                                  ps[:, half, :].rearrange("p (k n) -> p k n", n=P),
                                  xeT_hi[:, 4 * half:4 * half + 4, :].bitcast(F32), ALU.subtract).then_inc(xe_lo, 1)

            def hidden_lo(b, half):
                dve.wait_ge(ht_hi, b * 2 + half + 1)
                dve.tensor_tensor(hT_lo[:, 2 * half:2 * half + 2, :], ht_bank[half].rearrange("p (f n) -> p f n", n=P),
                                  hT_hi[:, 2 * half:2 * half + 2, :].bitcast(F32), ALU.subtract).then_inc(ht_lo, 1)

            def expert_dve(name, it, b, o=0):
                for j in range(AHEAD, 10):
                    split_lo(dve, name, o + j, it)
                taken(dve, name, o + 7, it)
                dve.wait_ge(silu, b + 1 + CR)
                for half in range(2):
                    part = slice(half * FF // 2, (half + 1) * FF // 2)
                    dve.tensor_tensor(hdn[:, part], silu_g[:, part], ps[:, 3, part], ALU.mult).then_inc(hdn_done, 1)
                hidden_lo(b, 0)
                split_lo(dve, name, o + 10, it)
                hidden_lo(b, 1)
                split_lo(dve, name, o + 11, it)
                inputs_lo(b + 1, 0)
                inputs_lo(b + 1, 1)
                for j in range(12, 12 + AHEAD):
                    split_lo(dve, name, o + j, it)

            inputs_lo(0, 0)
            inputs_lo(0, 1)
            with dve.Fori(0, E // 2) as it:
                for k in range(2):
                    expert_dve("expert", it, it * 2 + k, 12 * k)
            count = dve.value_load(regs[0:1, 0:1], min_val=0, max_val=OVER)
            with dve.Fori(0, OVER) as b:
                with dve.If(b < count):
                    expert_dve("over", b, b + E)

            def combine(i):
                for k, s in ((0, sum1), (1, sum2)):
                    dve.wait_ge(pick_sem[k][i], 16)
                    dve.scalar_tensor_tensor(out=h[:, i, :], in0=picked(k, i), scalar=w_tok[:, k, i:i + 1],
                                             in1=h[:, i, :], op0=ALU.mult, op1=ALU.add).then_inc(s, 1)
                    dve.wait_ge(s, i + 1)

            def recip(i):
                dve.wait_ge(s_std3, i + 1)
                dve.reciprocal(rstd[:, 12 + i:13 + i], std[:, 12 + i:13 + i]).then_inc(s_recip3, 1)

            combine(0)
            for i in range(1, TILES):
                combine(i)
                recip(i - 1)
            dve.wait_ge(s_gfin, 16)
            for i in range(TILES - 2, TILES):
                if i == TILES - 1:
                    recip(i)
                dve.wait_ge(s_recip3, i + 1)
                dve.scalar_tensor_tensor(out=h[:, i, :], in0=h[:, i, :], scalar=rstd[:, 12 + i:13 + i], in1=g_fin[:, :],
                                         op0=ALU.mult, op1=ALU.mult).then_inc(s_fin_last, 1)

        @block.tensor
        def _(pe):
            for s in (used, t_done, av_done):
                pe.sem_inc(s, CR)
            pe.wait_ge(s_const, 2)

            for i in range(TILES + 1):
                n = P if i < TILES else META
                pe.wait_ge(s_xn, i + 1)
                if i == TILES:
                    pe.wait_ge(s_xlo, 1)
                src = xn[0:n, i % 2, :].rearrange("p (q k) -> p k q", k=KB)
                for k in range(KB):
                    dst = ps[:, 2 * i + k // 4, (k % 4) * P:(k % 4 + 1) * P] if i < TILES else \
                        ps[:, 0, k * META:(k + 1) * META]
                    last = pe.transpose(dst, src[:, k, :], ident[0:n, 0:n])
                last.then_inc(s_xt, 1)
            pe.wait_ge(s_xlo, 2)
            n = TAPS + 3
            pe.wait_ge(s_pack, 16 * 4)
            for c in range(PAIRS):
                last = pe.transpose(ps[:, 2, c * n:(c + 1) * n], pack[0:n, c * P:(c + 1) * P], ident[0:n, 0:n])
            last.then_inc(s_cwt, 1)
            pe.wait_ge(s_xlo, TILES + 1)
            pe.wait_ge(s_cw, 1)
            pe.wait_ge(s_const, 3)

            def channels_by_tokens(name, j, it, outs):
                hi, lo = weights(pe, name, j, it, P)
                for dst, tok in outs:
                    for k in range(KB):
                        last = product(pe, dst, (hi[:, k, :], lo[:, k, :]), (xnT_hi[:, k, tok], xnT_lo[:, k, tok]),
                                       k == 0, k == KB - 1)
                return last

            all_tokens = [slice(0, HALF), slice(HALF, L)]

            def ahead(steps, j, c):
                hi, lo = weights(pe, "pair", j, c, P)
                for step in steps:
                    b, k = step // KB, step % KB
                    last = product(pe, ps[:, 3 + b, 0:HALF], (hi[:, k, :], lo[:, k, :]),
                                   (xnT_hi[:, k, all_tokens[b]], xnT_lo[:, k, all_tokens[b]]), k == 0, k == KB - 1)
                if steps[-1] == 2 * KB - 1:
                    last.then_inc(used, 1)

            ahead(range(2 * KB), 0, 0)
            with pe.Fori(0, PAIRS) as c:
                def project(j, outs, count=None):
                    last = channels_by_tokens("pair", j, c, outs)
                    last.then_inc(used, 1)

                pe.wait_ge(tev, c * 8 + CR)
                pe.wait_ge(sig_done, c * 8 - 1 + CR)
                project(1, [(ps[:, b, 0:HALF], all_tokens[b]) for b in range(2)])
                pe.wait_ge(sig_done, c * 8 + CR)
                project(2, [(ps[:, 2, :], slice(META, L))])
                pe.wait_ge(ev, c * 5 + 1 + CR)
                project(3, [(ps[:, 3 + b, 0:HALF], all_tokens[b]) for b in range(2)])

                def scores(u):
                    hh, i = u // 4, 3 - u % 4
                    if u >= 2:
                        pe.wait_ge(sig_done, c * 8 + u - 1 + CR)
                    if u == 4:
                        pe.wait_ge(tev, c * 8 + 2 + CR)
                    q = qT[hh * DH:(hh + 1) * DH, i * P:(i + 1) * P]
                    n = META + (i + 1) * P
                    for b, (lo, hi) in enumerate([(0, HALF), (HALF, L)] if i == 3 else [(0, n)]):
                        dst = ps[:, 2 * (u % 2) + b, :]
                        pe.matmul(dst[:, 0:hi - lo], q, kT[hh * DH:(hh + 1) * DH, lo:hi], start=True, stop=hi < n)
                    last = pe.matmul(dst[:, hi - lo - P:hi - lo], ident_bf[:, :], mask_bf[:, :], start=False, stop=True)
                    last.then_inc(z_done, 1)

                def turn(u):
                    i, ub, bank = 3 - u % 4, u % 3, turn_bank[u % 2]
                    off = L - META - (i + 1) * P
                    pe.wait_ge(prob_done, c * 8 + u + 1 + CR)
                    if u == 0:
                        pe.wait_ge(mev, c * 2 + CR)
                    pe.wait_ge(tev, c * 8 + u - 1 + CR)
                    if u == 3:
                        pe.wait_ge(sig_done, c * 8 + 5 + CR)
                    if u == 4:
                        pe.wait_ge(mev, c * 2 + 1 + CR)
                    pe.transpose(ps[0:META, 6, i * P:(i + 1) * P], sig[:, ub, off:off + META], ident[:, :])
                    for j in range(i + 1):
                        at_ = off + META + j * P
                        last = pe.transpose(ps[:, bank, j * P:(j + 1) * P], sig[:, ub, at_:at_ + P], ident[:, :])
                    last.then_inc(t_done, 1)

                def values(hh):
                    pe.wait_ge(mev, c * 2 + hh + 1 + CR)
                    pe.wait_ge(tev, c * 8 + 4 * hh + 4 + CR)
                    rows = slice(hh * DH, (hh + 1) * DH)
                    pe.matmul(ps[rows, 7, :], v_meta[:, rows], probT_meta[:, :], start=True, stop=False)
                    for j in range(TILES):
                        last = pe.matmul(ps[rows, 7, j * P:], v_sb[:, j, rows], probT[:, j, j * P:], start=False,
                                         stop=(j == TILES - 1))
                    last.then_inc(av_done, 1)

                pe.wait_ge(ev, c * 5 + 3 + CR)
                scores(0)
                scores(1)
                pe.wait_ge(ev, c * 5 + 4 + CR)
                project(4, [(ps[:, 3 + b, 0:HALF], all_tokens[b]) for b in range(2)])
                fill, step = (0, 0, 2, 4, 2, 3, 3, 2), 0
                for u in range(8):
                    turn(u)
                    if u + 2 < 8:
                        scores(u + 2)
                    if fill[u]:
                        if step == 0:
                            pe.wait_ge(v_ev, c + 1 + CR)
                        ahead(range(step, step + fill[u]), 5, c)
                        step += fill[u]
                    if u == 0:
                        pe.wait_ge(ev, c * 5 + 5 + CR)
                        pe.wait_ge(av_lo, c + CR)
                        pe.transpose(ps[0:META, 3, 0:P], vT[:, 0:META], ident[:, :])
                        for j in range(TILES):
                            last = pe.transpose(ps[:, 7, j * P:(j + 1) * P], vT[:, META + j * P:META + (j + 1) * P],
                                                ident[:, :])
                        last.then_inc(vt_done, 1)
                    if u == 3:
                        values(0)
                values(1)

            def gate(m, m2, name, j, it, which=range(2)):
                for k in which:
                    if not isinstance(m, int) or m >= 2:
                        pe.wait_ge(g_ev, m * 2 + (k - 3) + CR)
                    last = channels_by_tokens(name, j + k, it, [(ps[:, gate_bank[m2][k], :], slice(META, L))])
                    last.then_inc(used, 1)

            def mean(m):
                return pe.matmul(ps[:, 5, :], mean_w[:, :], y[:, m, :], start=(m == 0), stop=(m == PAIRS - 1))

            gate(0, 0, "gate", 0, 0, [1])
            pe.wait_ge(conv_done, PAIRS - 1 + CR)
            for m in range(PAIRS - 1):
                mean(m)
            pe.wait_ge(av_lo, PAIRS + CR)
            gate(1, 1, "gate", 2, 0)
            pe.wait_ge(conv_done, PAIRS + CR)
            mean(PAIRS - 1).then_inc(ln_mean, 1)
            gate(2, 0, "gate", 4, 0, [0])
            for m in range(PAIRS):
                pe.wait_ge(ln_sq, m + 1)
                last = pe.matmul(ps[:, 6, :], mean_w[:, :], sq_ln[:, m, :], start=(m == 0), stop=(m == PAIRS - 1))
            last.then_inc(ln_var, 1)
            gate(2, 0, "gate", 4, 0, [1])

            def branches(name, j, it, m, m2):
                hi, lo = weights(pe, name, j, it, P)
                pe.wait_ge(br_ev, m * 2 - 2 + CR)
                if name == "mix" and m2 == 0:
                    pe.wait_ge(g_ev, 1 + CR)
                for b, (left_hi, left_lo) in enumerate(((attT_hi, attT_lo), (yT_hi, yT_lo))):
                    for c in range(PAIRS):
                        if b:
                            pe.wait_ge(ln_lo, c + 1)
                        w = (hi[:, 4 * b + c, :], lo[:, 4 * b + c, :])
                        last = product(pe, ps[:, branch_bank[m2][b], :], w, (left_hi[:, c, :], left_lo[:, c, :]), c == 0, c == PAIRS - 1)
                    if b == 0:
                        last.then_inc(br_done, 1)
                last.then_inc(used, 1)

            with pe.Fori(0, 2) as it:
                for k in range(2):
                    branches("mix", 3 * k, it, it * 2 + k, k)
                    gate(it * 2 + (k + 3), (k + 1) % 2, "mix", 3 * k + 1, it)
            branches("last", 0, 0, 4, 0)
            gate(7, 1, "last", 1, 0)
            for k in range(3):
                branches("last", 3 + k, 0, 5 + k, (5 + k) % 2)

            for half in range(2):
                pe.wait_ge(g_ev, 14 + 2 * half + CR)
                pe.wait_ge(br_ev, 14 + 2 * half + CR)
                for q in range(4):
                    hi, lo = weights(pe, "out", 4 * half + q, 0, 512)

                    def part(i, m2):
                        tok = slice(i * P, (i + 1) * P)
                        m = 2 * q + m2
                        return product(pe, ps[:, out_bank[4 * half + i], :], (mT_hi[:, m, tok], mT_lo[:, m, tok]),
                                       (hi[:, m2, :], lo[:, m2, :]), m == 0, m == KB - 1)

                    if q < 3:
                        for m2 in range(2):
                            pe.wait_ge(m_lo, 2 * q + m2 + 1)
                            for i in range(TILES):
                                last = part(i, m2)
                    else:
                        pe.wait_ge(m_lo, KB)
                        for i in range(TILES):
                            part(i, 0)
                            last = part(i, 1)
                            if i < TILES - 1:
                                last.then_inc(out_done, 1)
                    last.then_inc(used, 1)

            pe.wait_ge(res, TILES + 1)

            def turn2(i):
                pe.wait_ge(s_xn2, i + 1)
                if i >= 2:
                    pe.wait_ge(s_xe2, i - 1)
                src = xn2[:, i, :].rearrange("p (q k) -> p k q", k=KB)
                for k in range(KB):
                    last = pe.transpose(ps[:, 2 * (i % 2) + k // 4, (k % 4) * P:(k % 4 + 1) * P], src[:, k, :], ident[:, :])
                last.then_inc(s_xt2, 1)

            turn2(0)
            turn2(1)
            pe.wait_ge(s_router, 16 * 4)
            for i in range(TILES):
                pe.wait_ge(s_xe2, i + 1)
                for k in range(KB):
                    last = pe.matmul(ps[0:GROUPS + E, 4, i * P:(i + 1) * P], router_w[:, k, :], xn2T[:, i % 2, k, :],
                                     start=(k == 0), stop=(k == KB - 1))
                last.then_inc(s_logit, 1)
                if i + 2 < TILES:
                    turn2(i + 2)
            pe.wait_ge(s_lcopy, 1)
            pe.wait_ge(res, 2 * TILES)
            n = GROUPS + E
            for i in range(TILES):
                last = pe.transpose(ps[:, 7, i * n:(i + 1) * n], logitT[:, i * P:(i + 1) * P], ident[0:n, 0:n])
            last.then_inc(s_lturn, 1)
            pe.wait_ge(s_hotx, 1)
            for i in range(TILES + 1):
                for j in range(min(i + 1, TILES)):
                    last = pe.matmul(ps[:, 6, i * E:(i + 1) * E], (before_bf if j == i else ones_bf)[:, :], H_bf[:, j, :],
                                     start=(j == 0), stop=(j == min(i, TILES - 1)))
            last.then_inc(s_rank, 1)
            pe.wait_ge(s_place, 1)
            M = TOP * TILES
            for m in range(M):
                last = pe.matmul(ps[:, 5, 0:ICOLS], place_hot[:, m, :], block_hot[:, m, :], start=(m == 0), stop=(m == M - 1))
            last.then_inc(s_table, 1)

            def inputs(b, half):
                pe.wait_ge(gath, b * 16 + 16)
                pe.wait_ge(xe_lo, b * 2 + half - 1 + CR)
                src = xe[:, :].rearrange("p (q k) -> p k q", k=KB)
                for k in range(4):
                    last = pe.transpose(ps[:, half, k * P:(k + 1) * P], src[:, 4 * half + k, :], ident[:, :])
                last.then_inc(tx, 1)

            def expert_pe(name, it, b, o=0):
                pe.wait_ge(xe_lo, b * 2 + 2 + CR)
                for part in range(2):
                    if part == 0:
                        pe.wait_ge(silu, b + CR)
                    else:
                        pe.wait_ge(hdn_done, b * 2 + CR)
                    for q in range(4):
                        hi, lo = weights(pe, name, o + 4 * part + q, it, FF)
                        for k2 in range(2):
                            k = 2 * q + k2
                            last = product(pe, ps[:, 2 + part, :], (xeT_hi[:, k, :], xeT_lo[:, k, :]),
                                           (hi[:, k2, :], lo[:, k2, :]), k == 0, k == KB - 1)
                        last.then_inc(used, 1)
                for half in range(2):
                    inputs(b + 1, half)
                    pe.wait_ge(hdn_done, b * 2 + half + 1 + CR)
                    for f in range(2):
                        last = pe.transpose(ht_bank[half][:, f * P:(f + 1) * P], hdn[:, (2 * half + f) * P:][:, 0:P],
                                            ident[:, :])
                    last.then_inc(ht, 1)
                pe.wait_ge(yev, b + CR)
                for f in range(FB):
                    hi, lo = weights(pe, name, o + 8 + f, it, 512)
                    if f % 2 == 0:
                        pe.wait_ge(ht_hi, b * 2 + f // 2 + 1)
                    for c in range(2):
                        pe.matmul(ps[:, 5 + c, :], hT_hi[:, f, :], hi[:, c, :], start=(f == 0), stop=False)
                        pe.matmul(ps[:, 5 + c, :], hT_hi[:, f, :], lo[:, c, :], start=False, stop=False)
                    if f % 2 == 0:
                        pe.wait_ge(ht_lo, b * 2 + f // 2 + 1)
                    for c in range(2):
                        last = pe.matmul(ps[:, 5 + c, :], hT_lo[:, f, :], hi[:, c, :], start=False, stop=(f == FB - 1))
                    last.then_inc(used, 1)

            inputs(0, 0)
            inputs(0, 1)
            with pe.Fori(0, E // 2) as it:
                for k in range(2):
                    expert_pe("expert", it, it * 2 + k, 12 * k)
            pe.wait_ge(s_regs, 1)
            count = pe.value_load(regs[0:1, 0:1], min_val=0, max_val=OVER)
            with pe.Fori(0, OVER) as b:
                with pe.If(b < count):
                    expert_pe("over", b, b + E)


_INS = ["x", "meta", "norm_mix", "w_in", "w_sb_o", "conv_w", "conv_b", "conv_ln_g", "conv_ln_b", "w_conv_o", "w_out",
        "norm_ffn", "w_router_group", "b_router_group", "w_router_expert", "b_router_expert", "w_gate", "w_up", "w_down",
        "norm_final"]


def kernel(**inputs):
    import numpy as np
    import concourse.bacc as bacc
    from concourse.bass_utils import run_bass_kernel_spmd

    nc = bacc.Bacc("TRN2", target_bir_lowering=False, num_devices=1)
    arrays, args = {}, []
    for name in _INS:
        a = np.ascontiguousarray(inputs[name])
        arrays[f"in_{name}"] = a
        args.append(nc.dram_tensor(f"in_{name}", a.shape, mybir.dt.from_np(a.dtype), kind="ExternalInput").ap())
    args.append(nc.dram_tensor("out", (1, SEQ, D), F32, kind="ExternalOutput").ap())
    args.append(nc.dram_tensor("xn2_dram", (SEQ, D), F32, kind="Internal").ap())
    args.append(nc.dram_tensor("y_dram", (BLOCKS * P, D), F32, kind="Internal").ap())
    build(nc, *args)
    return run_bass_kernel_spmd(nc, [arrays], core_ids=[0]).results[0]["out"]
```

```python
from contextlib import ExitStack

import concourse.bass as bass
from concourse import mybir

F32 = mybir.dt.float32
F32R = mybir.dt.float32r
BF16 = mybir.dt.bfloat16
I32 = mybir.dt.int32
U32 = mybir.dt.uint32
ALU = mybir.AluOpType
ACT = mybir.ActivationFunctionType
AX = mybir.AxisListType
ds = bass.ds

P = 128
D = 1024
KB = D // P
SEQ = 512
META = 16
L = META + SEQ
TILES = SEQ // P
HALF = L // 2
DH = 64
PAIRS = 4
CONV = 512
TAPS = 31
HIST = TAPS - 1
EPS = 1e-6
SCALE = DH ** -0.5
MASKED = -1e30
COL_Q, COL_K, COL_V, COL_A, COL_B, COL_GSB, COL_GCV = 0, 512, 1024, 1536, 2048, 2560, 3584
GROUPS, PER_GROUP = 4, 4
E = GROUPS * PER_GROUP
FF = 512
FB = FF // P
TOP = 2
OVER = (TOP * SEQ - 2) // P
OVER_RUNS = (OVER + 1) // 2
BLOCKS = E + 2 * OVER_RUNS
ICOLS = BLOCKS + 4
CHUNK = 1024
CR = 24


class Stream:

    def __init__(self, segments):
        self.seg, g, taken = {}, 0, {}
        last_raw, last_split = {}, {}
        for name, iters, slots, peeled in segments:
            per = {r: sum(1 for a, _ in slots if a == r) for r, _ in slots}
            info = {"peeled": peeled, "g": g, "n": len(slots), "slots": slots, "per": per, "base": dict(taken),
                    "raw": [99] * len(slots), "split": [99] * len(slots), "first": [99] * len(slots)}
            for it in range(iters):
                for j, (r, s) in enumerate(slots):
                    dist = "first" if peeled and it == 0 else "raw"
                    info[dist][j] = min(info[dist][j], g - last_raw.get(r, g - CR))
                    info["split"][j] = min(info["split"][j], g - last_split.get(s, g - CR))
                    last_raw[r], last_split[s] = g, g
                    taken[r] = taken.get(r, 0) + 1
                    g += 1
            self.seg[name] = info

    def at(self, name, j, it):
        info = self.seg[name]
        if j >= info["n"]:
            j, it = j - info["n"], it + 1
        r, s = info["slots"][j]
        before = sum(1 for a, _ in info["slots"][:j] if a == r)
        loads = it * info["per"][r] + info["base"].get(r, 0) + before + 1
        dist = info["first" if info["peeled"] and isinstance(it, int) and it == 0 else "raw"]
        return it * info["n"] + info["g"] + j, r, s, loads, min(dist[j], CR), min(info["split"][j], CR)


RAW, SPLIT = 24, 6
AHEAD = 5
STREAM = Stream([
    ("pair", PAIRS, [(0, 0), (1, 1), (2, 2), (3, 3), (4, 1)], False),
    ("gate", 1, [(0, 0), (1, 1), (2, 2), (3, 3), (4, 1), (5, 2)], False),
    ("mix", 2, [(0, 0), (1, 1), (2, 2), (3, 0), (4, 1), (5, 2)], False),
    ("last", 1, [(0, 0), (1, 1), (2, 2), (3, 3), (4, 0), (5, 1)], False),
    ("out", 1, [(0, 2), (1, 3), (2, 0), (3, 1), (4, 2), (5, 3), (3, 2), (4, 3)], False),
    ("expert", E // 2, [(j, j % SPLIT) for j in range(24)], True),
    ("over", OVER_RUNS, [(j, j % SPLIT) for j in range(24)], False),
])


def build(nc, x, meta, norm_mix, w_in, w_sb_o, conv_w, conv_b, conv_ln_g, conv_ln_b, w_conv_o, w_out, norm_ffn,
          w_router_group, b_router_group, w_router_expert, b_router_expert, w_gate, w_up, w_down, norm_final, out,
          xn2_dram, y_dram):
    with ExitStack() as ctx:
        ctx.enter_context(nc.allow_non_contiguous_dma(reason="small vectors"))
        at = [0]

        def sb(name, shape, dt=F32):
            n = 1
            for k in shape[1:]:
                n *= k
            t = nc.alloc_sbuf_tensor_at(name, shape, dt, offset=at[0])
            at[0] += -(-n * (2 if dt == BF16 else 4) // 32) * 32
            return t

        def sem(name):
            return ctx.enter_context(nc.semaphore(name))

        at[0] = -(-nc.sbuf_base // 32) * 32
        raw = [sb(f"raw{i}", [P, CHUNK]) for i in range(6)]
        w_hi = [sb(f"w_hi{i}", [P, CHUNK], F32R) for i in range(4)]
        w_lo = [sb(f"w_lo{i}", [P, CHUNK], F32R) for i in range(4)]
        h = sb("h", [P, TILES, D])
        ident = sb("ident", [P, P])
        ident_bf = sb("ident_bf", [P, P], BF16)
        mask_bf = sb("mask_bf", [P, P], BF16)
        before_bf = sb("before_bf", [P, P], BF16)
        ones_bf = sb("ones_bf", [P, P], BF16)
        mean_w = sb("mean_w", [P, P])
        ones_row = sb("ones_row", [P, L])
        eps = sb("eps", [P, 1])
        table = sb("table", [P, 1])
        zero_row = sb("zero_row", [P, D // 4])
        sumsq = sb("sumsq", [P, 16])
        std = sb("std", [P, 16])
        rstd = sb("rstd", [P, 16])
        w_tok = sb("w_tok", [P, TOP, TILES])
        slot_y = sb("slot_y", [P, TOP, TILES], U32)
        regs = sb("regs", [P, 3 + OVER + 2], I32)
        cw = sb("cw", [P, PAIRS, TAPS + 3])
        router_w = sb("router_w", [P, KB, GROUPS + E])
        bias_rt = sb("bias_rt", [P, GROUPS + E])
        region = at[0]
        attT_hi = sb("attT_hi", [P, PAIRS, SEQ], F32R)
        attT_lo = sb("attT_lo", [P, PAIRS, SEQ], F32R)
        vT = nc.alloc_sbuf_tensor_at("vT", [P, L], F32, offset=at[0])
        sgate = sb("sgate", [P, 2, SEQ])
        cgate = sb("cgate", [P, 2, SEQ])
        merged = sb("merged", [P, SEQ])
        y = sb("y", [P, PAIRS, SEQ])
        region_end = at[0]
        at[0] = region
        raw += [sb(f"raw{i}", [P, CHUNK]) for i in range(6, 12)]
        w_hi.append(sb("w_hi4", [P, CHUNK], F32R))
        w_lo.append(sb("w_lo4", [P, CHUNK], F32R))
        assert at[0] <= region_end
        at[0] = region_end
        region = at[0]
        xnT_hi = sb("xnT_hi", [P, KB, L], F32R)
        xnT_lo = sb("xnT_lo", [P, KB, L], F32R)
        region_end = at[0]
        at[0] = region
        g_ffn = sb("g_ffn", [P, D])
        square2 = sb("square2", [P, D])
        xn2 = sb("xn2", [P, TILES, D])
        rt = {}
        for name, n in (("logit", TILES * 20), ("ohg", TILES * 4), ("gtmp", TILES * 4), ("gsum", TILES),
                        ("gmax", TILES), ("cand", TILES * 4), ("best", TILES), ("sel", TILES * E), ("el", TILES * 4),
                        ("ex", TILES), ("el2", TILES * 4), ("oh1", TILES * 4), ("oh2", TILES * 4), ("p1", TILES),
                        ("p2", TILES), ("H12", TOP * TILES * E), ("sel_t1", TOP * TILES * E),
                        ("sel_place_of", TOP * TILES * E), ("place_of", TILES * E), ("block", TOP * TILES),
                        ("place", TOP * TILES), ("row", TOP * TILES), ("hot", TOP * TILES * ICOLS), ("number", P),
                        ("token", TOP * TILES), ("fb", TILES * E), ("t1", TILES * E), ("t2", TILES * E), ("ovn", E),
                        ("cum", E), ("t3", E), ("bex", (OVER + 1) * E), ("bexi", OVER + 1), ("runs", 2), ("desc", 4),
                        ("eidx", E), ("rest", E), ("bidx", OVER + 1), ("onesE", E), ("over3", E * (TILES - 1)),
                        ("ge3", TILES * E * (TILES - 1)), ("steps", TILES - 1)):
            rt[name] = sb("rt_" + name, [P, n])
        H_bf = sb("H_bf", [P, TILES, E], BF16)
        assert at[0] <= region_end, (at[0], region_end)
        at[0] = region
        g_fin = nc.alloc_sbuf_tensor_at("g_fin", [P, D], F32, offset=region)
        late = {i: sb(f"raw{i}", [P, CHUNK]) for i in (14, 15, 16, 17, 18, 19, 22, 23)}
        assert at[0] <= region_end, (at[0], region_end)
        at[0] = region_end
        region = at[0]
        sig = sb("sig", [P, 3, L])
        stay = sb("stay", [P, 3, L + 1])
        xn = nc.alloc_sbuf_tensor_at("xn", [P, TILES + 1, D], F32, offset=at[0])
        after = sb("after", [P, 3, L])
        probT = sb("probT", [P, TILES, SEQ])
        probT_meta = sb("probT_meta", [META, SEQ])
        qT = sb("qT", [P, SEQ])
        kT = sb("kT", [P, L])
        v_sb = sb("v_sb", [P, TILES, P])
        v_meta = sb("v_meta", [META, P])
        attention_end = at[0]
        assert attention_end - region >= 2 * 12 * L + 4 * (TILES + 1) * D
        at[0] = region
        mT_hi = sb("mT_hi", [P, KB, SEQ], F32R)
        mT_lo = sb("mT_lo", [P, KB, SEQ], F32R)
        region_end = max(at[0], attention_end)
        sq_ln = nc.alloc_sbuf_tensor_at("sq_ln", [P, PAIRS, SEQ], F32, offset=region)
        at[0] = region
        xe = [sb("xe0", [P, D])]
        xeT_hi = sb("xeT_hi", [P, KB, P], F32R)
        xeT_lo = sb("xeT_lo", [P, KB, P], F32R)
        silu_g = sb("silu_g", [P, FF])
        hdn = sb("hdn", [P, FF])
        hT_hi = sb("hT_hi", [P, FB, P], F32R)
        hT_lo = sb("hT_lo", [P, FB, P], F32R)
        y_sb = [sb("y_sb0", [P, D])]
        index_sb = sb("index_sb", [P, ICOLS], I32)
        index_1 = sb("index_1", [P, 2], U32)
        w_hi.append(sb("w_hi5", [P, CHUNK], F32R))
        w_lo.append(sb("w_lo5", [P, CHUNK], F32R))
        assert at[0] <= region_end
        at[0] = region_end
        region = at[0]
        a_sb = sb("a_sb", [P, L])
        b_sb = sb("b_sb", [P, L])
        u_pad = sb("u_pad", [P, HIST + L])
        y_acc = sb("y_acc", [P, SEQ])
        cw_c = sb("cw_c", [P, TAPS + 3])
        conv_end = at[0]
        block_hot = nc.alloc_sbuf_tensor_at("block_hot", [P, TOP * TILES, ICOLS], F32R, offset=region + 4 * SEQ)
        late.update({20 + i: nc.alloc_sbuf_tensor_at(f"raw{20 + i}", [P, CHUNK], F32, offset=region + i * 4 * CHUNK)
                     for i in range(2)})
        assert region + 2 * 4 * CHUNK <= conv_end
        logitT = nc.alloc_sbuf_tensor_at("logitT", [GROUPS + E, SEQ], F32, offset=region)
        at[0] = region
        rstd_ln = sb("rstd_ln", [P, SEQ])
        silu_y = sb("silu_y", [P, 2, SEQ])
        at[0] = max(conv_end, at[0])
        region = at[0]
        x_meta = sb("x_meta", [META, D])
        g_mix = sb("g_mix", [P, D])
        pack = sb("pack", [TAPS + 3, CONV])
        norm_end = at[0]
        at[0] = region
        yT_hi = sb("yT_hi", [P, PAIRS, SEQ], F32R)
        yT_lo = sb("yT_lo", [P, PAIRS, SEQ], F32R)
        at[0] = region
        pick = sb("pick", [P, 2, D])
        late.update({12 + i: nc.alloc_sbuf_tensor_at(f"raw{12 + i}", [P, CHUNK], F32, offset=region + i * 4 * CHUNK)
                     for i in range(2)})
        raw += [late[i] for i in range(12, RAW)]
        xn2T = nc.alloc_sbuf_tensor_at("xn2T", [P, 2, KB, P], F32, offset=region)
        xe.append(sb("xe1", [P, D]))
        y_sb.append(nc.alloc_sbuf_tensor_at("y_sb1", [P, D], F32, offset=at[0]))
        place_hot = sb("place_hot", [P, TOP * TILES, P], F32R)
        at[0] = max(at[0], norm_end)
        assert at[0] <= nc.sbuf_usable_end, (at[0], nc.sbuf_usable_end)
        square = y

        ps = ctx.enter_context(nc.psum_tensor("ps", [P, 8, 512], F32))

        s_const = sem("s_const")
        s_x = [sem(f"s_x{i}") for i in range(TILES + 1)]
        s_gmix = sem("s_gmix")
        s_pack = sem("s_pack")
        s_router = sem("s_router")
        s_sq = sem("s_sq")
        s_std = sem("s_std")
        s_xn = sem("s_xn")
        s_xt = sem("s_xt")
        s_xhi = sem("s_xhi")
        s_xlo = sem("s_xlo")
        s_cwt = sem("s_cwt")
        s_cw = sem("s_cw")
        load = [sem(f"load{i}") for i in range(RAW)]
        hi_done = sem("hi_done")
        lo_done = sem("lo_done")
        used = sem("used")
        ev = sem("ev")
        z_done = sem("z_done")
        sig_done = sem("sig_done")
        scan_done = sem("scan_done")
        prob_done = sem("prob_done")
        t_done = sem("t_done")
        tev = sem("tev")
        mev = sem("mev")
        vt_done = sem("vt_done")
        v_ev = sem("v_ev")
        av_done = sem("av_done")
        av_hi = sem("av_hi")
        av_lo = sem("av_lo")
        u_done = sem("u_done")
        conv_done = sem("conv_done")
        g_ev = sem("g_ev")
        ln_mean = sem("ln_mean")
        ln_xc = sem("ln_xc")
        ln_sq = sem("ln_sq")
        ln_var = sem("ln_var")
        ln_std = sem("ln_std")
        ln_rstd = sem("ln_rstd")
        ln_n = sem("ln_n")
        ln_act = sem("ln_act")
        ln_hi = sem("ln_hi")
        ln_lo = sem("ln_lo")
        br_done = sem("br_done")
        br_ev = sem("br_ev")
        m_hi = sem("m_hi")
        m_lo = sem("m_lo")
        out_done = sem("out_done")
        res = sem("res")
        s_sq2 = sem("s_sq2")
        s_std2 = sem("s_std2")
        s_xn2 = sem("s_xn2")
        s_xn2_out = [sem(f"s_xn2_out{i}") for i in range(TILES)]
        s_xt2 = sem("s_xt2")
        s_xe2 = sem("s_xe2")
        s_logit = sem("s_logit")
        s_lcopy = sem("s_lcopy")
        s_lturn = sem("s_lturn")
        s_gffn = sem("s_gffn")
        s_gexp = sem("s_gexp")
        s_need = sem("s_need")
        s_hot = sem("s_hot")
        s_rank = sem("s_rank")
        s_hotx = sem("s_hotx")
        br_mul = sem("br_mul")
        s_slot = sem("s_slot")
        s_yzero = sem("s_yzero")
        s_place = sem("s_place")
        s_table = sem("s_table")
        s_regs = sem("s_regs")
        s_rows = sem("s_rows")
        s_weights = sem("s_weights")
        idx1 = [sem(f"idx1_{k}") for k in range(2)]
        gath = [sem(f"gath{k}") for k in range(2)]
        tx = sem("tx")
        xe_hi = sem("xe_hi")
        xe_lo = sem("xe_lo")
        silu = sem("silu")
        hdn_done = sem("hdn_done")
        ht = sem("ht")
        ht_hi = sem("ht_hi")
        ht_lo = sem("ht_lo")
        yev = sem("yev")
        ystore = [sem(f"ystore{k}") for k in range(2)]
        pick_sem = [[sem(f"pick{k}_{i}") for i in range(TILES)] for k in range(TOP)]
        s_split_end = sem("s_split_end")
        sum1 = sem("sum1")
        sum2 = sem("sum2")
        s_sq3 = sem("s_sq3")
        s_std3 = sem("s_std3")
        s_recip3 = sem("s_recip3")
        s_r3 = sem("s_r3")
        s_fin_last = sem("s_fin_last")
        s_fin = sem("s_fin")
        s_out = sem("s_out")
        s_gfin = sem("s_gfin")
        passed = sem("passed")
        dchain = sem("dchain")
        pchain = sem("pchain")

        def cols(w, n):
            return w.rearrange("p (k n) -> p k n", n=n)

        def w_in_cols(col):
            return w_in[0].rearrange("(p k) n -> p k n", k=KB)[:, :, col]

        def split_hi(act, name, j, it):
            g, r, s, loads, _, back = STREAM.at(name, j, it)
            act.wait_ge(load[r], loads * 32)
            act.wait_ge(used, g - back + 1 + CR)
            act.copy(w_hi[s][:, :], raw[r][:, :]).then_inc(hi_done, 1)

        def split_lo(dve, name, j, it):
            g, r, s, _, _, _ = STREAM.at(name, j, it)
            dve.wait_ge(hi_done, g + 1)
            dve.tensor_tensor(w_lo[s][:, :], raw[r][:, :], w_hi[s][:, :].bitcast(F32), ALU.subtract)\
               .then_inc(lo_done, 1)

        def weights(pe, name, j, it, n):
            g, _, s, _, _, _ = STREAM.at(name, j, it)
            pe.wait_ge(lo_done, g + 1 + CR)
            return cols(w_hi[s][:, :], n), cols(w_lo[s][:, :], n)

        def taken(eng, name, j, it):
            eng.wait_ge(used, STREAM.at(name, j, it)[0] + 1 + CR)

        def product(pe, dst, left, right, start, stop):
            pe.matmul(dst, left[0], right[0], start=start, stop=False)
            pe.matmul(dst, left[0], right[1], start=False, stop=False)
            return pe.matmul(dst, left[1], right[0], start=False, stop=stop)

        gate_bank = [(0, 2), (1, 7)]
        branch_bank = [(3, 4), (5, 6)]
        out_bank = [3, 4, 0, 2, 1, 7, 5, 6]
        turn_bank = [5, 1]

        def last_user(u):
            return u - 2 if u >= 3 else (-1, 0, -2)[u]

        ht_bank = [ps[:, 4, 0:2 * P], ps[:, 7, 0:2 * P]]

        def picked(k, i):
            return xn2[:, i, :] if k == 0 else pick[:, i, :] if i < 2 else raw[i][:, :]

        def first_tile(t):
            if t == 0:
                return META, x_meta[:, :], xn[0:META, 0, :], ps[:, 0, 0:KB * META].rearrange("p (k n) -> p k n", n=META), \
                    slice(0, META)
            bank = 2 * (t % 4)
            return P, h[:, t - 1, :], xn[:, t, :], ps[:, bank:bank + 2, :].rearrange("p b (k n) -> p (b k) n", n=P), \
                slice(META + (t - 1) * P, META + t * P)

        def first_lo(dve, t):
            _, _, _, src, to = first_tile(t)
            dve.wait_ge(s_xhi, t + 1)
            dve.tensor_tensor(xnT_lo[:, :, to], src, xnT_hi[:, :, to].bitcast(F32), ALU.subtract).then_inc(s_xlo, 1)

        block = ctx.enter_context(nc.Block())

        @block.sync
        def _(sp):
            sp.dma_start(x_meta[:, :], meta).then_inc(s_x[0], 16)
            for i in range(TILES):
                sp.dma_start(h[:, i, :], x[0, i * P:(i + 1) * P, :]).then_inc(s_x[i + 1], 16)
                if i == 0:
                    sp.dma_start(g_mix[:, :], norm_mix[0].partition_broadcast(P)).then_inc(s_gmix, 16)

            def chunk(name, j, it, pieces):
                g, r, _, _, back, _ = STREAM.at(name, j, it)
                sp.wait_ge(lo_done, g - back + 1 + CR)
                sp.sem_inc(passed, 1)
                sp.dma_start(*pieces(raw[r])).then_inc(load[r], 32)

            def in_cols(col):
                return lambda slot: (cols(slot[:, :], P), w_in_cols(col))

            def branch_chunk(name, j, it, m):
                g, r, _, _, back, _ = STREAM.at(name, j, it)
                sp.wait_ge(lo_done, g - back + 1 + CR)
                sp.sem_inc(passed, 1)
                v = raw[r][:, :].rearrange("p (b c n) -> p b c n", b=2, n=P)
                sp.dma_start(v[:, 0], w_sb_o[0].rearrange("(c p) n -> p c n", p=P)[:, :, ds(m * P, P)])\
                  .then_inc(load[r], 16)
                sp.dma_start(v[:, 1], w_conv_o[0].rearrange("(c p) n -> p c n", p=P)[:, :, ds(m * P, P)])\
                  .then_inc(load[r], 16)

            with sp.Fori(0, PAIRS) as c:
                for j, col in enumerate((COL_A, COL_K, COL_Q, COL_B, COL_V)):
                    chunk("pair", j, c, in_cols(ds(c * P + col, P)))
            for m in range(3):
                chunk("gate", 2 * m, 0, in_cols(ds(COL_GSB + m * P, P)))
                chunk("gate", 2 * m + 1, 0, in_cols(ds(COL_GCV + m * P, P)))
            with sp.Fori(0, 2) as n:
                for k in range(2):
                    branch_chunk("mix", 3 * k, n, n * 2 + k)
                    chunk("mix", 3 * k + 1, n, in_cols(ds(n * (2 * P) + (COL_GSB + (k + 3) * P), P)))
                    chunk("mix", 3 * k + 2, n, in_cols(ds(n * (2 * P) + (COL_GCV + (k + 3) * P), P)))
            branch_chunk("last", 0, 0, 4)
            chunk("last", 1, 0, in_cols(ds(COL_GSB + 7 * P, P)))
            chunk("last", 2, 0, in_cols(ds(COL_GCV + 7 * P, P)))
            for k in range(3):
                branch_chunk("last", 3 + k, 0, 5 + k)
            wo = w_out[0].rearrange("(m p) n -> p m n", p=P)
            for half in range(2):
                for q in range(4):
                    chunk("out", 4 * half + q, 0, lambda slot: (
                        cols(slot[:, :], 512), wo[:, 2 * q:2 * q + 2, 512 * half:512 * half + 512]))

            def expert_loads(name, it, e, which):
                for j in which:
                    part, q = (j % 12) // 4, j % 4
                    if part < 2:
                        src = (w_gate, w_up)[part][0, ds(e, 1)].rearrange("e (p k) n -> p (e k) n", k=KB)
                        chunk(name, j, it, lambda slot: (cols(slot[:, :], FF), src[:, 2 * q:2 * q + 2, :]))
                    else:
                        src = w_down[0, ds(e, 1)].rearrange("e (f p) n -> p (e f) n", f=FB)
                        chunk(name, j, it, lambda slot: (slot[:, :], src[:, q, :]))

            expert_loads("expert", 0, 0, range(6))
            taken(sp, "last", 5, 0)
            sp.wait_ge(br_ev, 16 + CR)
            expert_loads("expert", 0, 0, range(6, 12))
            for i in range(TILES):
                sp.wait_ge(s_xn2, i + 1)
                sp.dma_start(xn2_dram[i * P:(i + 1) * P, :], xn2[:, i, :]).then_inc(s_xn2_out[i], 16)
            expert_loads("expert", 0, 1, (14,))
            sp.wait_ge(s_sq2, TILES)
            expert_loads("expert", 0, 1, (15,))
            sp.wait_ge(s_logit, TILES)
            expert_loads("expert", 0, 1, (12, 13))
            sp.wait_ge(s_xt2, TILES)
            for i in range(TILES):
                sp.wait_ge(s_xn2_out[i], 16)
                expert_loads("expert", 0, 1, (16 + i,))
            sp.wait_ge(s_table, 1)
            sp.wait_ge(gath[0], 16)
            expert_loads("expert", 0, 1, (20, 21))
            sp.wait_ge(s_weights, 1)
            expert_loads("expert", 0, 1, (22, 23))
            with sp.Fori(1, E // 2) as it:
                expert_loads("expert", it, it * 2, range(12))
                expert_loads("expert", it, it * 2 + 1, range(12, 24))
            sp.wait_ge(s_regs, 1)
            count = sp.value_load(regs[0:1, 0:1], min_val=0, max_val=OVER)
            first = sp.value_load(regs[0:1, 1:2], min_val=0, max_val=E - 1)
            expert_loads("over", 0, first, range(AHEAD))
            with sp.Fori(0, OVER_RUNS) as it:
                for k in range(2):
                    with sp.If(it * 2 + k < count):
                        e = sp.value_load(regs[0:1, ds(it * 2 + (k + 1), 1)], min_val=0, max_val=E - 1)
                        expert_loads("over", it, e, range(12 * k + AHEAD, 12 * k + 12))
                        following = sp.value_load(regs[0:1, ds(it * 2 + (k + 2), 1)], min_val=0, max_val=E - 1)
                        expert_loads("over", it, following, range(12 * k + 12, 12 * k + 12 + AHEAD))
            sp.wait_ge(s_split_end, 1)
            sp.dma_start(g_fin[:, :], norm_final.partition_broadcast(P)).then_inc(s_gfin, 16)
            for i in range(TILES):
                if i < TILES - 2:
                    sp.wait_ge(s_fin, i + 1)
                else:
                    sp.wait_ge(s_fin_last, i - (TILES - 2) + 1)
                sp.dma_start(out[0, i * P:(i + 1) * P, :], h[:, i, :]).then_inc(s_out, 16)
            sp.wait_ge(s_out, 16 * TILES)

        @block.gpsimd
        def _(pool):
            for s in (u_done, prob_done):
                pool.sem_inc(s, CR)
            n = [0]

            def link(ins):
                n[0] += 1
                ins.then_inc(pchain, 1)
                pool.wait_ge(pchain, n[0])

            pool.memset(eps[:, :], EPS).then_inc(s_const, 1)
            link(pool.memset(ident[:, :], 0.0))
            pool.affine_select(out=ident[:, :], in_=ident[:, :], compare_op=ALU.not_equal, fill=1.0, base=0,
                               pattern=[[-1, P]], channel_multiplier=1).then_inc(s_const, 1)
            for row, src in ((0, conv_w[0]), (TAPS, conv_b), (TAPS + 1, conv_ln_g), (TAPS + 2, conv_ln_b)):
                pool.dma_start(pack[row:row + (TAPS if row == 0 else 1), :], src).then_inc(s_pack, 16)
            pool.wait_ge(s_const, 2)
            pool.tensor_copy(ident_bf[:, :], ident[:, :])
            link(pool.memset(mask_bf[:, :], 0.0))
            pool.affine_select(out=mask_bf[:, :], in_=mask_bf[:, :], compare_op=ALU.is_gt, fill=MASKED, base=0,
                               pattern=[[-1, P]], channel_multiplier=1)
            link(pool.memset(before_bf[:, :], 0.0))
            pool.affine_select(out=before_bf[:, :], in_=before_bf[:, :], compare_op=ALU.is_ge, fill=1.0, base=0,
                               pattern=[[-1, P]], channel_multiplier=1)
            pool.memset(ones_bf[:, :], 1.0)
            pool.memset(mean_w[:, :], 1.0 / CONV)
            pool.memset(ones_row[:, :], 1.0)
            pool.memset(stay[:, :, L:L + 1], 1.0)
            link(pool.memset(u_pad[:, 0:HIST], 0.0))
            pool.sem_inc(s_const, 1)
            pool.dma_start(router_w[:, :, 0:GROUPS], w_router_group[0].rearrange("(p k) n -> p k n", k=KB))\
                .then_inc(s_router, 16)
            pool.dma_start(router_w[:, :, GROUPS:], w_router_expert[0].rearrange("(p k) n -> p k n", k=KB))\
                .then_inc(s_router, 16)
            pool.dma_start(bias_rt[:, 0:GROUPS], b_router_group[0].partition_broadcast(P)).then_inc(s_router, 16)
            pool.dma_start(bias_rt[:, GROUPS:], b_router_expert[0].partition_broadcast(P)).then_inc(s_router, 16)

            with pool.Fori(0, PAIRS) as c:
                pool.wait_ge(ev, c * 5 + 4 + CR)
                pool.wait_ge(conv_done, c + CR)
                pool.tensor_tensor(u_pad[:, HIST:], a_sb[:, :], b_sb[:, :], ALU.mult).then_inc(u_done, 1)
                for u in range(8):
                    off = (u % 4) * P
                    pool.wait_ge(scan_done, c * 8 + u + 1)
                    pool.tensor_tensor(sig[:, u % 3, off:], sig[:, u % 3, off:], after[:, u % 3, off:], ALU.mult)\
                        .then_inc(prob_done, 1)

            link(pool.memset(zero_row[:, :], 0.0))
            for b in range(E, BLOCKS):
                pool.dma_start(y_dram[b * P:(b + 1) * P, :].rearrange("p (r c) -> p r c", r=4),
                               zero_row[:, :].unsqueeze(1).to_broadcast([P, 4, D // 4]))\
                    .then_inc(s_yzero if b < BLOCKS - 2 else ystore[b - (BLOCKS - 2)], 16)

            taken(pool, "out", 3, 0)
            for k in range(4):
                pool.memset(rt["desc"][:, k:k + 1], 4.0 - k)
            pool.memset(rt["onesE"][:, :], 1.0)

            def number(name, pattern, base=0, per_partition=0):
                return pool.iota(rt[name][:, :], pattern=pattern, base=base, channel_multiplier=per_partition,
                                 allow_small_or_imprecise_dtypes=True)

            number("eidx", [[1, E]])
            number("steps", [[P, TILES - 1]], base=P)
            number("rest", [[-1, E]], base=E - 1)
            number("bidx", [[1, OVER + 1]])
            number("number", [[1, P]])
            number("token", [[0, TOP], [P, TILES]], per_partition=1).then_inc(s_need, 1)
            pool.dma_start(g_ffn[:, :], norm_ffn[0].partition_broadcast(P)).then_inc(s_gffn, 16)
            taken(pool, "last", 5, 0)
            pool.wait_ge(s_yzero, 16 * (BLOCKS - E - 2))
            for k in range(2):
                pool.wait_ge(ystore[k], 16)
            for i in range(TILES):
                pool.wait_ge(s_xn2_out[i], 16)
            pool.wait_ge(s_slot, 1)

            def gather(n2, k):
                if not isinstance(n2, int) or n2:
                    pool.wait_ge(gath[k], n2 * 16)
                pool.tensor_copy(index_1[:, k:k + 1], index_sb[:, ds(n2 * 2 + k, 1)]).then_inc(idx1[k], 1)
                pool.wait_ge(idx1[k], n2 + 1)
                pool.sem_inc(passed, 1)
                pool.indirect_dma_start(out=xe[k][:, :], out_offset=None, in_=xn2_dram,
                                        in_offset=bass.IndirectOffsetOnAxis(ap=index_1[:, k:k + 1], axis=0))\
                    .then_inc(gath[k], 16)

            def expert_pool(b2, k):
                b = b2 * 2 + k
                pool.wait_ge(tx, b * 2 + 4)
                gather(b2 + 1 + k, 1 - k)
                pool.wait_ge(yev, b + 1 + CR)
                pool.dma_start(y_dram[ds(b * P, P), :], y_sb[k][:, :]).then_inc(ystore[k], 16)

            gather(0, 0)
            gather(0, 1)
            pool.wait_ge(tx, 2)
            gather(1, 0)
            with pool.Fori(0, E // 2) as it:
                for k in range(2):
                    expert_pool(it, k)
            pool.wait_ge(s_regs, 1)
            count = pool.value_load(regs[0:1, 0:1], min_val=0, max_val=OVER)
            with pool.Fori(0, OVER_RUNS) as it:
                for k in range(2):
                    with pool.If(it * 2 + k < count):
                        expert_pool(it + E // 2, k)
            pool.wait_ge(s_split_end, 1)
            pool.wait_ge(s_rows, 1)
            stores = [pool.value_load(regs[0:1, OVER + 3 + k:OVER + 4 + k], min_val=16 * (E // 2 + 1),
                                      max_val=16 * (BLOCKS + 2)) for k in range(2)]
            for k in range(2):
                pool.wait_ge(ystore[k], stores[k])
                pool.sem_inc(passed, 1)
            for i in range(TILES):
                for k in range(TOP):
                    pool.indirect_dma_start(
                        out=picked(k, i), out_offset=None, in_=y_dram,
                        in_offset=bass.IndirectOffsetOnAxis(ap=slot_y[:, k, i:i + 1], axis=0))\
                        .then_inc(pick_sem[k][i], 16)
            pool.wait_ge(s_gfin, 16)
            for i in range(TILES - 2):
                pool.wait_ge(s_r3, i + 1)
                pool.tensor_tensor(h[:, i, :], h[:, i, :], g_fin[:, :], ALU.mult).then_inc(s_fin, 1)

        @block.scalar
        def _(act):
            for s in (ev, v_ev, sig_done, tev, mev, g_ev, silu, yev):
                act.sem_inc(s, CR)

            act.wait_ge(s_const, 1)
            act.activation(table[:, :], eps[:, :], ACT.Sqrt)
            scratch = square[:, 0:2, :].rearrange("p a n -> p (a n)")

            def first_norm(t):
                n, src, _, _, _ = first_tile(t)
                act.wait_ge(s_x[t], 16)
                if t:
                    act.wait_ge(s_sq, t)
                act.activation(scratch[0:n], src, ACT.Square, accum_out=sumsq[0:n, t:t + 1]).then_inc(s_sq, 1)
                act.wait_ge(s_sq, t + 1)
                act.activation(std[0:n, t:t + 1], sumsq[0:n, t:t + 1], ACT.Sqrt, bias=eps[0:n, :], scale=1.0 / D)\
                   .then_inc(s_std, 1)

            for t in range(3):
                first_norm(t)
            for t in range(TILES + 1):
                _, _, _, src, to = first_tile(t)
                act.wait_ge(s_xt, t + 1)
                act.copy(xnT_hi[:, :, to], src).then_inc(s_xhi, 1)
                if t < 2:
                    first_norm(t + 3)
                elif t == 2:
                    split_hi(act, "pair", 0, 0)
            act.wait_ge(s_cwt, 1)
            act.copy(cw[:, :, :], ps[:, 6, 0:PAIRS * (TAPS + 3)].rearrange("p (c n) -> p c n", c=PAIRS)).then_inc(s_cw, 1)
            for j in range(1, 4):
                split_hi(act, "pair", j, 0)

            two = ps[:, 0:2, 0:HALF]
            pr = ps[:, 3:5, 0:HALF]
            act.activation(table[:, :], eps[:, :], ACT.Sigmoid)
            with act.Fori(0, PAIRS) as c:
                def halves(t):
                    return t[:, :].rearrange("p (b n) -> p b n", b=2)

                def out_of_psum(nth, dst, src, func=None, last=True):
                    ins = act.activation(dst, src, func) if func else act.copy(dst, src)
                    if last:
                        ins.then_inc(ev, 1)

                taken(act, "pair", 0, c)
                act.wait_ge(u_done, c + CR)
                out_of_psum(1, halves(a_sb), pr)
                taken(act, "pair", 1, c)
                out_of_psum(2, halves(kT), two)
                split_hi(act, "pair", 4, c)
                taken(act, "pair", 2, c)
                out_of_psum(3, qT[:, :], ps[:, 2, :])
                split_hi(act, "pair", 5, c)
                taken(act, "pair", 3, c)
                out_of_psum(4, halves(b_sb), pr, ACT.Sigmoid)

                def sigmoids(u):
                    i, ub = 3 - u % 4, u % 3
                    off = L - META - (i + 1) * P
                    act.wait_ge(z_done, c * 8 + u + 1)
                    act.wait_ge(t_done, c * 8 + last_user(u) + CR)
                    if i == 3:
                        src, view = two, lambda t: t[:, ub, off:L].rearrange("p (b n) -> p b n", b=2)
                    else:
                        src, view = ps[:, 2 * (u % 2), 0:L - off], lambda t: t[:, ub, off:L]
                    act.activation(view(sig), src, ACT.Sigmoid, scale=SCALE)
                    act.activation(view(stay), src, ACT.Sigmoid, scale=-SCALE).then_inc(sig_done, 1)

                def copy_weights(u):
                    i = 3 - u % 4
                    act.wait_ge(t_done, c * 8 + u + 1 + CR)
                    act.wait_ge(av_done, c * 2 + u // 4 + CR)
                    act.copy(probT[:, 0:i + 1, i * P:(i + 1) * P],
                                   ps[:, turn_bank[u % 2], 0:(i + 1) * P].rearrange("p (j n) -> p j n", n=P))\
                       .then_inc(tev, 1)
                    if i == 0:
                        act.copy(probT_meta[:, :], ps[0:META, 6, :]).then_inc(mev, 1)

                sigmoids(0)
                sigmoids(1)
                taken(act, "pair", 4, c)
                out_of_psum(5, halves(vT), pr)
                for u in range(8):
                    copy_weights(u)
                    if u + 2 < 8:
                        sigmoids(u + 2)
                    if u == 0:
                        act.wait_ge(vt_done, c + 1)
                        act.copy(v_sb[:, :, :], ps[:, 7, :].rearrange("p (j n) -> p j n", n=P))
                        act.copy(v_meta[:, :], ps[0:META, 3, 0:P]).then_inc(v_ev, 1)
                    if 5 <= u:
                        split_hi(act, "pair", u + 1, c)
                act.wait_ge(av_done, c * 2 + 2 + CR)
                act.copy(attT_hi[:, ds(c, 1), :].rearrange("p a n -> p (a n)"), ps[:, 7, :])\
                   .then_inc(av_hi, 1)

            def gates(m, m2, name, j, it, which=range(2)):
                for k in which:
                    dst = (sgate, cgate)[k]
                    taken(act, name, j + k, it)
                    if not isinstance(m, int) or m >= 2:
                        act.wait_ge(br_ev, m * 2 - 2 + CR)
                    act.activation(dst[:, m2, :], ps[:, gate_bank[m2][k], :], ACT.Sigmoid).then_inc(g_ev, 1)

            taken(act, "gate", 0, 0)
            act.activation(sgate[:, 0, 0:HALF - META], ps[:, 3, META:HALF], ACT.Sigmoid)
            act.activation(sgate[:, 0, HALF - META:], ps[:, 4, 0:HALF], ACT.Sigmoid).then_inc(g_ev, 1)
            gates(0, 0, "gate", 0, 0, [1])
            split_hi(act, "gate", 4, 0)
            split_hi(act, "gate", 5, 0)
            gates(1, 1, "gate", 2, 0)
            for m in range(PAIRS):
                act.wait_ge(ln_xc, m + 1)
                act.activation(sq_ln[:, m, :], y[:, m, :], ACT.Square).then_inc(ln_sq, 1)
            split_hi(act, "mix", 0, 0)
            act.wait_ge(ln_var, 1)
            act.activation(rstd_ln[:, :], ps[:, 6, :], ACT.Sqrt, bias=eps[:, :]).then_inc(ln_std, 1)
            act.activation(table[:, :], eps[:, :], ACT.Silu)
            split_hi(act, "mix", 1, 0)
            for m in range(PAIRS):
                act.wait_ge(ln_n, m + 1)
                if m >= 2:
                    act.wait_ge(ln_lo, m - 1)
                act.activation(silu_y[:, m % 2, :], y[:, m, :], ACT.Silu, scale=cw[:, m, TAPS + 1:TAPS + 2],
                               bias=cw[:, m, TAPS + 2:TAPS + 3]).then_inc(ln_act, 1)
                act.wait_ge(ln_act, m + 1)
                act.copy(yT_hi[:, m, :], silu_y[:, m % 2, :]).then_inc(ln_hi, 1)
            split_hi(act, "mix", 2, 0)

            def merge_hi(m):
                act.wait_ge(br_ev, m * 2 + 2 + CR)
                act.copy(mT_hi[:, ds(m, 1), :].rearrange("p a n -> p (a n)"), merged[:, :])\
                   .then_inc(m_hi, 1)

            act.activation(table[:, :], eps[:, :], ACT.Sigmoid)
            with act.Fori(0, 2) as it:
                for k in range(2):
                    split_hi(act, "mix", 3 * k + 3, it)
                    merge_hi(it * 2 + k)
                    gates(it * 2 + (k + 2), k, "mix", 3 * k - 2, it)
                    split_hi(act, "mix", 3 * k + 4, it)
                    split_hi(act, "mix", 3 * k + 5, it)
            split_hi(act, "last", 3, 0)
            merge_hi(4)
            gates(6, 0, "last", -2, 0)
            split_hi(act, "last", 4, 0)
            split_hi(act, "last", 5, 0)
            split_hi(act, "out", 0, 0)
            merge_hi(5)
            gates(7, 1, "last", 1, 0)
            split_hi(act, "out", 1, 0)
            merge_hi(6)
            split_hi(act, "out", 2, 0)
            merge_hi(7)
            for j in range(3, 8):
                split_hi(act, "out", j, 0)
            act.wait_ge(m_lo, KB)
            for j in range(2):
                split_hi(act, "expert", j, 0)
            act.activation(table[:, :], eps[:, :], ACT.Sqrt)

            def norm2(i):
                act.wait_ge(res, TILES + i + 1)
                if i:
                    act.wait_ge(s_sq2, i)
                act.activation(square2[:, :], h[:, i, :], ACT.Square, accum_out=sumsq[:, 8 + i:9 + i])\
                   .then_inc(s_sq2, 1)
                act.wait_ge(s_sq2, i + 1)
                act.activation(std[:, 8 + i:9 + i], sumsq[:, 8 + i:9 + i], ACT.Sqrt, bias=eps[:, :],
                               scale=1.0 / D).then_inc(s_std2, 1)

            norm2(0)
            norm2(1)
            for i in range(TILES):
                act.wait_ge(s_xt2, i + 1)
                if i >= 2:
                    act.wait_ge(s_logit, i - 1)
                act.copy(xn2T[:, i % 2, :, :], ps[:, 2 * (i % 2):2 * (i % 2) + 2, :]
                         .rearrange("p b (k n) -> p (b k) n", n=P)).then_inc(s_xe2, 1)
                if i + 2 < TILES:
                    norm2(i + 2)
                else:
                    split_hi(act, "expert", i, 0)
            split_hi(act, "expert", AHEAD - 1, 0)
            act.activation(table[:, :], eps[:, :], ACT.Exp)
            act.wait_ge(s_logit, TILES)
            act.copy(logitT[:, :], ps[0:GROUPS + E, 4, :]).then_inc(s_lcopy, 1)
            act.wait_ge(s_gexp, 1)
            act.activation(rt["gtmp"][:, :], rt["gtmp"][:, :], ACT.Exp).then_inc(s_hot, 1)
            act.wait_ge(s_gexp, 2)
            act.activation(rt["ex"][:, :], rt["p2"][:, :], ACT.Exp).then_inc(s_hot, 1)

            def inputs_hi(b, half):
                act.wait_ge(tx, b * 2 + half + 1)
                act.copy(xeT_hi[:, 4 * half:4 * half + 4, :], ps[:, half, :].rearrange("p (k n) -> p k n", n=P)).then_inc(xe_hi, 1)

            def hidden_hi(b, half):
                act.wait_ge(ht, b * 2 + half + 1)
                act.copy(hT_hi[:, 2 * half:2 * half + 2, :], ht_bank[half].rearrange("p (f n) -> p f n", n=P))\
                   .then_inc(ht_hi, 1)

            def expert_act(name, it, b2, k):
                b, o = b2 * 2 + k, 12 * k
                for j in (5, 6):
                    split_hi(act, name, o + j, it)
                taken(act, name, o + 3, it)
                act.wait_ge(hdn_done, b * 2 + CR)
                act.activation(silu_g[:, :], ps[:, 2, :], ACT.Silu).then_inc(silu, 1)
                for j in range(7, 12):
                    split_hi(act, name, o + j, it)
                hidden_hi(b, 0)
                inputs_hi(b + 1, 0)
                hidden_hi(b, 1)
                inputs_hi(b + 1, 1)
                for j in range(12, 12 + AHEAD):
                    split_hi(act, name, o + j, it)
                taken(act, name, o + 11, it)
                act.wait_ge(ystore[k], b2 * 16 + 16)
                act.copy(y_sb[k][:, :], ps[:, 5:7, :].rearrange("p b n -> p (b n)")).then_inc(yev, 1)

            inputs_hi(0, 0)
            inputs_hi(0, 1)
            act.activation(table[:, :], eps[:, :], ACT.Silu)
            with act.Fori(0, E // 2) as it:
                for k in range(2):
                    expert_act("expert", it, it, k)
            act.wait_ge(s_regs, 1)
            count = act.value_load(regs[0:1, 0:1], min_val=0, max_val=OVER)
            with act.Fori(0, OVER_RUNS) as it:
                for k in range(2):
                    with act.If(it * 2 + k < count):
                        expert_act("over", it, it + E // 2, k)
            act.activation(table[:, :], eps[:, :], ACT.Sqrt)
            for i in range(TILES):
                act.wait_ge(sum2, i + 1)
                act.activation(square2[:, :], h[:, i, :], ACT.Square, accum_out=sumsq[:, 12 + i:13 + i])\
                   .then_inc(s_sq3, 1)
                act.wait_ge(s_sq3, i + 1)
                act.activation(std[:, 12 + i:13 + i], sumsq[:, 12 + i:13 + i], ACT.Sqrt, bias=eps[:, :],
                               scale=1.0 / D).then_inc(s_std3, 1)
                if i < TILES - 2:
                    act.wait_ge(s_recip3, i + 1)
                    act.activation(h[:, i, :], h[:, i, :], ACT.Copy, scale=rstd[:, 12 + i:13 + i]).then_inc(s_r3, 1)

        @block.vector
        def _(dve):
            for s in (lo_done, conv_done, av_lo, br_ev, xe_lo, hdn_done):
                dve.sem_inc(s, CR)

            class Chain:
                done, start, run, per = 0, 0, None, 0

                def loop(self, run, per):
                    self.start, self.run, self.per, self.done = self.start + self.done, run, per, 0

                def end(self, runs):
                    assert self.done == self.per, self.done
                    self.start, self.run, self.done = self.start + runs * self.per, None, 0

                def free(self, ins):
                    self.done += 1
                    ins.then_inc(dchain, 1)

                def link(self, ins):
                    self.done += 1
                    ins.then_inc(dchain, 1)
                    at = self.start + self.done
                    dve.wait_ge(dchain, at if self.run is None else self.run * self.per + at)

            chain = Chain()
            link, free = chain.link, chain.free

            def first_norm(t):
                n, src, dst, _, _ = first_tile(t)
                dve.wait_ge(s_std, t + 1)
                link(dve.reciprocal(rstd[0:n, t:t + 1], std[0:n, t:t + 1]))
                if t == 0:
                    dve.wait_ge(s_gmix, 16)
                dve.scalar_tensor_tensor(out=dst, in0=src, scalar=rstd[0:n, t:t + 1], in1=g_mix[0:n, :], op0=ALU.mult,
                                         op1=ALU.mult).then_inc(s_xn, 1)

            for t in range(3):
                first_norm(t)
            first_lo(dve, 0)
            first_lo(dve, 1)
            first_norm(3)
            first_lo(dve, 2)
            first_norm(4)
            split_lo(dve, "pair", 0, 0)
            first_lo(dve, 3)
            first_lo(dve, 4)
            dve.wait_ge(s_cw, 1)
            for j in range(1, 4):
                split_lo(dve, "pair", j, 0)
            dve.wait_ge(s_const, 3)

            with dve.Fori(0, PAIRS) as c:
                chain.loop(c, TAPS)
                tap = [0]

                def taps(n):
                    for _ in range(n):
                        k = tap[0]
                        if k == TAPS:
                            return
                        tap[0] += 1
                        win = u_pad[:, META + k:META + k + SEQ]
                        if k == 0:
                            dve.wait_ge(u_done, c + 1 + CR)
                            link(dve.tensor_copy(cw_c[:, :], cw[:, ds(c, 1), :].rearrange("p a n -> p (a n)")))
                            link(dve.tensor_scalar(y_acc[:, :], win, cw_c[:, 0:1], cw_c[:, TAPS:TAPS + 1],
                                                   ALU.mult, ALU.add))
                        elif k < TAPS - 1:
                            link(dve.scalar_tensor_tensor(out=y_acc[:, :], in0=win, scalar=cw_c[:, k:k + 1],
                                                          in1=y_acc[:, :], op0=ALU.mult, op1=ALU.add))
                        else:
                            ins = dve.scalar_tensor_tensor(
                                out=y[:, ds(c, 1), :].rearrange("p a n -> p (a n)"), in0=win,
                                scalar=cw_c[:, k:k + 1], in1=y_acc[:, :], op0=ALU.mult, op1=ALU.add)
                            ins.then_inc(conv_done, 1)

                def scan(u):
                    ub, off = u % 3, (u % 4) * P
                    dve.wait_ge(sig_done, c * 8 + u + 1 + CR)
                    dve.wait_ge(prob_done, c * 8 + last_user(u) + CR)
                    dve.tensor_tensor_scan(after[:, ub, off:L][:, ::-1], stay[:, ub, off + 1:L + 1][:, ::-1],
                                           ones_row[:, off:L], 1.0, ALU.mult, ALU.mult).then_inc(scan_done, 1)

                split_lo(dve, "pair", 4, c)
                split_lo(dve, "pair", 5, c)
                for u in range(8):
                    scan(u)
                    if u == 1:
                        taps(6)
                    elif 1 < u < 7:
                        taps(2 - u % 2)
                split_lo(dve, "pair", 6, c)
                dve.wait_ge(av_hi, c + 1)
                dve.tensor_tensor(attT_lo[:, ds(c, 1), :].rearrange("p a n -> p (a n)"), ps[:, 7, :],
                                  attT_hi[:, ds(c, 1), :].rearrange("p a n -> p (a n)").bitcast(F32), ALU.subtract)\
                   .then_inc(av_lo, 1)
                split_lo(dve, "pair", 7, c)
                split_lo(dve, "pair", 8, c)
                taps(TAPS)
                chain.end(PAIRS)
            split_lo(dve, "gate", 4, 0)
            dve.wait_ge(ln_mean, 1)
            for m in range(PAIRS):
                dve.tensor_tensor(y[:, m, :], y[:, m, :], ps[:, 5, :], ALU.subtract).then_inc(ln_xc, 1)
            split_lo(dve, "gate", 5, 0)
            split_lo(dve, "mix", 0, 0)
            dve.wait_ge(ln_std, 1)
            dve.reciprocal(rstd_ln[:, :], rstd_ln[:, :]).then_inc(ln_rstd, 1)
            dve.wait_ge(ln_rstd, 1)
            for m in range(PAIRS):
                dve.tensor_tensor(y[:, m, :], y[:, m, :], rstd_ln[:, :], ALU.mult).then_inc(ln_n, 1)
            split_lo(dve, "mix", 1, 0)
            for m in range(PAIRS):
                dve.wait_ge(ln_hi, m + 1)
                dve.tensor_tensor(yT_lo[:, m, :], silu_y[:, m % 2, :], yT_hi[:, m, :].bitcast(F32), ALU.subtract)\
                   .then_inc(ln_lo, 1)
            split_lo(dve, "mix", 2, 0)

            def merge(m, m2, name, j, it):
                dve.wait_ge(g_ev, m * 2 + 2 + CR)
                dve.wait_ge(br_done, m + 1)
                dve.tensor_tensor(sgate[:, m2, :], sgate[:, m2, :], ps[:, branch_bank[m2][0], :], ALU.mult).then_inc(br_ev, 1)
                taken(dve, name, j, it)
                dve.wait_ge(br_ev, m * 2 + 1 + CR)
                dve.tensor_tensor(cgate[:, m2, :], cgate[:, m2, :], ps[:, branch_bank[m2][1], :], ALU.mult).then_inc(br_mul, 1)
                dve.wait_ge(br_mul, m + 1)
                dve.tensor_tensor(merged[:, :], sgate[:, m2, :], cgate[:, m2, :], ALU.add).then_inc(br_ev, 1)

            def merge_lo(m):
                dve.wait_ge(m_hi, m + 1)
                dve.tensor_tensor(mT_lo[:, ds(m, 1), :].rearrange("p a n -> p (a n)"), merged[:, :],
                                  mT_hi[:, ds(m, 1), :].rearrange("p a n -> p (a n)").bitcast(F32), ALU.subtract)\
                   .then_inc(m_lo, 1)

            with dve.Fori(0, 2) as it:
                for k in range(2):
                    merge(it * 2 + k, k, "mix", 3 * k, it)
                    split_lo(dve, "mix", 3 * k + 3, it)
                    merge_lo(it * 2 + k)
                    split_lo(dve, "mix", 3 * k + 4, it)
                    split_lo(dve, "mix", 3 * k + 5, it)
            merge(4, 0, "last", 0, 0)
            split_lo(dve, "last", 3, 0)
            merge_lo(4)
            split_lo(dve, "last", 4, 0)
            split_lo(dve, "last", 5, 0)
            split_lo(dve, "out", 0, 0)
            merge(5, 1, "last", 3, 0)
            merge_lo(5)
            split_lo(dve, "out", 1, 0)
            merge(6, 0, "last", 4, 0)
            merge_lo(6)
            split_lo(dve, "out", 2, 0)
            merge(7, 1, "last", 5, 0)
            merge_lo(7)

            def residual(half, tiles):
                for i in tiles:
                    if i < TILES - 1:
                        dve.wait_ge(out_done, (TILES - 1) * half + i + 1)
                    else:
                        taken(dve, "out", 4 * half + 3, 0)
                    part = h[:, i, 512 * half:512 * half + 512]
                    dve.tensor_tensor(part, part, ps[:, out_bank[4 * half + i], :], ALU.add).then_inc(res, 1)

            for j in range(3, 7):
                split_lo(dve, "out", j, 0)
            residual(0, range(TILES))
            split_lo(dve, "out", 7, 0)
            for j in range(2):
                split_lo(dve, "expert", j, 0)

            def norm2(i):
                dve.wait_ge(s_std2, i + 1)
                link(dve.reciprocal(rstd[:, 8 + i:9 + i], std[:, 8 + i:9 + i]))
                if i == 0:
                    dve.wait_ge(s_gffn, 16)
                dve.scalar_tensor_tensor(out=xn2[:, i, :], in0=h[:, i, :], scalar=rstd[:, 8 + i:9 + i],
                                         in1=g_ffn[:, :], op0=ALU.mult, op1=ALU.mult).then_inc(s_xn2, 1)

            residual(1, range(2))
            for i in range(TILES):
                norm2(i)
                if i + 2 < TILES:
                    residual(1, range(i + 2, i + 3))
            for j in range(2, AHEAD):
                split_lo(dve, "expert", j, 0)

            T = TILES

            def v2(name):
                return rt[name][:, :].rearrange("p (t n) -> p t n", t=T)

            def v3(name):
                return rt[name][:, :].rearrange("p (t g n) -> p t g n", t=T, g=GROUPS)

            def over(name, n):
                return rt[name][:, :].unsqueeze(2).to_broadcast([P, T, n])

            def row(name, n):
                return rt[name][:, :].unsqueeze(1).to_broadcast([P, T, n])

            def tt(o, a, b, op):
                link(dve.tensor_tensor(o, a, b, op))

            def reduce(o, a, op=ALU.add):
                link(dve.tensor_reduce(o, a, AX.X, op))

            def first_best(src, hot, best):
                reduce(rt[best][:, :], src, ALU.max)
                tt(v2("cand"), src, over(best, 4), ALU.is_equal)
                tt(v2("cand"), v2("cand"), row("desc", 4), ALU.mult)
                reduce(rt["best"][:, :], v2("cand"), ALU.max)
                tt(v2(hot), v2("cand"), over("best", 4), ALU.is_equal)

            dve.wait_ge(s_lturn, 1)
            dve.wait_ge(s_router, 16 * 4)
            dve.wait_ge(s_need, 1)
            link(dve.tensor_tensor(v2("logit"), ps[:, 7, 0:T * 20].rearrange("p (t n) -> p t n", t=T),
                                   bias_rt[:, :].unsqueeze(1).to_broadcast([P, T, 20]), ALU.add))
            first_best(v2("logit")[:, :, 0:4], "ohg", "gmax")
            free(dve.tensor_tensor(v2("gtmp"), v2("logit")[:, :, 0:4], over("gmax", 4), ALU.subtract))
            tt(v3("sel"), v2("logit")[:, :, 4:20].rearrange("p t (g n) -> p t g n", g=4),
               v2("ohg").unsqueeze(3).to_broadcast([P, T, 4, 4]), ALU.mult)
            dve.sem_inc(s_gexp, 1)
            reduce(v2("el"), v3("sel").rearrange("p t g n -> p t n g"))
            first_best(v2("el"), "oh1", "p1")
            link(dve.scalar_tensor_tensor(out=rt["el2"][:, :], in0=rt["oh1"][:, :], scalar=MASKED, in1=rt["el"][:, :],
                                          op0=ALU.mult, op1=ALU.add))
            first_best(v2("el2"), "oh2", "p2")
            free(dve.tensor_tensor(rt["p2"][:, :], rt["p2"][:, :], rt["p1"][:, :], ALU.subtract))
            H12 = rt["H12"][:, :].rearrange("p (k t n) -> p k t n", k=TOP, t=T)
            for k, hot in enumerate(("oh1", "oh2")):
                (free, link)[k](dve.tensor_tensor(
                    H12[:, k].rearrange("p t (g n) -> p t g n", g=GROUPS), v2("ohg").unsqueeze(3).to_broadcast([P, T, 4, 4]),
                    v2(hot).unsqueeze(2).to_broadcast([P, T, 4, 4]), ALU.mult))
            tt(H_bf[:, :, :], H12[:, 0], H12[:, 1], ALU.add)
            dve.sem_inc(s_hotx, 1)
            dve.sem_inc(s_gexp, 1)
            dve.wait_ge(s_rank, 1)
            S = T - 1
            rank = ps[:, 6, 0:T * E]
            over3 = rt["over3"][:, :].rearrange("p (n s) -> p n s", s=S)
            ge3 = rt["ge3"][:, :].rearrange("p (m s) -> p m s", s=S)
            free(dve.tensor_tensor(over3, ps[:, 6, T * E:T * E + E].unsqueeze(2).to_broadcast([P, E, S]),
                                   rt["steps"][:, :].unsqueeze(1).to_broadcast([P, E, S]), ALU.is_gt))
            tt(ge3, rank.unsqueeze(2).to_broadcast([P, T * E, S]),
               rt["steps"][:, :].unsqueeze(1).to_broadcast([P, T * E, S]), ALU.is_ge)
            free(dve.tensor_reduce(rt["ovn"][:, :], over3, AX.X, ALU.add))
            reduce(rt["fb"][:, :], ge3)
            free(dve.tensor_tensor_scan(rt["cum"][:, :], rt["onesE"][:, :], rt["ovn"][:, :], 0.0, ALU.mult, ALU.add))
            free(dve.tensor_tensor(rt["t3"][:, :], rt["rest"][:, :], rt["ovn"][:, :], ALU.subtract))
            link(dve.scalar_tensor_tensor(out=rt["place_of"][:, :], in0=rt["fb"][:, :], scalar=-float(P), in1=rank,
                                          op0=ALU.mult, op1=ALU.add))
            free(dve.tensor_tensor(v2("t2"), v2("fb"), row("eidx", E), ALU.add))
            tt(rt["t3"][:, :], rt["cum"][:, :], rt["t3"][:, :], ALU.add)
            tt(v2("t1"), ge3[:, :, 0].rearrange("p (t n) -> p t n", t=T), row("t3", E), ALU.mult)
            tt(rt["t1"][:, :], rt["t1"][:, :], rt["t2"][:, :], ALU.add)
            sel = {}
            for src in ("t1", "place_of"):
                sel[src] = rt["sel_" + src][:, :].rearrange("p (k t n) -> p k t n", k=TOP, t=T)
                (free if src == "t1" else link)(dve.tensor_tensor(
                    sel[src], H12, v2(src).unsqueeze(1).to_broadcast([P, TOP, T, E]), ALU.mult))
            free(dve.tensor_reduce(rt["block"][:, :], rt["sel_t1"][:, :].rearrange("p (m n) -> p m n", n=E), AX.X, ALU.add))
            reduce(rt["place"][:, :], rt["sel_place_of"][:, :].rearrange("p (m n) -> p m n", n=E))
            M = TOP * T
            hot = rt["hot"][:, :].rearrange("p (m n) -> p m n", n=ICOLS)
            free(dve.tensor_tensor(hot, rt["number"][:, 0:ICOLS].unsqueeze(1).to_broadcast([P, M, ICOLS]),
                                   rt["block"][:, :].unsqueeze(2).to_broadcast([P, M, ICOLS]), ALU.is_equal))
            tt(place_hot[:, :, :], rt["number"][:, :].unsqueeze(1).to_broadcast([P, M, P]),
               rt["place"][:, :].unsqueeze(2).to_broadcast([P, M, P]), ALU.is_equal)
            dve.tensor_tensor(block_hot[:, :, :], hot, rt["token"][:, :].unsqueeze(2).to_broadcast([P, M, ICOLS]),
                              ALU.mult).then_inc(s_place, 1)
            bex = rt["bex"][:, :].rearrange("p (b n) -> p b n", n=E)
            tt(bex, rt["cum"][:, :].unsqueeze(1).to_broadcast([P, OVER + 1, E]),
               rt["bidx"][:, :].unsqueeze(2).to_broadcast([P, OVER + 1, E]), ALU.is_le)
            dve.wait_ge(s_table, 1)
            dve.tensor_copy(index_sb[:, :], ps[:, 5, 0:ICOLS]).then_inc(s_slot, 1)
            reduce(rt["bexi"][:, :], bex)
            link(dve.tensor_scalar(rt["bexi"][:, :], rt["bexi"][:, :], float(E - 1), None, ALU.min))
            link(dve.tensor_copy(regs[:, 1:OVER + 2], rt["bexi"][:, :]))
            tt(rt["bexi"][:, :], rt["cum"][:, E - 1:E].to_broadcast([P, OVER + 1]), rt["bidx"][:, :], ALU.is_gt)
            reduce(rt["runs"][:, :], rt["bexi"][:, :].rearrange("p (n k) -> p k n", k=2))
            link(dve.tensor_scalar(regs[:, OVER + 3:OVER + 5], rt["runs"][:, :], 16.0, 16.0 * (E // 2 + 1), ALU.mult, ALU.add))
            dve.tensor_copy(regs[:, 0:1], rt["cum"][:, E - 1:E]).then_inc(s_regs, 1)
            link(dve.scalar_tensor_tensor(out=rt["row"][:, :], in0=rt["block"][:, :], scalar=float(P),
                                          in1=rt["place"][:, :], op0=ALU.mult, op1=ALU.add))
            dve.tensor_copy(slot_y[:, :, :], rt["row"][:, :].rearrange("p (k t) -> p k t", k=TOP)).then_inc(s_rows, 1)
            dve.wait_ge(s_hot, 2)
            reduce(rt["gsum"][:, :], v2("gtmp"))
            link(dve.scalar_tensor_tensor(out=rt["gsum"][:, :], in0=rt["ex"][:, :], scalar=1.0, in1=rt["gsum"][:, :],
                                          op0=ALU.add, op1=ALU.mult))
            link(dve.reciprocal(w_tok[:, 0, :], rt["gsum"][:, :]))
            tt(w_tok[:, 1, :], w_tok[:, 0, :], rt["ex"][:, :], ALU.mult)
            dve.sem_inc(s_weights, 1)

            def inputs_lo(b, half):
                dve.wait_ge(xe_hi, b * 2 + half + 1)
                dve.tensor_tensor(xeT_lo[:, 4 * half:4 * half + 4, :],
                                  ps[:, half, :].rearrange("p (k n) -> p k n", n=P),
                                  xeT_hi[:, 4 * half:4 * half + 4, :].bitcast(F32), ALU.subtract).then_inc(xe_lo, 1)

            def hidden_lo(b, half):
                dve.wait_ge(ht_hi, b * 2 + half + 1)
                dve.tensor_tensor(hT_lo[:, 2 * half:2 * half + 2, :], ht_bank[half].rearrange("p (f n) -> p f n", n=P),
                                  hT_hi[:, 2 * half:2 * half + 2, :].bitcast(F32), ALU.subtract).then_inc(ht_lo, 1)

            def expert_dve(name, it, b2, k):
                b, o = b2 * 2 + k, 12 * k
                for j in range(AHEAD, 10):
                    split_lo(dve, name, o + j, it)
                taken(dve, name, o + 7, it)
                dve.wait_ge(silu, b + 1 + CR)
                for half in range(2):
                    part = slice(half * FF // 2, (half + 1) * FF // 2)
                    dve.tensor_tensor(hdn[:, part], silu_g[:, part], ps[:, 3, part], ALU.mult).then_inc(hdn_done, 1)
                hidden_lo(b, 0)
                split_lo(dve, name, o + 10, it)
                hidden_lo(b, 1)
                split_lo(dve, name, o + 11, it)
                inputs_lo(b + 1, 0)
                inputs_lo(b + 1, 1)
                for j in range(12, 12 + AHEAD):
                    split_lo(dve, name, o + j, it)

            inputs_lo(0, 0)
            inputs_lo(0, 1)
            with dve.Fori(0, E // 2) as it:
                for k in range(2):
                    expert_dve("expert", it, it, k)
            count = dve.value_load(regs[0:1, 0:1], min_val=0, max_val=OVER)
            with dve.Fori(0, OVER_RUNS) as it:
                for k in range(2):
                    with dve.If(it * 2 + k < count):
                        expert_dve("over", it, it + E // 2, k)

            dve.memset(sumsq[:, 7:8], 0.0).then_inc(s_split_end, 1)

            def combine(i, k):
                done = (sum1, sum2)[k]
                dve.wait_ge(pick_sem[k][i], 16)
                dve.scalar_tensor_tensor(out=h[:, i, :], in0=picked(k, i), scalar=w_tok[:, k, i:i + 1],
                                         in1=h[:, i, :], op0=ALU.mult, op1=ALU.add).then_inc(done, 1)
                dve.wait_ge(done, i + 1)

            def recip(i):
                dve.wait_ge(s_std3, i + 1)
                dve.reciprocal(rstd[:, 12 + i:13 + i], std[:, 12 + i:13 + i]).then_inc(s_recip3, 1)

            for i in range(TILES):
                combine(i, 0)
                if i:
                    recip(i - 1)
                combine(i, 1)
            dve.wait_ge(s_gfin, 16)
            for i in range(TILES - 2, TILES):
                if i == TILES - 1:
                    recip(i)
                dve.wait_ge(s_recip3, i + 1)
                dve.scalar_tensor_tensor(out=h[:, i, :], in0=h[:, i, :], scalar=rstd[:, 12 + i:13 + i], in1=g_fin[:, :],
                                         op0=ALU.mult, op1=ALU.mult).then_inc(s_fin_last, 1)

        @block.tensor
        def _(pe):
            for s in (used, t_done, av_done):
                pe.sem_inc(s, CR)
            pe.wait_ge(s_const, 2)

            for t in range(TILES + 1):
                n, _, src, dst, _ = first_tile(t)
                pe.wait_ge(s_xn, t + 1)
                if t == 4:
                    pe.wait_ge(s_xlo, 1)
                src = src.rearrange("p (q k) -> p k q", k=KB)
                for k in range(KB):
                    last = pe.transpose(dst[:, k, :], src[:, k, :], ident[0:n, 0:n])
                last.then_inc(s_xt, 1)

            def channels_by_tokens(name, j, it, outs):
                hi, lo = weights(pe, name, j, it, P)
                for dst, tok in outs:
                    for k in range(KB):
                        last = product(pe, dst, (hi[:, k, :], lo[:, k, :]), (xnT_hi[:, k, tok], xnT_lo[:, k, tok]),
                                       k == 0, k == KB - 1)
                return last

            all_tokens = [slice(0, HALF), slice(HALF, L)]

            def ahead(steps, j, c):
                hi, lo = weights(pe, "pair", j, c, P)
                for step in steps:
                    b, k = step // KB, step % KB
                    last = product(pe, ps[:, 3 + b, 0:HALF], (hi[:, k, :], lo[:, k, :]),
                                   (xnT_hi[:, k, all_tokens[b]], xnT_lo[:, k, all_tokens[b]]), k == 0, k == KB - 1)
                if steps[-1] == 2 * KB - 1:
                    last.then_inc(used, 1)

            pe.wait_ge(s_xlo, 3)
            ahead(range(KB), 0, 0)
            pe.wait_ge(s_xlo, TILES + 1)
            n = TAPS + 3
            pe.wait_ge(s_pack, 16 * 4)
            for c in range(PAIRS):
                last = pe.transpose(ps[:, 6, c * n:(c + 1) * n], pack[0:n, c * P:(c + 1) * P], ident[0:n, 0:n])
            last.then_inc(s_cwt, 1)
            ahead(range(KB, 2 * KB), 0, 0)
            pe.wait_ge(s_cw, 1)
            pe.wait_ge(s_const, 3)
            with pe.Fori(0, PAIRS) as c:
                def project(j, outs, count=None):
                    last = channels_by_tokens("pair", j, c, outs)
                    last.then_inc(used, 1)

                pe.wait_ge(tev, c * 8 + CR)
                pe.wait_ge(sig_done, c * 8 - 1 + CR)
                project(1, [(ps[:, b, 0:HALF], all_tokens[b]) for b in range(2)])
                pe.wait_ge(sig_done, c * 8 + CR)
                project(2, [(ps[:, 2, :], slice(META, L))])
                pe.wait_ge(ev, c * 5 + 1 + CR)
                project(3, [(ps[:, 3 + b, 0:HALF], all_tokens[b]) for b in range(2)])

                def scores(u):
                    hh, i = u // 4, 3 - u % 4
                    if u >= 2:
                        pe.wait_ge(sig_done, c * 8 + u - 1 + CR)
                    if u == 4:
                        pe.wait_ge(tev, c * 8 + 2 + CR)
                    q = qT[hh * DH:(hh + 1) * DH, i * P:(i + 1) * P]
                    n = META + (i + 1) * P
                    for b, (lo, hi) in enumerate([(0, HALF), (HALF, L)] if i == 3 else [(0, n)]):
                        dst = ps[:, 2 * (u % 2) + b, :]
                        pe.matmul(dst[:, 0:hi - lo], q, kT[hh * DH:(hh + 1) * DH, lo:hi], start=True, stop=hi < n)
                    last = pe.matmul(dst[:, hi - lo - P:hi - lo], ident_bf[:, :], mask_bf[:, :], start=False, stop=True)
                    last.then_inc(z_done, 1)

                def turn(u):
                    i, ub, bank = 3 - u % 4, u % 3, turn_bank[u % 2]
                    off = L - META - (i + 1) * P
                    pe.wait_ge(prob_done, c * 8 + u + 1 + CR)
                    if u == 0:
                        pe.wait_ge(mev, c * 2 + CR)
                    pe.wait_ge(tev, c * 8 + u - 1 + CR)
                    if u == 3:
                        pe.wait_ge(sig_done, c * 8 + 5 + CR)
                    if u == 4:
                        pe.wait_ge(mev, c * 2 + 1 + CR)
                    pe.transpose(ps[0:META, 6, i * P:(i + 1) * P], sig[:, ub, off:off + META], ident[:, :])
                    for j in range(i + 1):
                        at_ = off + META + j * P
                        last = pe.transpose(ps[:, bank, j * P:(j + 1) * P], sig[:, ub, at_:at_ + P], ident[:, :])
                    last.then_inc(t_done, 1)

                def values(hh):
                    pe.wait_ge(mev, c * 2 + hh + 1 + CR)
                    pe.wait_ge(tev, c * 8 + 4 * hh + 4 + CR)
                    rows = slice(hh * DH, (hh + 1) * DH)
                    pe.matmul(ps[rows, 7, :], v_meta[:, rows], probT_meta[:, :], start=True, stop=False)
                    for j in range(TILES):
                        last = pe.matmul(ps[rows, 7, j * P:], v_sb[:, j, rows], probT[:, j, j * P:], start=False,
                                         stop=(j == TILES - 1))
                    last.then_inc(av_done, 1)

                pe.wait_ge(ev, c * 5 + 3 + CR)
                scores(0)
                scores(1)
                pe.wait_ge(ev, c * 5 + 4 + CR)
                project(4, [(ps[:, 3 + b, 0:HALF], all_tokens[b]) for b in range(2)])
                fill, step = (0, 0, 2, 4, 2, 3, 3, 2), 0
                for u in range(8):
                    turn(u)
                    if u + 2 < 8:
                        scores(u + 2)
                    if fill[u]:
                        if step == 0:
                            pe.wait_ge(v_ev, c + 1 + CR)
                        ahead(range(step, step + fill[u]), 5, c)
                        step += fill[u]
                    if u == 0:
                        pe.wait_ge(ev, c * 5 + 5 + CR)
                        pe.wait_ge(av_lo, c + CR)
                        pe.transpose(ps[0:META, 3, 0:P], vT[:, 0:META], ident[:, :])
                        for j in range(TILES):
                            last = pe.transpose(ps[:, 7, j * P:(j + 1) * P], vT[:, META + j * P:META + (j + 1) * P],
                                                ident[:, :])
                        last.then_inc(vt_done, 1)
                    if u == 3:
                        values(0)
                values(1)

            def gate(m, m2, name, j, it, which=range(2)):
                for k in which:
                    if not isinstance(m, int) or m >= 2:
                        pe.wait_ge(g_ev, m * 2 + (k - 3) + CR)
                    last = channels_by_tokens(name, j + k, it, [(ps[:, gate_bank[m2][k], :], slice(META, L))])
                    last.then_inc(used, 1)

            def mean(m):
                return pe.matmul(ps[:, 5, :], mean_w[:, :], y[:, m, :], start=(m == 0), stop=(m == PAIRS - 1))

            gate(0, 0, "gate", 0, 0, [1])
            pe.wait_ge(conv_done, PAIRS - 1 + CR)
            for m in range(PAIRS - 1):
                mean(m)
            pe.wait_ge(av_lo, PAIRS + CR)
            gate(1, 1, "gate", 2, 0)
            pe.wait_ge(conv_done, PAIRS + CR)
            mean(PAIRS - 1).then_inc(ln_mean, 1)
            gate(2, 0, "gate", 4, 0, [0])
            for m in range(PAIRS):
                pe.wait_ge(ln_sq, m + 1)
                last = pe.matmul(ps[:, 6, :], mean_w[:, :], sq_ln[:, m, :], start=(m == 0), stop=(m == PAIRS - 1))
            last.then_inc(ln_var, 1)
            gate(2, 0, "gate", 4, 0, [1])

            def branches(name, j, it, m, m2):
                hi, lo = weights(pe, name, j, it, P)
                pe.wait_ge(br_ev, m * 2 - 2 + CR)
                if name == "mix" and m2 == 0:
                    pe.wait_ge(g_ev, 1 + CR)
                for b, (left_hi, left_lo) in enumerate(((attT_hi, attT_lo), (yT_hi, yT_lo))):
                    for c in range(PAIRS):
                        if b:
                            pe.wait_ge(ln_lo, c + 1)
                        w = (hi[:, 4 * b + c, :], lo[:, 4 * b + c, :])
                        last = product(pe, ps[:, branch_bank[m2][b], :], w, (left_hi[:, c, :], left_lo[:, c, :]), c == 0, c == PAIRS - 1)
                    if b == 0:
                        last.then_inc(br_done, 1)
                last.then_inc(used, 1)

            with pe.Fori(0, 2) as it:
                for k in range(2):
                    branches("mix", 3 * k, it, it * 2 + k, k)
                    gate(it * 2 + (k + 3), (k + 1) % 2, "mix", 3 * k + 1, it)
            branches("last", 0, 0, 4, 0)
            gate(7, 1, "last", 1, 0)
            for k in range(3):
                branches("last", 3 + k, 0, 5 + k, (5 + k) % 2)

            for half in range(2):
                pe.wait_ge(g_ev, 14 + 2 * half + CR)
                pe.wait_ge(br_ev, 14 + 2 * half + CR)
                for q in range(4):
                    hi, lo = weights(pe, "out", 4 * half + q, 0, 512)

                    def part(i, m2):
                        tok = slice(i * P, (i + 1) * P)
                        m = 2 * q + m2
                        return product(pe, ps[:, out_bank[4 * half + i], :], (mT_hi[:, m, tok], mT_lo[:, m, tok]),
                                       (hi[:, m2, :], lo[:, m2, :]), m == 0, m == KB - 1)

                    if q < 3:
                        for m2 in range(2):
                            pe.wait_ge(m_lo, 2 * q + m2 + 1)
                            for i in range(TILES):
                                last = part(i, m2)
                    else:
                        pe.wait_ge(m_lo, KB)
                        for i in range(TILES):
                            part(i, 0)
                            last = part(i, 1)
                            if i < TILES - 1:
                                last.then_inc(out_done, 1)
                    last.then_inc(used, 1)

            pe.wait_ge(res, TILES + 1)

            def turn2(i):
                pe.wait_ge(s_xn2, i + 1)
                if i >= 2:
                    pe.wait_ge(s_xe2, i - 1)
                src = xn2[:, i, :].rearrange("p (q k) -> p k q", k=KB)
                for k in range(KB):
                    last = pe.transpose(ps[:, 2 * (i % 2) + k // 4, (k % 4) * P:(k % 4 + 1) * P], src[:, k, :], ident[:, :])
                last.then_inc(s_xt2, 1)

            turn2(0)
            turn2(1)
            pe.wait_ge(s_router, 16 * 4)
            for i in range(TILES):
                pe.wait_ge(s_xe2, i + 1)
                for k in range(KB):
                    last = pe.matmul(ps[0:GROUPS + E, 4, i * P:(i + 1) * P], router_w[:, k, :], xn2T[:, i % 2, k, :],
                                     start=(k == 0), stop=(k == KB - 1))
                last.then_inc(s_logit, 1)
                if i + 2 < TILES:
                    turn2(i + 2)
            pe.wait_ge(s_lcopy, 1)
            pe.wait_ge(res, 2 * TILES)
            n = GROUPS + E
            for i in range(TILES):
                last = pe.transpose(ps[:, 7, i * n:(i + 1) * n], logitT[:, i * P:(i + 1) * P], ident[0:n, 0:n])
            last.then_inc(s_lturn, 1)
            pe.wait_ge(s_hotx, 1)
            for i in range(TILES + 1):
                for j in range(min(i + 1, TILES)):
                    last = pe.matmul(ps[:, 6, i * E:(i + 1) * E], (before_bf if j == i else ones_bf)[:, :], H_bf[:, j, :],
                                     start=(j == 0), stop=(j == min(i, TILES - 1)))
            last.then_inc(s_rank, 1)
            pe.wait_ge(s_place, 1)
            M = TOP * TILES
            for m in range(M):
                last = pe.matmul(ps[:, 5, 0:ICOLS], place_hot[:, m, :], block_hot[:, m, :], start=(m == 0), stop=(m == M - 1))
            last.then_inc(s_table, 1)

            def inputs(n2, k, half):
                pe.wait_ge(gath[k], n2 * 16 + 16)
                pe.wait_ge(xe_lo, (n2 * 2 + k) * 2 + half - 1 + CR)
                src = xe[k][:, :].rearrange("p (q k) -> p k q", k=KB)
                for j in range(4):
                    last = pe.transpose(ps[:, half, j * P:(j + 1) * P], src[:, 4 * half + j, :], ident[:, :])
                last.then_inc(tx, 1)

            def expert_pe(name, it, b2, k):
                b, o = b2 * 2 + k, 12 * k
                pe.wait_ge(xe_lo, b * 2 + 2 + CR)
                for part in range(2):
                    if part == 0:
                        pe.wait_ge(silu, b + CR)
                    else:
                        pe.wait_ge(hdn_done, b * 2 + CR)
                    for q in range(4):
                        hi, lo = weights(pe, name, o + 4 * part + q, it, FF)
                        for k2 in range(2):
                            kb = 2 * q + k2
                            last = product(pe, ps[:, 2 + part, :], (xeT_hi[:, kb, :], xeT_lo[:, kb, :]),
                                           (hi[:, k2, :], lo[:, k2, :]), kb == 0, kb == KB - 1)
                        last.then_inc(used, 1)
                for half in range(2):
                    inputs(b2 + k, 1 - k, half)
                    pe.wait_ge(hdn_done, b * 2 + half + 1 + CR)
                    for f in range(2):
                        last = pe.transpose(ht_bank[half][:, f * P:(f + 1) * P], hdn[:, (2 * half + f) * P:][:, 0:P],
                                            ident[:, :])
                    last.then_inc(ht, 1)
                pe.wait_ge(yev, b + CR)
                for f in range(FB):
                    hi, lo = weights(pe, name, o + 8 + f, it, 512)
                    if f % 2 == 0:
                        pe.wait_ge(ht_hi, b * 2 + f // 2 + 1)
                    for c in range(2):
                        pe.matmul(ps[:, 5 + c, :], hT_hi[:, f, :], hi[:, c, :], start=(f == 0), stop=False)
                        pe.matmul(ps[:, 5 + c, :], hT_hi[:, f, :], lo[:, c, :], start=False, stop=False)
                    if f % 2 == 0:
                        pe.wait_ge(ht_lo, b * 2 + f // 2 + 1)
                    for c in range(2):
                        last = pe.matmul(ps[:, 5 + c, :], hT_lo[:, f, :], hi[:, c, :], start=False, stop=(f == FB - 1))
                    last.then_inc(used, 1)

            inputs(0, 0, 0)
            inputs(0, 0, 1)
            with pe.Fori(0, E // 2) as it:
                for k in range(2):
                    expert_pe("expert", it, it, k)
            pe.wait_ge(s_regs, 1)
            count = pe.value_load(regs[0:1, 0:1], min_val=0, max_val=OVER)
            with pe.Fori(0, OVER_RUNS) as it:
                for k in range(2):
                    with pe.If(it * 2 + k < count):
                        expert_pe("over", it, it + E // 2, k)


_INS = ["x", "meta", "norm_mix", "w_in", "w_sb_o", "conv_w", "conv_b", "conv_ln_g", "conv_ln_b", "w_conv_o", "w_out",
        "norm_ffn", "w_router_group", "b_router_group", "w_router_expert", "b_router_expert", "w_gate", "w_up", "w_down",
        "norm_final"]


def kernel(**inputs):
    import numpy as np
    import concourse.bacc as bacc
    from concourse.bass_utils import run_bass_kernel_spmd

    nc = bacc.Bacc("TRN2", target_bir_lowering=False, num_devices=1)
    arrays, args = {}, []
    for name in _INS:
        a = np.ascontiguousarray(inputs[name])
        arrays[f"in_{name}"] = a
        args.append(nc.dram_tensor(f"in_{name}", a.shape, mybir.dt.from_np(a.dtype), kind="ExternalInput").ap())
    args.append(nc.dram_tensor("out", (1, SEQ, D), F32, kind="ExternalOutput").ap())
    args.append(nc.dram_tensor("xn2_dram", (SEQ, D), F32, kind="Internal").ap())
    args.append(nc.dram_tensor("y_dram", (BLOCKS * P, D), F32, kind="Internal").ap())
    build(nc, *args)
    return run_bass_kernel_spmd(nc, [arrays], core_ids=[0]).results[0]["out"]
```
